# Optimizing a Trainium2 kernel written in Bass

```python
import jax, jax.numpy as jnp
from jax import lax
import numpy as np

D_MODEL = 1024
BATCH = 1
SEQ = 256
DEPTH = 1

ATTN_HEAD_DIM = 64
ATTN_HEADS = D_MODEL // ATTN_HEAD_DIM
ATTN_KV_HEADS = ATTN_HEADS // 4
ATTN_GROUP = ATTN_HEADS // ATTN_KV_HEADS
WINDOW = 128

MLSTM_HEADS = 8
MLSTM_V_DIM = D_MODEL // MLSTM_HEADS
MLSTM_QK_DIM = MLSTM_V_DIM // 2
MLSTM_CHUNK = 64
CONV_WIDTH = 4
GATE_SOFTCAP = 15.0

D_FF = ((8 * D_MODEL // 3 + 127) // 128) * 128
FFN_RESIDUAL_WEIGHT = 0.5
NORM_EPS = 1e-6

SZ_AQ = ATTN_HEADS * ATTN_HEAD_DIM
SZ_AK = ATTN_KV_HEADS * ATTN_HEAD_DIM
SZ_AV = ATTN_KV_HEADS * ATTN_HEAD_DIM
SZ_MQ = MLSTM_HEADS * MLSTM_QK_DIM
SZ_MK = MLSTM_HEADS * MLSTM_QK_DIM
SZ_MV = MLSTM_HEADS * MLSTM_V_DIM
SZ_MO = MLSTM_HEADS * MLSTM_V_DIM
SZ_MI = MLSTM_HEADS
SZ_MF = MLSTM_HEADS
SZ_GATES = 2 * D_MODEL
SPLIT_POINTS = (
    SZ_AQ,
    SZ_AQ + SZ_AK,
    SZ_AQ + SZ_AK + SZ_AV,
    SZ_AQ + SZ_AK + SZ_AV + SZ_MQ,
    SZ_AQ + SZ_AK + SZ_AV + SZ_MQ + SZ_MK,
    SZ_AQ + SZ_AK + SZ_AV + SZ_MQ + SZ_MK + SZ_MV,
    SZ_AQ + SZ_AK + SZ_AV + SZ_MQ + SZ_MK + SZ_MV + SZ_MO,
    SZ_AQ + SZ_AK + SZ_AV + SZ_MQ + SZ_MK + SZ_MV + SZ_MO + SZ_MI,
    SZ_AQ + SZ_AK + SZ_AV + SZ_MQ + SZ_MK + SZ_MV + SZ_MO + SZ_MI + SZ_MF,
)
F_OFFSET = SPLIT_POINTS[7]
IN_WIDTH = SPLIT_POINTS[8] + SZ_GATES


def rms_norm(x, g):
    xf = x.astype(jnp.float32)
    y = xf * lax.rsqrt(jnp.mean(xf * xf, axis=-1, keepdims=True) + NORM_EPS)
    return (y * g.astype(jnp.float32)).astype(x.dtype)

def swiglu(x, w_gate, w_up, w_down):
    return (jax.nn.silu(x @ w_gate) * (x @ w_up)) @ w_down

def causal_depthwise_conv(x, w):
    s = x.shape[1]
    xp = jnp.pad(x, ((0, 0), (CONV_WIDTH - 1, 0), (0, 0)))
    out = xp[:, 0:s] * w[0]
    for j in range(1, CONV_WIDTH):
        out = out + xp[:, j:j + s] * w[j]
    return out

def sliding_window_attention(q, k, v, sinks):
    b, s = q.shape[0], q.shape[1]
    nb = s // WINDOW
    qb = q.reshape(b, nb, WINDOW, ATTN_KV_HEADS, ATTN_GROUP, ATTN_HEAD_DIM)

    def band(t):
        tp = jnp.pad(t, ((0, 0), (WINDOW, 0), (0, 0), (0, 0)))
        tp = tp.reshape(b, nb + 1, WINDOW, ATTN_KV_HEADS, ATTN_HEAD_DIM)
        return jnp.concatenate([tp[:, :-1], tp[:, 1:]], axis=2)

    kb, vb = band(k), band(v)
    scale = ATTN_HEAD_DIM ** -0.5
    scores = jnp.einsum('bnqhgd,bnkhd->bhgnqk', qb, kb).astype(jnp.float32) * scale
    qi = jnp.arange(WINDOW)[:, None]
    kj = jnp.arange(2 * WINDOW)[None, :]
    in_window = (kj > qi) & (kj <= qi + WINDOW)
    is_pad = (jnp.arange(nb)[:, None, None] == 0) & (kj < WINDOW)[None]
    valid = in_window[None] & ~is_pad
    scores = jnp.where(valid, scores, -jnp.inf)
    sink = jnp.broadcast_to(
        sinks.astype(jnp.float32).reshape(ATTN_KV_HEADS, ATTN_GROUP)[None, :, :, None, None, None],
        scores.shape[:-1] + (1,))
    probs = jax.nn.softmax(jnp.concatenate([scores, sink], axis=-1), axis=-1)[..., :-1]
    out = jnp.einsum('bhgnqk,bnkhd->bnqhgd', probs.astype(v.dtype), vb)
    return out.reshape(b, s, ATTN_HEADS * ATTN_HEAD_DIM)

def mlstm_chunkwise(q, k, v, i_pre, f_pre):
    b, s = q.shape[0], q.shape[1]
    nc = s // MLSTM_CHUNK
    f32 = jnp.float32

    def to_chunks(t):
        return t.astype(f32).reshape(b, nc, MLSTM_CHUNK, MLSTM_HEADS, t.shape[-1]).transpose(1, 0, 3, 2, 4)

    def gate_chunks(t):
        return t.astype(f32).reshape(b, nc, MLSTM_CHUNK, MLSTM_HEADS).transpose(1, 0, 3, 2)

    qc, kc, vc = to_chunks(q), to_chunks(k), to_chunks(v)
    ic = gate_chunks(i_pre)
    lfc = jax.nn.log_sigmoid(gate_chunks(f_pre))
    causal = jnp.tril(jnp.ones((MLSTM_CHUNK, MLSTM_CHUNK), dtype=bool))

    def step(carry, inp):
        c_prev, n_prev, m_prev = carry
        q_, k_, v_, i_, lf_ = inp
        cum = jnp.cumsum(lf_, axis=-1)
        logw = cum[..., :, None] - cum[..., None, :] + i_[..., None, :]
        logw = jnp.where(causal, logw, -jnp.inf)
        log_inter = cum + m_prev[..., None]
        m_t = jnp.maximum(log_inter, jnp.max(logw, axis=-1))
        w_intra = jnp.exp(logw - m_t[..., None])
        w_inter = jnp.exp(log_inter - m_t)
        sc = jnp.einsum('bhtd,bhsd->bhts', q_, k_) * w_intra
        num = jnp.einsum('bhts,bhsv->bhtv', sc, v_) + w_inter[..., None] * jnp.einsum('bhtd,bhdv->bhtv', q_, c_prev)
        den = jnp.sum(sc, axis=-1) + w_inter * jnp.einsum('bhtd,bhd->bht', q_, n_prev)
        h = num / jnp.maximum(jnp.abs(den), jnp.exp(-m_t))[..., None]
        total = cum[..., -1]
        log_k = total[..., None] - cum + i_
        m_new = jnp.maximum(total + m_prev, jnp.max(log_k, axis=-1))
        wk = jnp.exp(log_k - m_new[..., None])
        decay = jnp.exp(total + m_prev - m_new)
        c_new = decay[..., None, None] * c_prev + jnp.einsum('bhs,bhsd,bhsv->bhdv', wk, k_, v_)
        n_new = decay[..., None] * n_prev + jnp.einsum('bhs,bhsd->bhd', wk, k_)
        return (c_new, n_new, m_new), h

    init = (jnp.zeros((b, MLSTM_HEADS, MLSTM_QK_DIM, MLSTM_V_DIM), f32),
            jnp.zeros((b, MLSTM_HEADS, MLSTM_QK_DIM), f32),
            jnp.zeros((b, MLSTM_HEADS), f32))
    _, hs = lax.scan(step, init, (qc, kc, vc, ic, lfc))
    return hs.transpose(1, 0, 3, 2, 4).reshape(b, s, MLSTM_HEADS, MLSTM_V_DIM)

def softcap(t):
    return GATE_SOFTCAP * jnp.tanh(t / GATE_SOFTCAP)

def first_inputs(seed: int = 0) -> dict:
    key = jax.random.key(seed)
    ks = jax.random.split(key, 24)
    f32 = jnp.float32

    def dense(k, fan_in, fan_out):
        return jax.random.normal(k, (DEPTH, fan_in, fan_out), f32) * fan_in ** -0.5

    def gain(k, shape):
        return 1.0 + 0.05 * jax.random.normal(k, shape, f32)

    b_in = 0.02 * jax.random.normal(ks[7], (DEPTH, IN_WIDTH), f32)
    f_bias = jnp.linspace(3.0, 6.0, MLSTM_HEADS, dtype=f32)
    b_in = b_in.at[:, F_OFFSET:F_OFFSET + SZ_MF].add(f_bias)
    return {
        "x": jax.random.normal(ks[0], (BATCH, SEQ, D_MODEL), f32),
        "ffn1_norm": gain(ks[1], (DEPTH, D_MODEL)),
        "ffn1_w_gate": dense(ks[2], D_MODEL, D_FF),
        "ffn1_w_up": dense(ks[3], D_MODEL, D_FF),
        "ffn1_w_down": dense(ks[4], D_FF, D_MODEL),
        "mix_norm": gain(ks[5], (DEPTH, D_MODEL)),
        "w_in": dense(ks[6], D_MODEL, IN_WIDTH),
        "b_in": b_in,
        "attn_sinks": 0.5 * jax.random.normal(ks[8], (DEPTH, ATTN_HEADS), f32),
        "mlstm_conv": jax.random.normal(ks[9], (DEPTH, CONV_WIDTH, SZ_MQ + SZ_MK), f32) * CONV_WIDTH ** -0.5,
        "mlstm_head_norm": gain(ks[10], (DEPTH, MLSTM_HEADS, MLSTM_V_DIM)),
        "w_proj_attn": dense(ks[11], SZ_AQ, D_MODEL),
        "w_proj_mlstm": dense(ks[12], SZ_MV, D_MODEL),
        "w_out": dense(ks[13], D_MODEL, D_MODEL),
        "ffn2_norm": gain(ks[14], (DEPTH, D_MODEL)),
        "ffn2_w_gate": dense(ks[15], D_MODEL, D_FF),
        "ffn2_w_up": dense(ks[16], D_MODEL, D_FF),
        "ffn2_w_down": dense(ks[17], D_FF, D_MODEL),
        "final_norm": gain(ks[18], (D_MODEL,)),
    }

def first_block(x, ffn1_norm, ffn1_w_gate, ffn1_w_up, ffn1_w_down, mix_norm, w_in, b_in,
              attn_sinks, mlstm_conv, mlstm_head_norm, w_proj_attn, w_proj_mlstm, w_out,
              ffn2_norm, ffn2_w_gate, ffn2_w_up, ffn2_w_down, final_norm):
    b, s, _ = x.shape
    for l in range(DEPTH):
        h = rms_norm(x, ffn1_norm[l])
        x = x + FFN_RESIDUAL_WEIGHT * swiglu(h, ffn1_w_gate[l], ffn1_w_up[l], ffn1_w_down[l])

        h = rms_norm(x, mix_norm[l])
        z = h @ w_in[l] + b_in[l]
        a_q, a_k, a_v, m_q, m_k, m_v, m_o, m_i, m_f, g_pre = jnp.split(z, SPLIT_POINTS, axis=-1)

        y_attn = sliding_window_attention(
            a_q.reshape(b, s, ATTN_HEADS, ATTN_HEAD_DIM),
            a_k.reshape(b, s, ATTN_KV_HEADS, ATTN_HEAD_DIM),
            a_v.reshape(b, s, ATTN_KV_HEADS, ATTN_HEAD_DIM),
            attn_sinks[l]) @ w_proj_attn[l]

        qk = jax.nn.silu(causal_depthwise_conv(jnp.concatenate([m_q, m_k], axis=-1), mlstm_conv[l]))
        mq = qk[..., :SZ_MQ].reshape(b, s, MLSTM_HEADS, MLSTM_QK_DIM)
        mk = qk[..., SZ_MQ:].reshape(b, s, MLSTM_HEADS, MLSTM_QK_DIM) * MLSTM_QK_DIM ** -0.5
        mv = m_v.reshape(b, s, MLSTM_HEADS, MLSTM_V_DIM)
        hm = mlstm_chunkwise(mq, mk, mv,
                             softcap(m_i.astype(jnp.float32)), softcap(m_f.astype(jnp.float32)))
        hm = rms_norm(hm, mlstm_head_norm[l]).reshape(b, s, SZ_MV)
        hm = (jax.nn.sigmoid(m_o.astype(jnp.float32)) * hm).astype(x.dtype)
        y_mlstm = hm @ w_proj_mlstm[l]

        gates = jax.nn.sigmoid(g_pre.astype(jnp.float32)).astype(x.dtype).reshape(b, s, 2, D_MODEL)
        merged = gates[:, :, 0] * y_attn + gates[:, :, 1] * y_mlstm
        x = x + merged @ w_out[l]

        h = rms_norm(x, ffn2_norm[l])
        x = x + FFN_RESIDUAL_WEIGHT * swiglu(h, ffn2_w_gate[l], ffn2_w_up[l], ffn2_w_down[l])
    return rms_norm(x, final_norm)


MEM_TOKENS = 256
EPS = 1e-6
GLA_HEADS = 4
GLA_DK = 64
GLA_DV = 128
GLA_GATE_RANK = 16
GLA_GATE_NORM = 16.0
GLA_CHUNK = 64
MLA_HEADS = 8
MLA_Q_RANK = 256
MLA_KV_RANK = 128
MLA_NOPE = 64
MLA_ROPE = 32
MLA_QK = MLA_NOPE + MLA_ROPE
MLA_V = 64
ROPE_THETA = 10000.0
Q_BLOCK = 128
XA_HEADS = 4
XA_HEAD_DIM = 128
D_FF_2 = 2816
CONV_W = 3

GLA_QK_W = GLA_HEADS * GLA_DK
GLA_V_W = GLA_HEADS * GLA_DV
MLA_OUT_W = MLA_HEADS * MLA_V
MIX_WIDTH = GLA_V_W + MLA_OUT_W
IN_SPLITS = (GLA_QK_W, GLA_QK_W, GLA_V_W, GLA_GATE_RANK, GLA_V_W, MLA_Q_RANK, MLA_KV_RANK, MLA_ROPE)
IN_WIDTH_2 = int(sum(IN_SPLITS))
IN_SPLIT_POINTS = tuple(int(p) for p in np.cumsum(IN_SPLITS)[:-1])


def rms_norm_2(x, g):
    xf = x.astype(jnp.float32)
    y = xf * lax.rsqrt(jnp.mean(xf * xf, axis=-1, keepdims=True) + EPS)
    return (y * g.astype(jnp.float32)).astype(x.dtype)

def to_heads(t, n_heads):
    b, s, _ = t.shape
    return t.reshape(b, s, n_heads, -1).transpose(0, 2, 1, 3)

def from_heads(t):
    b, h, s, d = t.shape
    return t.transpose(0, 2, 1, 3).reshape(b, s, h * d)

def rope(x, pos):
    half = x.shape[-1] // 2
    inv = ROPE_THETA ** (-jnp.arange(half, dtype=jnp.float32) / half)
    ang = pos.astype(jnp.float32)[:, None, :, None] * inv
    cos, sin = jnp.cos(ang), jnp.sin(ang)
    xf = x.astype(jnp.float32)
    x1, x2 = xf[..., :half], xf[..., half:]
    return jnp.concatenate([x1 * cos - x2 * sin, x2 * cos + x1 * sin], axis=-1).astype(x.dtype)

def gla_chunked(q, k, v, log_a):
    b, h, s, dk = q.shape
    dv = v.shape[-1]
    c = GLA_CHUNK
    n = s // c
    rs = lambda t: t.reshape(b, h, n, c, t.shape[-1]).astype(jnp.float32)
    qf, kf, vf, la = rs(q) * (GLA_DK ** -0.5), rs(k), rs(v), rs(log_a)
    cum = jnp.cumsum(la, axis=3)
    cum_last = cum[:, :, :, -1:]
    q_dec = qf * jnp.exp(cum)
    k_inv = kf * jnp.exp(-cum)
    k_end = kf * jnp.exp(cum_last - cum)
    att = jnp.einsum('bhnik,bhnjk->bhnij', q_dec, k_inv)
    causal = jnp.tril(jnp.ones((c, c), dtype=bool))
    att = jnp.where(causal, att, 0.0)
    o_intra = jnp.einsum('bhnij,bhnjv->bhniv', att, vf)
    d_state = jnp.einsum('bhnjk,bhnjv->nbhkv', k_end, vf)
    decay = jnp.exp(cum_last[:, :, :, 0]).transpose(2, 0, 1, 3)

    def step(state, inp):
        d, ds = inp
        return d[..., None] * state + ds, state

    _, s_prev = lax.scan(step, jnp.zeros((b, h, dk, dv), jnp.float32), (decay, d_state))
    o_inter = jnp.einsum('bhnik,nbhkv->bhniv', q_dec, s_prev)
    return (o_intra + o_inter).reshape(b, h, s, dv)

def causal_block_attention(q, k, v):
    b, h, s, d = q.shape
    dv = v.shape[-1]
    nb = s // Q_BLOCK
    scale = d ** -0.5
    qb = q.reshape(b, h, nb, Q_BLOCK, d).transpose(2, 0, 1, 3, 4)
    starts = jnp.arange(nb, dtype=jnp.int32) * Q_BLOCK
    key_idx = jnp.arange(s, dtype=jnp.int32)
    kf = k.astype(jnp.float32)
    vf = v.astype(jnp.float32)

    def one_block(args):
        qi, s0 = args
        sc = jnp.einsum('bhqd,bhkd->bhqk', qi.astype(jnp.float32), kf) * scale
        q_idx = s0 + jnp.arange(Q_BLOCK, dtype=jnp.int32)
        sc = jnp.where(key_idx[None, :] <= q_idx[:, None], sc, -jnp.inf)
        p = jax.nn.softmax(sc, axis=-1)
        return jnp.einsum('bhqk,bhkd->bhqd', p, vf)

    out = lax.map(one_block, (qb, starts))
    return out.transpose(1, 2, 0, 3, 4).reshape(b, h, s, dv).astype(v.dtype)

def second_inputs(seed: int = 0) -> dict:
    key = jax.random.key(seed)
    ks = jax.random.split(key, 32)
    L, D, F = DEPTH, D_MODEL, D_FF_2

    def w(k, shape, fan_in):
        return jax.random.normal(k, shape, jnp.float32) * (fan_in ** -0.5)

    def gain(k, shape):
        return 1.0 + 0.02 * jax.random.normal(k, shape, jnp.float32)

    x = jax.random.normal(ks[0], (BATCH, SEQ, D), jnp.float32)
    mem = jax.random.normal(ks[1], (BATCH, MEM_TOKENS, D), jnp.float32)
    positions = (jnp.arange(SEQ, dtype=jnp.int32)[None, :]
                 + jax.random.randint(ks[2], (BATCH, 1), 0, 1024, dtype=jnp.int32))
    return {
        "x": x,
        "mem": mem,
        "positions": positions,
        "norm_mix": gain(ks[3], (L, D)),
        "w_in": w(ks[4], (L, D, IN_WIDTH_2), D),
        "gla_gate_w2": w(ks[5], (L, GLA_GATE_RANK, GLA_QK_W), GLA_GATE_RANK),
        "gla_gate_b": 0.1 * jax.random.normal(ks[6], (L, GLA_QK_W), jnp.float32),
        "gla_out_norm": gain(ks[7], (L, GLA_DV)),
        "mla_q_a_norm": gain(ks[8], (L, MLA_Q_RANK)),
        "mla_w_uq": w(ks[9], (L, MLA_Q_RANK, MLA_HEADS * MLA_QK), MLA_Q_RANK),
        "mla_kv_a_norm": gain(ks[10], (L, MLA_KV_RANK)),
        "mla_w_ukv": w(ks[11], (L, MLA_KV_RANK, MLA_HEADS * (MLA_NOPE + MLA_V)), MLA_KV_RANK),
        "mla_q_norm": gain(ks[12], (L, MLA_QK)),
        "mla_k_norm": gain(ks[13], (L, MLA_QK)),
        "w_out": w(ks[14], (L, MIX_WIDTH, D), MIX_WIDTH),
        "norm_xa": gain(ks[15], (L, D)),
        "norm_mem": gain(ks[16], (L, D)),
        "xa_w_q": w(ks[17], (L, D, XA_HEADS * XA_HEAD_DIM), D),
        "xa_w_kv": w(ks[18], (L, D, 2 * XA_HEADS * XA_HEAD_DIM), D),
        "xa_q_norm": gain(ks[19], (L, XA_HEAD_DIM)),
        "xa_k_norm": gain(ks[20], (L, XA_HEAD_DIM)),
        "xa_w_o": w(ks[21], (L, XA_HEADS * XA_HEAD_DIM, D), XA_HEADS * XA_HEAD_DIM),
        "norm_ffn": gain(ks[22], (L, D)),
        "ffn_w_gate": w(ks[23], (L, D, F), D),
        "ffn_w_up": w(ks[24], (L, D, F), D),
        "ffn_conv_w": w(ks[25], (L, CONV_W, F), CONV_W),
        "ffn_conv_b": 0.02 * jax.random.normal(ks[26], (L, F), jnp.float32),
        "ffn_w_down": w(ks[27], (L, F, D), F),
    }

def second_block(x, mem, positions, norm_mix, w_in, gla_gate_w2, gla_gate_b, gla_out_norm,
              mla_q_a_norm, mla_w_uq, mla_kv_a_norm, mla_w_ukv, mla_q_norm, mla_k_norm, w_out,
              norm_xa, norm_mem, xa_w_q, xa_w_kv, xa_q_norm, xa_k_norm, xa_w_o,
              norm_ffn, ffn_w_gate, ffn_w_up, ffn_conv_w, ffn_conv_b, ffn_w_down):
    b, s, _ = x.shape
    h = x
    for l in range(DEPTH):
        xn = rms_norm_2(h, norm_mix[l])
        proj = xn @ w_in[l]
        g_q, g_k, g_v, g_alr, g_og, c_q, c_kv, k_pe = jnp.split(proj, IN_SPLIT_POINTS, axis=-1)

        gate_logit = (g_alr @ gla_gate_w2[l] + gla_gate_b[l]).astype(jnp.float32)
        log_a = jax.nn.log_sigmoid(gate_logit) / GLA_GATE_NORM
        o_gla = gla_chunked(to_heads(g_q, GLA_HEADS), to_heads(g_k, GLA_HEADS),
                            to_heads(g_v, GLA_HEADS), to_heads(log_a, GLA_HEADS))
        o_gla = rms_norm_2(o_gla, gla_out_norm[l]).astype(h.dtype)
        o_gla = from_heads(o_gla) * jax.nn.silu(g_og)

        q = to_heads(rms_norm_2(c_q, mla_q_a_norm[l]) @ mla_w_uq[l], MLA_HEADS)
        kv = to_heads(rms_norm_2(c_kv, mla_kv_a_norm[l]) @ mla_w_ukv[l], MLA_HEADS)
        k_nope, v = kv[..., :MLA_NOPE], kv[..., MLA_NOPE:]
        k_rot = jnp.broadcast_to(k_pe[:, None], (b, MLA_HEADS, s, MLA_ROPE))
        k = jnp.concatenate([k_nope, k_rot], axis=-1)
        q = rms_norm_2(q, mla_q_norm[l])
        k = rms_norm_2(k, mla_k_norm[l])
        q = jnp.concatenate([q[..., :MLA_NOPE], rope(q[..., MLA_NOPE:], positions)], axis=-1)
        k = jnp.concatenate([k[..., :MLA_NOPE], rope(k[..., MLA_NOPE:], positions)], axis=-1)
        o_mla = from_heads(causal_block_attention(q, k, v))

        h = h + jnp.concatenate([o_gla, o_mla], axis=-1) @ w_out[l]

        hn = rms_norm_2(h, norm_xa[l])
        mn = rms_norm_2(mem, norm_mem[l])
        xq = rms_norm_2((hn @ xa_w_q[l]).reshape(b, s, XA_HEADS, XA_HEAD_DIM), xa_q_norm[l])
        xkv = (mn @ xa_w_kv[l]).reshape(b, mem.shape[1], 2, XA_HEADS, XA_HEAD_DIM)
        xk = rms_norm_2(xkv[:, :, 0], xa_k_norm[l])
        xv = xkv[:, :, 1]
        sc = jnp.einsum('bqhd,bkhd->bhqk', xq.astype(jnp.float32), xk.astype(jnp.float32)) * (XA_HEAD_DIM ** -0.5)
        p = jax.nn.softmax(sc, axis=-1)
        xo = jnp.einsum('bhqk,bkhd->bqhd', p, xv.astype(jnp.float32)).astype(h.dtype)
        h = h + xo.reshape(b, s, XA_HEADS * XA_HEAD_DIM) @ xa_w_o[l]

        fn = rms_norm_2(h, norm_ffn[l])
        g = fn @ ffn_w_gate[l]
        g_pad = jnp.pad(g, ((0, 0), (CONV_W - 1, 0), (0, 0)))
        cw = ffn_conv_w[l]
        g_conv = ffn_conv_b[l] + sum(cw[i] * g_pad[:, i:i + s] for i in range(CONV_W))
        h = h + (jax.nn.silu(g_conv) * (fn @ ffn_w_up[l])) @ ffn_w_down[l]
    return h


def setup_inputs(seed=0):
    out = dict(first_inputs(seed))
    for name, value in second_inputs(seed + 1).items():
        if name != "x":
            out[name + "_2"] = value
    return out


def reference(
    x, ffn1_norm, ffn1_w_gate, ffn1_w_up, ffn1_w_down, mix_norm, w_in, b_in, attn_sinks,
    mlstm_conv, mlstm_head_norm, w_proj_attn, w_proj_mlstm, w_out, ffn2_norm, ffn2_w_gate,
    ffn2_w_up, ffn2_w_down, final_norm, mem_2, positions_2, norm_mix_2, w_in_2, gla_gate_w2_2,
    gla_gate_b_2, gla_out_norm_2, mla_q_a_norm_2, mla_w_uq_2, mla_kv_a_norm_2, mla_w_ukv_2,
    mla_q_norm_2, mla_k_norm_2, w_out_2, norm_xa_2, norm_mem_2, xa_w_q_2, xa_w_kv_2,
    xa_q_norm_2, xa_k_norm_2, xa_w_o_2, norm_ffn_2, ffn_w_gate_2, ffn_w_up_2, ffn_conv_w_2,
    ffn_conv_b_2, ffn_w_down_2,
):
    x = first_block(
        x, ffn1_norm, ffn1_w_gate, ffn1_w_up, ffn1_w_down, mix_norm, w_in, b_in, attn_sinks,
        mlstm_conv, mlstm_head_norm, w_proj_attn, w_proj_mlstm, w_out, ffn2_norm, ffn2_w_gate,
        ffn2_w_up, ffn2_w_down, final_norm,
    )
    return second_block(
        x, mem_2, positions_2, norm_mix_2, w_in_2, gla_gate_w2_2, gla_gate_b_2, gla_out_norm_2,
        mla_q_a_norm_2, mla_w_uq_2, mla_kv_a_norm_2, mla_w_ukv_2, mla_q_norm_2, mla_k_norm_2,
        w_out_2, norm_xa_2, norm_mem_2, xa_w_q_2, xa_w_kv_2, xa_q_norm_2, xa_k_norm_2, xa_w_o_2,
        norm_ffn_2, ffn_w_gate_2, ffn_w_up_2, ffn_conv_w_2, ffn_conv_b_2, ffn_w_down_2,
    )


_drawn_inputs = setup_inputs


def setup_inputs(seed=0):
    import zlib

    import numpy as np

    out = dict(_drawn_inputs(seed))
    spreads = {}
    factors = {'attn_sinks': 7.427,
     'mlstm_head_norm': 2.941,
     'norm_mix_2': 3.087,
     'gla_gate_b_2': 2.87,
     'gla_out_norm_2': 7.546,
     'mla_q_a_norm_2': 8.0,
     'mla_kv_a_norm_2': 8.0,
     'mla_q_norm_2': 8.0,
     'mla_k_norm_2': 8.0,
     'norm_xa_2': 8.0,
     'norm_mem_2': 8.0,
     'xa_q_norm_2': 8.0,
     'xa_k_norm_2': 8.0,
     'norm_ffn_2': 13.47,
     'ffn_conv_b_2': 18.749}
    for name, (base, spread) in spreads.items():
        noise = np.random.default_rng([zlib.crc32(name.encode()), seed]).standard_normal(out[name].shape)
        drawn = base * np.exp(spread * noise) if base else spread * noise
        out[name] = __import__('jax').numpy.asarray(drawn.astype(out[name].dtype))
    for name, factor in factors.items():
        out[name] = (out[name] * factor).astype(out[name].dtype)
    return out
```

```python
import numpy as np
import concourse.bass as bass
from concourse import mybir
from contextlib import ExitStack

P = 128
T = 256
TB = T // P
D = 1024
DC = D // P
FF = 2816
FC = FF // P
FP = FC // 2
SLAB = 11 * 256
VEC_LOADS, SMALL_LOADS = 28, 9
EPS = 1e-6
NEG = -1.0e30

C_ID, C_ONE = 0, 128
C_PREV, C_OWN, C_ZERO, C_OWN2 = 256, 384, 512, 768
C_RESET, C_GLA, C_SEL, C_HOT = 896, 1152, 1280, 2304
C_INV, C_SIGN, C_EPS = 2368, 2369, 2370
C_ALL = 2371

V_FFN1, V_MIX, V_FFN2, V_FINAL, V_MIX2, V_XA, V_MEM, V_FFN3 = 0, 8, 16, 24, 32, 40, 48, 56
V_BQ, V_BK, V_BMQK, V_BMO, V_BG = 64, 72, 74, 82, 90
V_HEAD, V_GATEB, V_GLA, V_QA, V_KVA, V_XQ, V_XK, V_MLAQ, V_MLAK = 106, 114, 116, 117, 119, 120, 121, 122, 123
VEC0 = 124
V_FCW, V_FCB, V_MCONV = 128, 128 + 3 * FC, 128 + 4 * FC
VEC1 = 4 * FC + 32

I_AQ, I_AK, I_AV, I_MQK, I_MV, I_MO, I_MI, I_G = 0, 1024, 1280, 1536, 2560, 3584, 4608, 4624
J_Q, J_K, J_V, J_ALR, J_OG, J_CQ, J_CKV, J_PE = 0, 256, 512, 1024, 1040, 1552, 1808, 1936

STAGES = [("f1u", 22, 22), ("f1d", 8, 4), ("wq", 4, 4), ("wkv", 2, 2), ("wmqk", 4, 4), ("wmv", 4, 4),
          ("wmo", 4, 4), ("wg", 8, 8), ("proj", 8, 8), ("wo", 4, 4), ("f2u", 22, 22), ("f2d", 8, 4),
          ("w2", 8, 8), ("uq", 1, 4), ("ukv", 1, 6), ("wo2", 4, 4), ("xq", 2, 2), ("xk", 2, 2),
          ("xv", 2, 2), ("xo", 4, 4), ("f3u", 22, 22), ("f3d", 8, 4)]


def first_numbers():
    slab, acc, s, n = {}, {}, 0, 0
    for name, slabs, accs in STAGES:
        slab[name], acc[name] = s, n
        s, n = s + slabs, n + accs
    return slab, acc, s


def shared_signals():
    kinds = [
        ("norm", ("sq", "sum", "std"), (4, 1, 1), [(f"n{k}", 1) for k in range(1, 9)]),
        ("norm", ("xn", "hi", "lo"), (4, 4, 4), [(f"n{k}", 1) for k in (1, 2, 3, 5, 6, 7, 8)]),
        ("softmax", ("mx", "ex", "pn", "sc", "tp", "pt", "pv", "yo"), (4, 4, 4, 1, 1, 1, 1, 1), [("at", 8), ("ml", 4), ("xa", 2)]),
        ("ff", ("hh", "hl"), (1, 1), [("f1u", FP), ("f2u", FP), ("f3u", FP)]),
    ]
    found = {}
    for kind, signals, each, stages in kinds:
        for sig, n in zip(signals, each):
            base = 0
            for st, units in stages:
                found[f"{st}_{sig}"] = (f"{kind}_{sig}", base)
                base += n * units
    return found


SHARED = shared_signals()


def shape_constants():
    c = np.zeros((P, C_ALL), np.float32)
    i = np.arange(P)
    c[i, C_ID + i] = 1
    c[:, C_ONE:C_ONE + P] = 1
    q, k = i[:, None], i[None, :]
    c[:, C_PREV:C_PREV + P] = np.where(k > q, 0, NEG)
    c[:, C_OWN:C_OWN + P] = np.where(k <= q, 0, NEG)
    c[:, C_OWN2:C_OWN2 + P] = np.where(k <= q, 0, NEG)
    c[:, C_RESET:C_RESET + T] = np.arange(T) % 64 != 0
    c[:, C_GLA:C_GLA + P] = (q // 64 == k // 64) & (q <= k)
    for h in range(8):
        c[h, C_SEL + h * P:C_SEL + (h + 1) * P] = 1
        c[:, C_HOT + h * 8 + h] = 1
    c[:, C_INV] = np.float32(10000.0) ** (-(i % 16).astype(np.float32) / np.float32(16))
    c[:, C_SIGN] = np.where((i // 16) % 2 == 0, -1, 1)
    c[:, C_EPS] = EPS
    return c


def build(nc, A, consts, out):
    f32, f32r, i32 = mybir.dt.float32, mybir.dt.float32r, mybir.dt.int32
    ALU, ACT = mybir.AluOpType, mybir.ActivationFunctionType
    MUL, ADD, SUB, MAX, MIN = ALU.mult, ALU.add, ALU.subtract, ALU.max, ALU.min
    SLAB0, ACC0, SLABS = first_numbers()
    ctx = ExitStack()
    with ctx:
        def sb(name, shape, dt=f32, scope=ctx):
            return scope.enter_context(nc.sbuf_tensor(name, shape, dt))

        sems = {}

        def S(name):
            name = SHARED.get(name, (name, 0))[0]
            if name not in sems:
                sems[name] = ctx.enter_context(nc.semaphore("s_" + name))
            return sems[name]

        def signal(name, count):
            return S(name), SHARED.get(name, (name, 0))[1] + count

        raw = sb("raw", [P, 2, SLAB])
        wh = sb("wh", [P, 2, SLAB], f32r)
        wl = sb("wl", [P, 2, SLAB], f32r)
        xT = sb("xT", [P, DC, T])
        ah = sb("ah", [P, DC, T], f32r)
        al = sb("al", [P, DC, T], f32r)
        xn = sb("xn", [P, DC, T])
        sq = sb("sq", [P, 4, 512])
        cst = sb("cst", [P, C_ALL])
        vec = sb("vec", [P, 256])
        std = sb("std", [P, 512])
        rstd = sb("rstd", [P, 512])
        bav = sb("bav", [P, 256])
        bmv = sb("bmv", [P, 1024])
        nsink = sb("nsink", [P, 32])
        wif = sb("wif", [P, DC, 16])
        walr = sb("walr", [P, DC, 16])
        w2g = sb("w2g", [16, 256])
        bif = sb("bif", [8, 4])
        nege = sb("nege", [P, 8])
        rope_c = sb("rope_c", [P, T])
        rope_s = sb("rope_s", [P, T])
        rmx = sb("rmx", [P, 2, 4])
        rsm = sb("rsm", [P, 2, 4])
        rs2 = sb("rs2", [P, 2, 4])
        rin = sb("rin", [P, 2, 4])

        with ExitStack() as sc:
            xraw = sb("xraw", [P, TB, D], scope=sc)
            vraw = sb("vraw", [P, 2, P], scope=sc)
            posi = sb("posi", [P, T], i32, scope=sc)
            ang = sb("ang", [P, T], scope=sc)
            turn = sb("turn", [P, T], scope=sc)
            tmpr = sb("tmpr", [P, T], scope=sc)
            quarter = sb("quarter", [P, T], scope=sc)
        with ExitStack() as sc:
            hh = sb("hh", [P, FC, T], f32r, scope=sc)
            hl = sb("hl", [P, FC, T], f32r, scope=sc)
            sil = sb("sil", [P, 512], scope=sc)
            hid = sb("hid", [P, 512], scope=sc)
            gpad = sb("gpad", [P, 2, T + 2], scope=sc)
            gcv = sb("gcv", [P, 512], scope=sc)
        with ExitStack() as sc:
            sigo = sb("sigo", [P, 8, T], scope=sc)
            gate = sb("gate", [P, 16, T], scope=sc)
            with ExitStack() as s2:
                aq = sb("aq", [P, 8, T], scope=s2)
                qk = sb("qk", [P, 8, T], scope=s2)
                mv = sb("mv", [P, TB, D], scope=s2)
                akd = sb("akd", [P, 4, T], scope=s2)
                av = sb("av", [P, TB, 256], scope=s2)
                with ExitStack() as s3:
                    pad = sb("pad", [P, 8, T + 3], scope=s3)
                with ExitStack() as s3:
                    prob1 = sb("prob1", [P, 2, 4, T], scope=s3)
                    probT1 = sb("probT1", [P, 2, 512], scope=s3)
                with ExitStack() as s3:
                    wm = sb("wm", [P, 8, 384], scope=s3)
                    gtok = sb("gtok", [P, TB, 16], scope=s3)
                    acol = sb("acol", [P, TB, 8], scope=s3)
                    ti = sb("ti", [8, 512], scope=s3)
                    lse = sb("lse", [8, T], scope=s3)
                    Gc = sb("Gc", [8, T], scope=s3)
                    ai = sb("ai", [8, T], scope=s3)
                    Mx = sb("Mx", [8, T], scope=s3)
                    gm = sb("gm", [8, T], scope=s3)
                    en = sb("en", [8, T], scope=s3)
                    rden = sb("rden", [8, T], scope=s3)
            with ExitStack() as s2:
                bh = sb("bh", [P, DC, T], f32r, scope=s2)
                bl = sb("bl", [P, DC, T], f32r, scope=s2)
                ch = sb("ch", [P, DC, T], f32r, scope=s2)
                cl = sb("cl", [P, DC, T], f32r, scope=s2)
                mga = sb("mga", [P, 512], scope=s2)
                mgb = sb("mgb", [P, 512], scope=s2)
                mgs = sb("mgs", [P, 512], scope=s2)
        with ExitStack() as sc:
            cq = sb("cq", [P, 2, T], scope=sc)
            ckv = sb("ckv", [P, T], scope=sc)
            kpe = sb("kpe", [P, T], scope=sc)
            oh = sb("oh", [P, DC, T], f32r, scope=sc)
            ol = sb("ol", [P, DC, T], f32r, scope=sc)
            st8 = sb("st8", [8, 512], scope=sc)
            r8 = sb("r8", [8, 512], scope=sc)
            with ExitStack() as s2:
                gq = sb("gq", [P, 2, T], scope=s2)
                gk = sb("gk", [P, 2, T], scope=s2)
                gv = sb("gv", [P, TB, 512], scope=s2)
                sog = sb("sog", [P, 4, T], scope=s2)
                alr = sb("alr", [16, T], scope=s2)
                zg = sb("zg", [P, 512], scope=s2)
                lg = sb("lg", [P, 512], scope=s2)
                cum = sb("cum", [P, 512], scope=s2)
                eg = sb("eg", [P, 3, 512], scope=s2)
                qd = sb("qd", [P, 2, T], scope=s2)
                ki = sb("ki", [P, 2, T], scope=s2)
                ke = sb("ke", [P, 2, T], scope=s2)
                ketok = sb("ketok", [P, TB, 256], scope=s2)
                att = sb("att", [P, 2, 512], scope=s2)
                dec = sb("dec", [P, 8], scope=s2)
                stt_ = sb("stt_", [P, 3, 2, P], scope=s2)
            with ExitStack() as s2:
                qh = sb("qh", [P, 8, T], scope=s2)
                kh = sb("kh", [P, 8, T], scope=s2)
                vm = sb("vm", [P, TB, 512], scope=s2)
                cqh = sb("cqh", [P, 3, T], f32r, scope=s2)
                cql = sb("cql", [P, 3, T], f32r, scope=s2)
                prob2 = sb("prob2", [P, 2, 4, T], scope=s2)
                probT2 = sb("probT2", [P, 2, 512], scope=s2)
        with ExitStack() as sc:
            memraw = sb("memraw", [P, TB, D], scope=sc)
            mT = sb("mT", [P, DC, T], scope=sc)
            mh = sb("mh", [P, DC, T], f32r, scope=sc)
            ml = sb("ml", [P, DC, T], f32r, scope=sc)
            xq = sb("xq", [P, 8, T], scope=sc)
            xv = sb("xv", [P, TB, 512], scope=sc)
            sx8 = sb("sx8", [8, 512], scope=sc)
            rx8 = sb("rx8", [8, 512], scope=sc)
            prob3 = sb("prob3", [P, 2, 4, T], scope=sc)
            probT3 = sb("probT3", [P, 2, 512], scope=sc)
        with ExitStack() as sc:
            res = sb("res", [P, TB, D], scope=sc)

        L = [ctx.enter_context(nc.psum_tensor(f"acc{i}", [P, 512], f32)) for i in range(2)]
        Q = [ctx.enter_context(nc.psum_tensor(f"part{i}", [P, 512], f32)) for i in range(6)]

        ident = cst[:, C_ID:C_ID + P]
        ones = cst[:, C_ONE:C_ONE + P]
        eps = cst[:, C_EPS:C_EPS + 1]

        def sel(h):
            return cst[0:8, C_SEL + h * P:C_SEL + (h + 1) * P]

        def hot(h, rows=P):
            return cst[0:rows, C_HOT + h * 8:C_HOT + (h + 1) * 8]

        def col(n, lo=0, hi=P):
            return vec[lo:hi, n:n + 1]

        def pairs(t, j):
            return t[:, 2 * j:2 * j + 2, :].rearrange("p c t -> p (c t)")

        def rpair(t, j):
            return t[:, :, :].rearrange("p c t -> p (c t)")[:, bass.ds(j * 512, 512)]

        def f(ap):
            return ap.bitcast(f32)

        def loaded(eng, s, i=0):
            eng.wait_ge(*signal(f"raw{s % 2}", 16 * (s // 2 + 1) + 16 * i))

        def lo_ready(eng, s, i, half):
            eng.wait_ge(*signal("w_lo", 2 * s + half + 1 + 4 * i))

        def slab_used(eng, s, i=0, half=1):
            eng.wait_ge(*signal("w_used", 2 * s + half + 1 + 4 * i))

        def acc_freed(eng, n, i=0):
            eng.wait_ge(*signal(f"acc_free{n % 2}", n // 2 + 1 + i))

        def free_sem(n):
            return S(f"acc_free{n % 2}")

        def halves(nk):
            return (0, (nk + 1) // 2), ((nk + 1) // 2, nk)

        def looped(eng, n, body):
            if n > 2:
                with eng.Fori(0, n - 1) as i:
                    body(i, False)
            else:
                for i in range(n - 1):
                    body(i, False)
            body(n - 1, True)

        def columns(name):
            return {"f1d": 11, "f2d": 11, "f3d": 11, "xo": 4}.get(name, 8), 256

        EXTRA = {SLAB0["w2"] + 7: "pe", SLAB0["uq"]: "uq", SLAB0["ukv"]: "ukv"}
        STAGE_OF = {SLAB0[n] + k: n for n, c, _ in STAGES for k in range(c)}

        def shape_of(s):
            return columns(STAGE_OF[s]) if s in STAGE_OF else None

        def parts(kind, t, slot):
            r = raw[:, slot, :]
            w = t[:, slot, :]
            if kind == "pe":
                d = w[:, 0:2048].rearrange("p (k c) -> p k c", k=8)
                s = r[:, 0:8 * 160].rearrange("p (k c) -> p k c", k=8)
                return [(d[:, :, 0:160], s), (d[:, :, 160:192], s[:, :, 128:160]),
                        (d[:, :, 192:224], s[:, :, 128:160]), (d[:, :, 224:240], s[:, :, 144:160]),
                        (d[:, :, 240:256], s[:, :, 128:144])]
            if kind == "uq":
                d = w[:, 0:2048].rearrange("p (k c) -> p k c", k=16)
                s = r[:, 0:1536].rearrange("p (k c) -> p k c", k=16)
                return [(d[:, :, 0:96], s), (d[:, :, 96:112], s[:, :, 80:96]), (d[:, :, 112:128], s[:, :, 64:80])]
            return [(w[:, 0:512], r[:, 0:512]), (w[:, 512:1024], r[:, 512:1024])]

        def split_hi(act, s, i=0):
            if s >= SLABS:
                return
            loaded(act, s, i)
            slot = s % 2
            if s in EXTRA:
                slab_used(act, s - 2)
                todo = parts(EXTRA[s], wh, slot)
                for n, (d, r) in enumerate(todo):
                    ins = nc.scalar.activation(d, r, ACT.Copy)
                ins.then_inc(S("w_hi"), 2)
                return
            nk, nw = shape_of(s)
            for half, (a, b) in enumerate(halves(nk)):
                if s >= 2:
                    slab_used(act, s - 2, i, half if shape_of(s - 2) == (nk, nw) and s - 2 not in EXTRA else 1)
                nc.scalar.activation(wh[:, slot, a * nw:b * nw], raw[:, slot, a * nw:b * nw],
                                     ACT.Copy).then_inc(S("w_hi"), 1)

        def split_lo(dve, s, i=0):
            if s >= SLABS:
                return
            slot = s % 2
            if s in EXTRA:
                dve.wait_ge(*signal("w_hi", 2 * s + 2))
                for (d, r), (h, _) in zip(parts(EXTRA[s], wl, slot), parts(EXTRA[s], wh, slot)):
                    ins = nc.vector.tensor_tensor(d, r, f(h), SUB)
                ins.then_inc(S("w_lo"), 2)
                return
            nk, nw = shape_of(s)
            for half, (a, b) in enumerate(halves(nk)):
                dve.wait_ge(*signal("w_hi", 2 * s + half + 1 + 4 * i))
                nc.vector.tensor_tensor(wl[:, slot, a * nw:b * nw], raw[:, slot, a * nw:b * nw],
                                        f(wh[:, slot, a * nw:b * nw]), SUB).then_inc(S("w_lo"), 1)

        block = ctx.enter_context(nc.Block())

        @block.sync
        def _(sp):
            sp.dma_start(cst[:, :], consts).then_inc(S("consts"), 16)
            sp.dma_start(xraw[:, :, :], A["x"][0].rearrange("(b p) c -> p b c", p=P)).then_inc(S("x_in"), 16)
            win = A["w_in"][0].rearrange("(k p) c -> p k c", p=P)
            win2 = A["w_in_2"][0].rearrange("(k p) c -> p k c", p=P)

            def load(s, i, src, kind=None):
                if s >= 2:
                    sp.wait_ge(*signal("w_lo", 2 * s - 2 + 4 * i))
                nk, nw = shape_of(s)
                if kind == "pe":
                    d = raw[:, s % 2, 0:8 * 160].rearrange("p (k c) -> p k c", k=8)
                elif kind == "uq":
                    d = raw[:, s % 2, 0:1536].rearrange("p (k c) -> p k c", k=2)
                elif kind == "ukv":
                    d = raw[:, s % 2, 0:1024]
                else:
                    d = raw[:, s % 2, 0:nk * nw].rearrange("p (k c) -> p k c", k=nk)
                sp.dma_start(d, src).then_inc(S(f"raw{s % 2}"), 16)

            def many(name, w, first):
                s0, count = SLAB0[name], dict((n, c) for n, c, _ in STAGES)[name]

                def body(i):
                    for r in range(2):
                        load(s0 + r, i, w[:, :, bass.ds(first + i * 512 + r * 256, 256)])
                if count > 2:
                    with sp.Fori(0, count // 2) as i:
                        body(i)
                else:
                    body(0)

            def feed_forward(up, down, gate_w, up_w, down_w):
                g = gate_w.rearrange("(k p) c -> p k c", p=P)
                u = up_w.rearrange("(k p) c -> p k c", p=P)
                s0 = SLAB0[up]
                if s0 == 0:
                    load(0, 0, g[:, :, 0:256])
                    load(1, 0, u[:, :, 0:256])
                with sp.Fori(1 if s0 == 0 else 0, FP) as i:
                    for r, w in ((0, g), (1, u)):
                        sp.wait_ge(*signal("w_lo", 2 * (s0 + r) - 2 + 4 * i))
                        d = raw[:, (s0 + r) % 2, 0:2048].rearrange("p (k c) -> p k c", k=8)
                        sp.dma_start(d, w[:, :, bass.ds(i * 256, 256)]).then_inc(S(f"raw{(s0 + r) % 2}"), 16)
                d = down_w.rearrange("(k p) c -> p k c", p=P)
                s0 = SLAB0[down]
                with sp.Fori(0, 4) as i:
                    for r in range(2):
                        load(s0 + r, i, d[:, 11 * r:11 * r + 11, bass.ds(i * 256, 256)])

            feed_forward("f1u", "f1d", A["ffn1_w_gate"][0], A["ffn1_w_up"][0], A["ffn1_w_down"][0])
            many("wq", win, I_AQ)
            many("wkv", win, I_AK)
            many("wmqk", win, I_MQK)
            many("wmv", win, I_MV)
            many("wmo", win, I_MO)
            many("wg", win, I_G)
            pa = A["w_proj_attn"][0].rearrange("(k p) c -> p k c", p=P)
            pm = A["w_proj_mlstm"][0].rearrange("(k p) c -> p k c", p=P)
            with sp.Fori(0, 4) as i:
                for r, w in ((0, pa), (1, pm)):
                    load(SLAB0["proj"] + r, i, w[:, :, bass.ds(i * 256, 256)])
            many("wo", A["w_out"][0].rearrange("(k p) c -> p k c", p=P), 0)
            feed_forward("f2u", "f2d", A["ffn2_w_gate"][0], A["ffn2_w_up"][0], A["ffn2_w_down"][0])
            s0 = SLAB0["w2"]
            for k, c in enumerate((J_Q, J_K, J_V, J_V + 256, J_OG, J_OG + 256, J_CQ)):
                load(s0 + k, 0, win2[:, :, c:c + 256])
            load(s0 + 7, 0, win2[:, :, J_CKV:J_CKV + 160], "pe")
            load(SLAB0["uq"], 0, A["mla_w_uq_2"][0].rearrange("(k p) c -> p k c", p=P), "uq")
            load(SLAB0["ukv"], 0, A["mla_w_ukv_2"][0], "ukv")
            many("wo2", A["w_out_2"][0].rearrange("(k p) c -> p k c", p=P), 0)
            many("xq", A["xa_w_q_2"][0].rearrange("(k p) c -> p k c", p=P), 0)
            acc_freed(sp, ACC0["wo2"] + 2)
            acc_freed(sp, ACC0["wo2"] + 3)
            sp.dma_start(memraw[:, :, :], A["mem_2"][0].rearrange("(b p) c -> p b c", p=P)).then_inc(S("mem_in"), 16)
            kv = A["xa_w_kv_2"][0].rearrange("(k p) c -> p k c", p=P)
            many("xk", kv, 0)
            many("xv", kv, 512)
            many("xo", A["xa_w_o_2"][0].rearrange("(k p) c -> p k c", p=P), 0)
            feed_forward("f3u", "f3d", A["ffn_w_gate_2"][0], A["ffn_w_up_2"][0], A["ffn_w_down_2"][0])
            for tb in range(TB):
                sp.wait_ge(*signal("resa", tb + 1))
                sp.wait_ge(*signal("resd", tb + 1))
                sp.dma_start(out[0, tb * P:(tb + 1) * P, :], res[:, tb, :]).then_inc(S("stored"), 16)
            sp.wait_ge(*signal("stored", 16 * TB))

        @block.tensor
        def _(pe):
            mm = nc.tensor.matmul

            def norm(st, n=1):
                for j in range(4):
                    pe.wait_ge(*signal(st + "_sq", j + 1))
                    for c in range(2):
                        ins = mm(Q[0][:, 0:T], ones, sq[:, j, c * T:(c + 1) * T], start=j + c == 0, stop=j + c == 4)
                ins.then_inc(S(st + "_sum"), 1)

            def open_acc(n, i=0):
                if n >= 2:
                    acc_freed(pe, n - 2, i)

            def product(s, i, nk, n, xh, xl, k0=0, first=True, last=True, tokens=False):
                o, slot = L[n % 2], s % 2
                for half, (ka, kb) in enumerate(halves(nk)):
                    lo_ready(pe, s, i, half)
                    for k in range(ka, kb):
                        for m in range(2):
                            dst = o[:, m * T:(m + 1) * T]
                            st = first and k == 0 and m == 0
                            en_ = last and k == nk - 1 and m == 1
                            if tokens:
                                c = slice(k * 256, (k + 1) * 256)
                                t = slice(m * P, (m + 1) * P)
                                xa, xb = xh[:, k0 + k, t], xl[:, k0 + k, t]
                                three = ((xa, wh[:, slot, c]), (xb, wh[:, slot, c]), (xa, wl[:, slot, c]))
                            else:
                                c = slice(k * 256 + m * P, k * 256 + (m + 1) * P)
                                xa, xb = xh[:, k0 + k, :], xl[:, k0 + k, :]
                                three = ((wh[:, slot, c], xa), (wh[:, slot, c], xb), (wl[:, slot, c], xa))
                            for q, (a, b) in enumerate(three):
                                ins = mm(dst, a, b, start=st and q == 0, stop=en_ and q == 2, skip_group_check=True)
                    ins.then_inc(S("w_used"), 1)

            def two(name, xh, xl, nk=8, tokens=False, count=None):
                s, n = SLAB0[name], ACC0[name]
                count = count or dict((a, b) for a, b, _ in STAGES)[name]

                def body(i):
                    for r in range(2):
                        open_acc(n + r, i)
                        product(s + r, i, nk, n + r, xh, xl, tokens=tokens)
                if count > 2:
                    with pe.Fori(0, count // 2) as i:
                        body(i)
                else:
                    body(0)

            def feed_forward(up, down):
                s, n = SLAB0[up], ACC0[up]
                if n == 0:
                    product(s, 0, 8, n, ah, al)
                    product(s + 1, 0, 8, n + 1, ah, al)
                with pe.Fori(1 if n == 0 else 0, FP) as i:
                    for r in range(2):
                        pe.wait_ge(free_sem(n + r), (n + r - 2) // 2 + 1 + i)
                        product(s + r, i, 8, n + r, ah, al)
                s, n = SLAB0[down], ACC0[down]
                for q in range(4):
                    open_acc(n + q)
                    for r in range(2):
                        if q == 0:
                            pe.wait_ge(*signal(up + "_hl", FP if r else 6))
                        product(s + 2 * q + r, 0, 11, n + q, hh, hl, k0=11 * r, first=r == 0, last=r == 1)

            def attention(st, units, scores, prob, probT, values, outputs):
                U = len(units)

                def do_scores(u):
                    if u >= 1:
                        pe.wait_ge(*signal(st + "_mx", 4 * u))
                    for hh_ in range(4):
                        q, k = scores(u, hh_)
                        w = k.shape[1]
                        ins = mm(Q[hh_ % 2][:, (hh_ // 2) * 256:(hh_ // 2) * 256 + w], q, k,
                                 start=True, stop=True, skip_group_check=True)
                    ins.then_inc(S(st + "_sc"), 1)

                do_scores(0)
                for u, blocks in enumerate(units):
                    if u + 1 < U:
                        do_scores(u + 1)
                    if u >= 1:
                        pe.wait_ge(*signal(st + "_pt", u))
                    pe.wait_ge(*signal(st + "_pn", 4 * u + 4))
                    for b in range(blocks):
                        for hh_ in range(4):
                            ins = nc.tensor.transpose(Q[2 + b][:, hh_ * P:(hh_ + 1) * P],
                                                      prob[:, u % 2, hh_, b * P:(b + 1) * P], ident)
                    ins.then_inc(S(st + "_tp"), 1)
                    pe.wait_ge(*signal(st + "_pt", u + 1))
                    if u >= 2:
                        pe.wait_ge(*signal(st + "_yo", u - 1))
                    bank = Q[4 + u % 2]
                    for lo, hi, o0, hs in outputs:
                        for b in range(blocks):
                            v = values(u, b, hs[0])
                            x = probT[:, b, :].rearrange("p (h q) -> p h q", h=4)[:, hs[0]:hs[-1] + 1:max(1, (hs[-1] - hs[0])), :] \
                                if len(hs) > 1 else probT[:, b, hs[0] * P:(hs[0] + 1) * P]
                            ins = mm(bank[lo:hi, o0:o0 + P * len(hs)], v, x, start=b == 0 and o0 == 0,
                                     stop=b == blocks - 1, skip_group_check=True)
                    ins.then_inc(S(st + "_pv"), 1)

            def head_sums(st, x, heads, bank, o0, first, rows=P):
                for j in range(heads // 2):
                    pe.wait_ge(*signal(st + "_hs", j + 1))
                    for c in range(2):
                        h = 2 * j + c
                        ins = mm(bank[0:8, o0:o0 + T], hot(h, rows), x[0:rows, j, c * T:(c + 1) * T],
                                 start=first and h == 0, stop=h == heads - 1, skip_group_check=True)
                ins.then_inc(S(st + "_ss"), 1)

            def spread(st, r, o0, heads, banks, wait):
                for j in range(heads // 2):
                    wait(j)
                    for c in range(2):
                        h = 2 * j + c
                        ins = mm(banks[j % len(banks)][:, c * T:(c + 1) * T], sel(h), r[0:8, o0:o0 + T],
                                 start=c == 0, stop=c == 1, skip_group_check=True)
                    ins.then_inc(S(st + "_sp"), 1)

            pe.wait_ge(*signal("consts", 16))
            pe.wait_ge(*signal("vec_in", 16 * VEC_LOADS))
            nc.tensor.transpose(Q[4][:, 0:VEC0], vraw[0:VEC0, 0, :], cst[0:VEC0, C_ID:C_ID + VEC0])
            nc.tensor.transpose(Q[4][:, P:P + VEC1], vraw[0:VEC1, 1, :], cst[0:VEC1, C_ID:C_ID + VEC1])\
                .then_inc(S("vec_ps"), 1)
            pe.wait_ge(*signal("x_in", 16))

            def transpose_in(src, st):
                for j in range(4):
                    for c in range(2):
                        for b in range(TB):
                            o = (c * TB + b) * P
                            k = 2 * j + c
                            ins = nc.tensor.transpose(Q[j][:, o:o + P], src[:, b, k * P:(k + 1) * P], ident)
                    ins.then_inc(S(st), 1)

            transpose_in(xraw, "x_ps")
            pe.wait_ge(*signal("x_ok", 1))
            norm("n1")
            pe.wait_ge(*signal("n1_lo", 4))
            feed_forward("f1u", "f1d")

            norm("n2")
            pe.wait_ge(*signal("n2_lo", 4))
            two("wq", ah, al)
            s, n = SLAB0["wkv"], ACC0["wkv"]
            open_acc(n)
            product(s, 0, 8, n, ah, al)
            open_acc(n + 1)
            product(s + 1, 0, 8, n + 1, ah, al, tokens=True)
            two("wmqk", ah, al)
            two("wmv", ah, al, tokens=True)
            two("wmo", ah, al)
            two("wg", ah, al)

            pe.wait_ge(*signal("small_in", 16 * SMALL_LOADS))
            for b in range(TB):
                for k in range(DC):
                    ins = mm(Q[5][:, b * 16:(b + 1) * 16], xn[:, k, b * P:(b + 1) * P], wif[:, k, :],
                             start=k == 0 and b == 0, stop=k == DC - 1, skip_group_check=True)
            ins.then_inc(S("if_ps"), 1)
            pe.wait_ge(*signal("if_tok", 1))
            for g in range(2):
                for b in range(TB):
                    ins = nc.tensor.transpose(Q[4][0:8, g * T + b * P:g * T + (b + 1) * P],
                                              gtok[:, b, g * 8:(g + 1) * 8], ident)
            ins.then_inc(S("if_T"), 1)

            def a_scores(u, h):
                g, blk = u // 2, u % 2
                p0, hd = 64 * (h % 2), 4 * g + h
                return (aq[p0:p0 + 64, hd // 2, blk * P:(blk + 1) * P],
                        akd[p0:p0 + 64, g, 0:(blk + 1) * P])

            acc_freed(pe, ACC0["wkv"])
            acc_freed(pe, ACC0["wkv"] + 1)
            pe.wait_ge(*signal("if_use", 1))
            attention("at", [1, 2] * 4, a_scores, prob1, probT1,
                      lambda u, b, h: av[:, b, (u // 2) * 64:(u // 2 + 1) * 64],
                      [(0, 64, 0, [0, 2]), (64, P, 0, [1, 3])])

            pe.wait_ge(*signal("m_a", 1))
            for b in range(TB):
                ins = nc.tensor.transpose(Q[5][:, b * 8:(b + 1) * 8], ai[0:8, b * P:(b + 1) * P], cst[0:8, C_ID:C_ID + 8])
            ins.then_inc(S("m_acol"), 1)
            pe.wait_ge(*signal("m_M", 1))
            pe.wait_ge(*signal("at_pt", 8))
            spread("mm", Mx, 0, 8, Q[0:4], lambda j: None)
            for h in range(8):
                p0 = 64 * (h % 2)
                pe.wait_ge(*signal("m_qk", 1))
                if h < 4:
                    pe.wait_ge(*signal("m_D", 4 * (h + 1)))
                else:
                    pe.wait_ge(*signal("m_S", h - 3))
                bank = Q[h % 4]
                for b in range(TB):
                    ks = qk[p0:p0 + 64, 4 + h // 2, b * P:(b + 1) * P]
                    qs = qk[p0:p0 + 64, h // 2, b * P:T]
                    ins = mm(bank[:, b * 256:b * 256 + T - b * P], ks, qs, start=b == 0, stop=True, skip_group_check=True)
                ins.then_inc(S("m_qkT"), 1)
            for h in range(8):
                pe.wait_ge(*signal("m_S", max(h + 1, h // 2 + 5)))
                bank = Q[h // 2]
                for b in range(TB):
                    sc_ = wm[:, h, b * 256:b * 256 + T - b * P]
                    ins = mm(bank[:, (h % 2) * T + b * P:(h % 2) * T + T], mv[:, b, h * P:(h + 1) * P], sc_,
                             start=b == 0 and h % 2 == 0, stop=b == 1, skip_group_check=True)
                    if h == 0 and b == 0:
                        pe.wait_ge(*signal("m_acolr", 1))
                    den = mm(Q[5][0:8, b * P:T], hot(h), sc_, start=h == 0 and b == 0, stop=h == 7 and b == 1,
                             skip_group_check=True)
                den.then_inc(S("m_num"), 1)
            head_sums("m", sq, 8, Q[4], 0, True)
            spread("mf", rden, 0, 8, Q[0:4], lambda j: pe.wait_ge(*signal("m_r", 1)))

            s, n = SLAB0["proj"], ACC0["proj"]
            pe.wait_ge(*signal("at_lo", 4))
            pe.wait_ge(*signal("mo_lo", 4))
            with pe.Fori(0, 4) as i:
                open_acc(n, i)
                product(s, i, 8, n, ah, al)
                open_acc(n + 1, i)
                product(s + 1, i, 8, n + 1, bh, bl)
            pe.wait_ge(*signal("mg_lo", 4))
            two("wo", ch, cl)

            norm("n3")
            pe.wait_ge(*signal("n3_lo", 4))
            feed_forward("f2u", "f2d")
            norm("n4")
            pe.wait_ge(*signal("n4_out", 4))
            norm("n5")
            pe.wait_ge(*signal("n5_lo", 4))

            s, n = SLAB0["w2"], ACC0["w2"]
            for k in range(8):
                open_acc(n + k)
                product(s + k, 0, 8, n + k, ah, al, tokens=k in (2, 3))
            for k in range(DC):
                ins = mm(Q[0][0:16, 0:T], walr[:, k, :], xn[:, k, :], start=k == 0, stop=k == DC - 1)
            ins.then_inc(S("alr_ps"), 1)
            pe.wait_ge(*signal("alr", 1))
            for c in range(2):
                ins = mm(Q[1][:, c * T:(c + 1) * T], w2g[0:16, c * P:(c + 1) * P], alr[0:16, :],
                         start=c == 0, stop=True, skip_group_check=True)
            ins.then_inc(S("gl_z"), 1)
            pe.wait_ge(*signal("gl_ke", 1))
            for b in range(TB):
                for c in range(2):
                    ins = nc.tensor.transpose(Q[0][:, b * 256 + c * P:b * 256 + (c + 1) * P], ke[:, c, b * P:(b + 1) * P], ident)
            ins.then_inc(S("gl_keT"), 1)
            for c in range(2):
                for b in range(TB):
                    for e in range(2):
                        p0 = 64 * e
                        t = slice(b * P, (b + 1) * P)
                        ins = mm(Q[2 + e][:, c * 256 + b * P:c * 256 + (b + 1) * P], ki[p0:p0 + 64, c, t], qd[p0:p0 + 64, c, t],
                                 start=c == 0 and b == 0, stop=True, skip_group_check=True)
            ins.then_inc(S("gl_att"), 1)
            pe.wait_ge(*signal("gl_ketok", 1))
            pe.wait_ge(*signal("gl_zr", 1))
            for k in range(3):
                p0 = 64 * (k % 2)
                bank = (Q[4], Q[5], Q[1])[k]
                for c in range(2):
                    ins = mm(bank[:, c * 256:(c + 1) * 256], ketok[p0:p0 + 64, k // 2, c * P:(c + 1) * P],
                             gv[p0:p0 + 64, k // 2, c * 256:(c + 1) * 256], start=c == 0, stop=True, skip_group_check=True)
                ins.then_inc(S("gl_dS"), 1)
            pe.wait_ge(*signal("gl_am", 2))
            pe.wait_ge(*signal("gl_S", 3))
            for h in range(4):
                c, e = h // 2, h % 2
                p0 = 64 * e
                bank = Q[4 + e]
                for b in range(TB):
                    mm(bank[:, c * T + b * P:c * T + (b + 1) * P], gv[:, b, h * P:(h + 1) * P],
                       att[:, e, c * 256 + b * P:c * 256 + (b + 1) * P], start=c == 0 and b == 0, stop=False, skip_group_check=True)
                for k in range(1, 4):
                    ins = mm(bank[:, c * T + k * 64:c * T + (k + 1) * 64], stt_[p0:p0 + 64, k - 1, c, :],
                             qd[p0:p0 + 64, c, k * 64:(k + 1) * 64], start=False, stop=True, skip_group_check=True)
            ins.then_inc(S("gl_o"), 1)
            head_sums("gl", sq, 4, Q[0], 0, True)
            spread("gf", r8, 0, 4, Q[2:4], lambda j: pe.wait_ge(*signal("gl_r", 1)))

            pe.wait_ge(*signal("la_sq", 2))
            mm(Q[1][:, 0:T], ones, sq[:, 2, 0:T], start=True, stop=False, skip_group_check=True)
            mm(Q[1][:, 0:T], ones, sq[:, 2, T:512], start=False, stop=False, skip_group_check=True)
            mm(Q[1][:, T:512], ones, sq[:, 3, 0:T], start=False, stop=True, skip_group_check=True).then_inc(S("la_sum"), 1)
            pe.wait_ge(*signal("la_lo", 3))
            s, n = SLAB0["uq"], ACC0["uq"]
            lo_ready(pe, s, 0, 1)
            for j in range(4):
                open_acc(n + j)
                for c in range(2):
                    for k in range(2):
                        w = slice(k * 1024 + (2 * j + c) * P, k * 1024 + (2 * j + c + 1) * P)
                        dst = L[(n + j) % 2][:, c * T:(c + 1) * T]
                        mm(dst, wh[:, s % 2, w], cqh[:, k, :], start=k == 0 and c == 0, stop=False, skip_group_check=True)
                        mm(dst, wh[:, s % 2, w], cql[:, k, :], start=False, stop=False, skip_group_check=True)
                        ins = mm(dst, wl[:, s % 2, w], cqh[:, k, :], start=False, stop=k == 1, skip_group_check=True)
                ins.then_inc(S("uq_ps"), 1)
            s, n = SLAB0["ukv"], ACC0["ukv"]
            lo_ready(pe, s, 0, 1)
            for j in range(4):
                open_acc(n + j)
                for c in range(2):
                    w = slice((2 * j + c) * P, (2 * j + c + 1) * P)
                    dst = L[(n + j) % 2][:, c * T:(c + 1) * T]
                    mm(dst, wh[:, s % 2, w], cqh[:, 2, :], start=c == 0, stop=False, skip_group_check=True)
                    mm(dst, wh[:, s % 2, w], cql[:, 2, :], start=False, stop=False, skip_group_check=True)
                    ins = mm(dst, wl[:, s % 2, w], cqh[:, 2, :], start=False, stop=True, skip_group_check=True)
                ins.then_inc(S("uk_ps"), 1)
            vh = wh[:, s % 2, 0:1024].rearrange("p (h c) -> p h c", h=8)[:, :, 64:128]
            vl = wl[:, s % 2, 0:1024].rearrange("p (h c) -> p h c", h=8)[:, :, 64:128]
            for b in range(TB):
                open_acc(n + 4 + b)
                t = slice(b * P, (b + 1) * P)
                dst = L[(n + 4 + b) % 2][:, :]
                mm(dst, cqh[:, 2, t], vh, start=True, stop=False)
                mm(dst, cql[:, 2, t], vh, start=False, stop=False)
                ins = mm(dst, cqh[:, 2, t], vl, start=False, stop=True)
                ins.then_inc(S("w_used"), 2)
            head_sums("mq", sq, 8, Q[1], 0, True, rows=96)
            head_sums("mk", sq, 8, Q[1], T, False, rows=96)
            spread("mqf", r8, 0, 8, Q[2:4], lambda j: (pe.wait_ge(*signal("ml_r", 1)),
                                                       j >= 2 and pe.wait_ge(*signal("mqf_use", j - 1))))
            spread("mkf", r8, T, 8, Q[4:6], lambda j: j >= 2 and pe.wait_ge(*signal("mkf_use", j - 1)))
            pe.wait_ge(*signal("ml_k", 1))
            attention("ml", [1, 2] * 2,
                      lambda u, h: (qh[0:96, 4 * (u // 2) + h, (u % 2) * P:(u % 2 + 1) * P],
                                    kh[0:96, 4 * (u // 2) + h, 0:(u % 2 + 1) * P]),
                      prob2, probT2,
                      lambda u, b, h: vm[:, b, (4 * (u // 2) + h) * 64:(4 * (u // 2) + h + 1) * 64],
                      [(64 * (h % 2), 64 * (h % 2) + 64, (h // 2) * P, [h]) for h in range(4)])
            pe.wait_ge(*signal("go_lo", 2))
            pe.wait_ge(*signal("lo_lo", 2))
            two("wo2", oh, ol)

            pe.wait_ge(*signal("mem_in", 16))
            transpose_in(memraw, "mem_ps")
            pe.wait_ge(*signal("mem_ok", 1))
            norm("n6")
            pe.wait_ge(*signal("n6_lo", 4))
            two("xq", ah, al)
            norm("n7")
            pe.wait_ge(*signal("n7_lo", 4))
            two("xk", mh, ml)
            two("xv", mh, ml, tokens=True)
            head_sums("xx", sq, 8, Q[1], 0, True)
            spread("xf", rx8, 0, 8, Q[2:4], lambda j: (pe.wait_ge(*signal("xx_r", 1)),
                                                       j >= 2 and pe.wait_ge(*signal("xf_use", j - 1))))
            pe.wait_ge(*signal("xf_use", 4))
            attention("xa", [2, 2],
                      lambda u, h: (xq[:, h, u * P:(u + 1) * P], xq[:, 4 + h, :]),
                      prob3, probT3, lambda u, b, h: xv[:, b, h * P:(h + 1) * P],
                      [(0, P, h * P, [h]) for h in range(4)])
            pe.wait_ge(*signal("xo_lo", 2))
            two("xo", ah, al, nk=4)
            norm("n8")
            pe.wait_ge(*signal("n8_lo", 4))
            feed_forward("f3u", "f3d")
            for b in range(TB):
                for g in range(2):
                    if b == 0:
                        acc_freed(pe, ACC0["f3d"] + 2 * g)
                        acc_freed(pe, ACC0["f3d"] + 2 * g + 1)
                    for c in range(4):
                        ins = nc.tensor.transpose(Q[2 * b + g][:, c * P:(c + 1) * P],
                                                  xT[:, 4 * g + c, b * P:(b + 1) * P], ident)
                    ins.then_inc(S("res_ps"), 1)

        @block.scalar
        def _(act):
            A_ = nc.scalar.activation

            def norm(st, ready, src=xT, xh=ah, parts_=True):
                for j in range(4):
                    ready(act, j)
                    A_(sq[:, j, :], pairs(src, j), ACT.Square).then_inc(S(st + "_sq"), 1)
                act.wait_ge(*signal(st + "_sum", 1))
                A_(std[:, 0:T], Q[0][:, 0:T], ACT.Sqrt, bias=eps, scale=1.0 / D).then_inc(S(st + "_std"), 1)
                if parts_:
                    for j in range(4):
                        act.wait_ge(*signal(st + "_xn", j + 1))
                        A_(pairs(xh, j), pairs(xn, j), ACT.Copy).then_inc(S(st + "_hi"), 1)

            def from_accs(name):
                n = ACC0[name]
                return lambda e, j: acc_freed(e, n + j)

            def stage_loop(name, nslabs, evac):
                s, n = SLAB0[name], ACC0[name]

                def body(i, last):
                    for r in range(2):
                        if last and r == 1:
                            split_hi(act, s + 2 * i + 2)
                        else:
                            split_hi(act, s + r + 1, i)
                        if evac is not None:
                            slab_used(act, s + r, i)
                            evac(i, r)
                looped(act, nslabs // 2, body)

            def feed_forward(up, down, conv=False):
                s, n = SLAB0[up], ACC0[up]

                def body(i, last):
                    split_hi(act, s + 1, i)
                    slab_used(act, s, i)
                    if conv:
                        A_(gpad[:, :, 2:T + 2], L[n % 2][:, :].rearrange("p (c t) -> p c t", c=2), ACT.Copy)\
                            .then_inc(free_sem(n), 1)
                    else:
                        A_(sil[:, :], L[n % 2][:, :], ACT.Silu).then_inc(free_sem(n), 1)
                    if last:
                        split_hi(act, s + 2 * i + 2)
                    else:
                        split_hi(act, s + 2, i)
                    if conv:
                        act.wait_ge(*signal(up + "_cv", 6 * i + 6))
                        A_(sil[:, :], gcv[:, :], ACT.Silu).then_inc(S(up + "_si"), 1)
                    acc_freed(act, n + 1, i)
                    A_(rpair(hh, i), hid[:, :], ACT.Copy).then_inc(S(up + "_hh"), 1)
                looped(act, FP, body)
                s = SLAB0[down]
                for q in range(4):
                    split_hi(act, s + 2 * q + 1)
                    split_hi(act, s + 2 * q + 2)

            def attention(st, units, prob, probT, sinks=False):
                def exps(u, blocks):
                    for h in range(4):
                        act.wait_ge(*signal(st + "_mx", 4 * u + h + 1))
                        w = blocks * P
                        A_(prob[:, u % 2, h, 0:w], prob[:, u % 2, h, 0:w], ACT.Exp, bias=rmx[:, u % 2, h:h + 1],
                           scale=-1.0, accum_out=rsm[:, u % 2, h:h + 1]).then_inc(S(st + "_ex"), 1)
                    if sinks:
                        act.wait_ge(*signal(st + "_sk", u + 1))
                        A_(rs2[:, u % 2, :], rs2[:, u % 2, :], ACT.Exp).then_inc(S(st + "_se"), 1)

                exps(0, units[0])
                for u, blocks in enumerate(units):
                    if u + 1 < len(units):
                        exps(u + 1, units[u + 1])
                    act.wait_ge(*signal(st + "_tp", u + 1))
                    if u >= 1:
                        act.wait_ge(*signal(st + "_pv", u))
                    for b in range(blocks):
                        ins = A_(probT[:, b, :], Q[2 + b][:, :], ACT.Copy)
                    ins.then_inc(S(st + "_pt"), 1)

            def x_ready(e, j):
                e.wait_ge(*signal("x_ok", j + 1))

            rows = [(V_FFN1, "ffn1_norm"), (V_MIX, "mix_norm"), (V_FFN2, "ffn2_norm"),
                    (V_MIX2, "norm_mix_2"), (V_XA, "norm_xa_2"), (V_MEM, "norm_mem_2"), (V_FFN3, "norm_ffn_2"),
                    (V_GATEB, "gla_gate_b_2"), (V_GLA, "gla_out_norm_2"), (V_QA, "mla_q_a_norm_2"),
                    (V_KVA, "mla_kv_a_norm_2"), (V_XQ, "xa_q_norm_2"), (V_XK, "xa_k_norm_2")]
            todo = []
            for v, name in rows:
                n = A[name].shape[1] // P
                todo.append((vraw[v:v + n, 0, :], A[name][0].rearrange("(c p) -> c p", p=P)))
            todo.append((vraw[V_FINAL:V_FINAL + 8, 0, :], A["final_norm"].rearrange("(c p) -> c p", p=P)))
            todo.append((vraw[V_HEAD:V_HEAD + 8, 0, :], A["mlstm_head_norm"][0]))
            b = A["b_in"][0]
            for v, lo, n in ((V_BQ, I_AQ, 10), (V_BMQK, I_MQK, 8), (V_BMO, I_MO, 8), (V_BG, I_G, 16)):
                todo.append((vraw[v:v + n, 0, :], b[lo:lo + n * P].rearrange("(c p) -> c p", p=P)))
            for v, name in ((V_MLAQ, "mla_q_norm_2"), (V_MLAK, "mla_k_norm_2")):
                g = A[name]
                todo += [(vraw[v:v + 1, 0, 0:96], g), (vraw[v:v + 1, 0, 96:112], g[:, 80:96]),
                         (vraw[v:v + 1, 0, 112:128], g[:, 64:80])]
            todo.append((vraw[0:3 * FC, 1, :], A["ffn_conv_w_2"][0].rearrange("j (c p) -> (j c) p", p=P)))
            todo.append((vraw[3 * FC:4 * FC, 1, :], A["ffn_conv_b_2"][0].rearrange("(c p) -> c p", p=P)))
            todo.append((vraw[4 * FC:4 * FC + 32, 1, :], A["mlstm_conv"][0].rearrange("j (c p) -> (j c) p", p=P)))
            for d, s in todo:
                act.dma_start(d, s).then_inc(S("vec_in"), 16)
            assert len(todo) == VEC_LOADS

            win = A["w_in"][0].rearrange("(k p) c -> p k c", p=P)
            win2 = A["w_in_2"][0].rearrange("(k p) c -> p k c", p=P)

            def small(dst, src):
                act.dma_start(dst, src).then_inc(S("small_in"), 16)

            small(bav[:, :], A["b_in"][:, I_AV:I_AV + 256].broadcast_to([P, 256]))
            small(bmv[:, :], A["b_in"][:, I_MV:I_MV + 1024].broadcast_to([P, 1024]))
            small(nsink[:, 0:16], A["attn_sinks"].broadcast_to([P, 16]))
            small(posi[:, :], A["positions_2"].broadcast_to([P, T]))
            small(wif[:, :, :], win[:, :, I_MI:I_MI + 16])
            small(walr[:, :, :], win2[:, :, J_ALR:J_ALR + 16])
            small(w2g[:, :], A["gla_gate_w2_2"][0])
            small(bif[:, 0:1], A["b_in"][0, I_MI:I_MI + 8].rearrange("(p a) -> p a", a=1))
            small(bif[:, 1:2], A["b_in"][0, I_MI + 8:I_MI + 16].rearrange("(p a) -> p a", a=1))

            act.wait_ge(*signal("consts", 16))
            split_hi(act, 0)
            norm("n1", x_ready)
            act.wait_ge(*signal("angles", 1))
            A_(rope_c[64:P, :], rope_c[64:P, :], ACT.Sin)
            A_(rope_s[64:P, :], rope_s[64:P, :], ACT.Sin).then_inc(S("sines"), 1)
            feed_forward("f1u", "f1d")
            norm("n2", from_accs("f1d"))
            stage_loop("wq", 4, None)
            stage_loop("wkv", 2, None)
            stage_loop("wmqk", 4, None)
            stage_loop("wmv", 4, None)

            def sigmoids(dst, v, n):
                def evac(i, r):
                    for m in range(2):
                        c = i * 4 + r * 2 + m
                        ins = A_(dst[:, :, :].rearrange("p c t -> p (c t)")[:, bass.ds(c * T, T)],
                                 L[(n + r) % 2][:, m * T:(m + 1) * T], ACT.Sigmoid, bias=vec[:, bass.ds(c + v, 1)])
                    ins.then_inc(free_sem(n + r), 1)
                return evac

            stage_loop("wmo", 4, sigmoids(sigo, V_BMO, ACC0["wmo"]))
            stage_loop("wg", 8, sigmoids(gate, V_BG, ACC0["wg"]))

            act.wait_ge(*signal("if_T", 1))
            act.wait_ge(*signal("if_b", 1))
            A_(ti[:, 0:T], Q[4][0:8, 0:T], ACT.Tanh, bias=bif[:, 2:3], scale=1.0 / 15)
            A_(ti[:, T:512], Q[4][0:8, T:512], ACT.Tanh, bias=bif[:, 3:4], scale=1.0 / 15).then_inc(S("if_use"), 1)
            act.wait_ge(*signal("if_use", 1))
            A_(lse[:, :], ti[:, T:512], ACT.Exp, scale=-15.0).then_inc(S("m_e"), 1)
            act.wait_ge(*signal("m_e", 1))
            A_(lse[:, :], lse[:, :], ACT.Ln, bias=1.0).then_inc(S("m_e"), 1)
            attention("at", [1, 2] * 4, prob1, probT1, sinks=True)
            for j in range(4):
                act.wait_ge(*signal("at_yo", 2 * j + 2))
                A_(pairs(ah, j), pairs(aq, j), ACT.Copy).then_inc(S("at_hi"), 1)
            act.wait_ge(*signal("conv", 32))
            for j in range(4):
                ins = A_(pairs(qk, j), pairs(qk, j), ACT.Silu)
            ins.then_inc(S("m_qk"), 1)
            act.wait_ge(*signal("m_gm", 1))
            A_(en[:, :], gm[:, :], ACT.Exp).then_inc(S("m_en"), 1)
            for j in range(4):
                act.wait_ge(*signal("m_D", 4 * j + 4))
                v = wm[:, 2 * j:2 * j + 2, :]
                A_(v, v, ACT.Exp, scale=-1.0).then_inc(S("m_w"), 1)
            for j in range(4):
                act.wait_ge(*signal("m_nu", j + 1))
                A_(sq[:, j, :], pairs(xn, j), ACT.Square).then_inc(S("m_hs"), 1)
            act.wait_ge(*signal("m_v", 1))
            A_(gm[:, :], gm[:, :], ACT.Sqrt, bias=eps[0:8, :]).then_inc(S("m_sd"), 1)
            for j in range(4):
                act.wait_ge(*signal("mo_y", j + 1))
                A_(pairs(bh, j), pairs(xn, j), ACT.Copy).then_inc(S("mo_hi"), 1)

            s = SLAB0["proj"]

            def merge(i, last):
                split_hi(act, s + 1, i)
                if last:
                    split_hi(act, s + 2 * i + 2)
                else:
                    split_hi(act, s + 2, i)
                act.wait_ge(*signal("mg", i + 1))
                A_(rpair(ch, i), mgs[:, :], ACT.Copy).then_inc(S("mg_hi"), 1)
            looped(act, 4, merge)
            stage_loop("wo", 4, None)
            norm("n3", from_accs("wo"))
            feed_forward("f2u", "f2d")
            norm("n4", from_accs("f2d"), parts_=False)
            norm("n5", lambda e, j: e.wait_ge(*signal("n4_out", j + 1)))

            s, n = SLAB0["w2"], ACC0["w2"]
            for k in range(8):
                split_hi(act, s + k + 1)
                if k in (4, 5):
                    slab_used(act, s + k)
                    A_(pairs(sog, k - 4), L[(n + k) % 2][:, :], ACT.Silu).then_inc(free_sem(n + k), 1)
            act.wait_ge(*signal("gl_zr", 1))
            A_(lg[:, :], zg[:, :], ACT.Abs).then_inc(S("gl_l"), 1)
            act.wait_ge(*signal("gl_l", 1))
            A_(lg[:, :], lg[:, :], ACT.Exp, scale=-1.0).then_inc(S("gl_l"), 1)
            act.wait_ge(*signal("gl_l", 2))
            A_(lg[:, :], lg[:, :], ACT.Ln, bias=1.0).then_inc(S("gl_l"), 1)
            act.wait_ge(*signal("gl_cum", 2))
            A_(eg[:, 0, :], cum[:, :], ACT.Exp, scale=1.0 / 16).then_inc(S("gl_e"), 1)
            A_(eg[:, 1, :], cum[:, :], ACT.Exp, scale=-1.0 / 16).then_inc(S("gl_e"), 1)
            ends = cum[:, :].rearrange("p (n c) -> p n c", n=8)[:, :, 63]
            A_(dec[:, :], ends, ACT.Exp, scale=1.0 / 16)
            act.wait_ge(*signal("gl_d", 1))
            A_(eg[:, 2, :], zg[:, :], ACT.Exp, scale=-1.0 / 16).then_inc(S("gl_e"), 1)
            act.wait_ge(*signal("gl_keT", 1))
            A_(ketok[:, :, :].rearrange("p b c -> p (b c)"), Q[0][:, :], ACT.Copy).then_inc(S("gl_ketok"), 1)
            for j in range(2):
                act.wait_ge(*signal("gl_or", 1))
                A_(sq[:, j, :], pairs(xn, j), ACT.Square).then_inc(S("gl_hs"), 1)
            acc_freed(act, n + 6)
            A_(sq[:, 2, :], pairs(cq, 0), ACT.Square).then_inc(S("la_sq"), 1)
            acc_freed(act, n + 7)
            A_(sq[:, 3, 0:T], ckv[:, :], ACT.Square).then_inc(S("la_sq"), 1)
            act.wait_ge(*signal("gl_ss", 1))
            A_(st8[:, 0:T], Q[0][0:8, 0:T], ACT.Sqrt, bias=eps[0:8, :], scale=1.0 / P).then_inc(S("gl_sd"), 1)
            act.wait_ge(*signal("la_sum", 1))
            A_(std[:, 0:T], Q[1][:, 0:T], ACT.Sqrt, bias=eps, scale=1.0 / 256)
            A_(std[:, T:512], Q[1][:, T:512], ACT.Sqrt, bias=eps, scale=1.0 / P).then_inc(S("la_sd"), 1)
            for j in range(2):
                act.wait_ge(*signal("go_y", j + 1))
                A_(pairs(oh, j), pairs(xn, j), ACT.Copy).then_inc(S("go_hi"), 1)
            act.wait_ge(*signal("la_n", 3))
            A_(cqh[:, 0:2, :], cq[:, :, :], ACT.Copy).then_inc(S("la_hi"), 1)
            A_(cqh[:, 2, :], ckv[:, :], ACT.Copy).then_inc(S("la_hi"), 1)
            split_hi(act, SLAB0["ukv"])
            for part, dst in (("mq", qh), ("mk", kh)):
                n = ACC0["uq"] if part == "mq" else ACC0["ukv"]
                if part == "mk":
                    act.wait_ge(*signal("mq_ss", 1))
                for j in range(4):
                    acc_freed(act, n + j)
                    if part == "mk":
                        act.wait_ge(*signal("kpe_in", 1))
                    A_(sq[0:96, j, :], dst[0:96, 2 * j:2 * j + 2, :].rearrange("p c t -> p (c t)"), ACT.Square)\
                        .then_inc(S(part + "_hs"), 1)
            split_hi(act, SLAB0["wo2"])
            act.wait_ge(*signal("mk_ss", 1))
            A_(st8[:, :], Q[1][0:8, :], ACT.Sqrt, bias=eps[0:8, :], scale=1.0 / 96).then_inc(S("ml_sd"), 1)
            attention("ml", [1, 2] * 2, prob2, probT2)
            for j in range(2):
                act.wait_ge(*signal("ml_yo", 2 * j + 2))
                A_(pairs(oh, 2 + j), pairs(xn, 2 + j), ACT.Copy).then_inc(S("lo_hi"), 1)
            stage_loop("wo2", 4, None)

            norm("n6", from_accs("wo2"))
            stage_loop("xq", 2, None)
            norm("n7", lambda e, j: e.wait_ge(*signal("mem_ok", j + 1)), src=mT, xh=mh)
            stage_loop("xk", 2, None)
            stage_loop("xv", 2, None)
            for j in range(4):
                acc_freed(act, ACC0["xq"] + j)
                A_(sq[:, j, :], pairs(xq, j), ACT.Square).then_inc(S("xx_hs"), 1)
            act.wait_ge(*signal("xx_ss", 1))
            A_(sx8[:, 0:T], Q[1][0:8, 0:T], ACT.Sqrt, bias=eps[0:8, :], scale=1.0 / P).then_inc(S("xx_sd"), 1)
            attention("xa", [2, 2], prob3, probT3)
            for j in range(2):
                act.wait_ge(*signal("xa_yo", 2))
                A_(pairs(ah, j), pairs(xn, j), ACT.Copy).then_inc(S("xo_hi"), 1)
            stage_loop("xo", 4, None)
            norm("n8", from_accs("xo"))
            feed_forward("f3u", "f3d", conv=True)
            for k in range(2):
                act.wait_ge(*signal("res_ps", 2 * k + 1))
                A_(res[:, k, 0:512], Q[2 * k][:, :], ACT.Copy).then_inc(S("resa"), 1)

        @block.vector
        def _(dve):
            V = nc.vector
            steps = [0]

            def link(ins, n=1):
                ins.then_inc(S("dve_step"), 1)
                steps[0] += 1
                dve.wait_ge(*signal("dve_step", steps[0]))

            def norm(st, g, src=xT, dst=xn, xh=ah, xl=al, parts_=True):
                dve.wait_ge(*signal(st + "_std", 1))
                link(V.reciprocal(rstd[:, 0:T], std[:, 0:T]))
                for j in range(4):
                    for c in (2 * j, 2 * j + 1):
                        ins = V.scalar_tensor_tensor(dst[:, c, :], src[:, c, :], col(g + c), rstd[:, 0:T], MUL, MUL)
                    ins.then_inc(S(st + ("_xn" if parts_ else "_out")), 1)
                if parts_:
                    lows(st, xn, xh, xl, 4)

            def lows(st, src, xh, xl, n, j0=0):
                for j in range(n):
                    dve.wait_ge(*signal(st + "_hi", j + 1))
                    V.tensor_tensor(pairs(xl, j0 + j), pairs(src, j0 + j), f(pairs(xh, j0 + j)), SUB)\
                        .then_inc(S(st + "_lo"), 1)

            def stage_loop(name, nslabs, evac):
                s, n = SLAB0[name], ACC0[name]

                def body(i, last):
                    for r in range(2):
                        if last and r == 1:
                            split_lo(dve, s + 2 * i + 2)
                        else:
                            split_lo(dve, s + r + 1, i)
                        evac(i, r)
                looped(dve, nslabs // 2, body)

            def feed_forward(up, down, conv=False):
                s, n = SLAB0[up], ACC0[up]

                def body(i, last):
                    split_lo(dve, s + 1, i)
                    if conv:
                        acc_freed(dve, n, i)
                        for j in range(3):
                            for m in range(2):
                                w = vec[:, bass.ds(V_FCW + j * FC + m + i * 2, 1)]
                                o, x = gcv[:, m * T:(m + 1) * T], gpad[:, m, j:j + T]
                                if j == 0:
                                    ins = V.tensor_scalar(o, x, w, vec[:, bass.ds(V_FCB + m + i * 2, 1)], MUL, ADD)
                                else:
                                    dve.wait_ge(*signal(up + "_cv", 6 * i + 2 * j + m - 1))
                                    ins = V.scalar_tensor_tensor(o, x, w, o, MUL, ADD)
                                ins.then_inc(S(up + "_cv"), 1)
                    if last:
                        split_lo(dve, s + 2 * i + 2)
                    else:
                        split_lo(dve, s + 2, i)
                    slab_used(dve, s + 1, i)
                    if conv:
                        dve.wait_ge(*signal(up + "_si", i + 1))
                    else:
                        acc_freed(dve, n, i)
                    V.tensor_tensor(hid[:, :], L[(n + 1) % 2][:, :], sil[:, :], MUL).then_inc(free_sem(n + 1), 1)
                    dve.wait_ge(*signal(up + "_hh", i + 1))
                    V.tensor_tensor(rpair(hl, i), hid[:, :], f(rpair(hh, i)), SUB).then_inc(S(up + "_hl"), 1)
                looped(dve, FP, body)
                s, n = SLAB0[down], ACC0[down]
                for q in range(4):
                    split_lo(dve, s + 2 * q + 1)
                    split_lo(dve, s + 2 * q + 2)
                    slab_used(dve, s + 2 * q + 1)
                    V.scalar_tensor_tensor(pairs(xT, q), L[(n + q) % 2][:, :], 1.0 if conv else 0.5, pairs(xT, q),
                                           MUL, ADD).then_inc(free_sem(n + q), 1)

            def add_to_x(name, s, n):
                def evac(i, r):
                    slab_used(dve, s + r, i)
                    V.tensor_tensor(rpair(xT, i * 2 + r), L[(n + r) % 2][:, :], rpair(xT, i * 2 + r), ADD)\
                        .then_inc(free_sem(n + r), 1)
                return evac

            def attention(st, units, prob, scale, mask, yout, sink=None):
                def maxima(u, blocks):
                    dve.wait_ge(*signal(st + "_sc", u + 1))
                    if u >= 2:
                        dve.wait_ge(*signal(st + "_tp", u - 1))
                    w = blocks * P
                    for h in range(4):
                        V.tensor_tensor_reduce(out=prob[:, u % 2, h, 0:w], in0=Q[h % 2][:, (h // 2) * 256:(h // 2) * 256 + w],
                                               in1=mask(blocks), scale=-scale, scalar=sink(u, h) if sink else 3.0e38,
                                               op0=ADD, op1=MIN, accum_out=rmx[:, u % 2, h:h + 1]).then_inc(S(st + "_mx"), 1)
                    if sink:
                        dve.wait_ge(*signal(st + "_mx", 4 * u + 4))
                        g = u // 2
                        V.tensor_tensor(rs2[:, u % 2, :], rmx[:, u % 2, :], nsink[:, 4 * g:4 * g + 4], SUB)\
                            .then_inc(S(st + "_sk"), 1)

                def divide(u, blocks):
                    w = blocks * P
                    dve.wait_ge(*signal(st + "_ex", 4 * u + 4))
                    if sink:
                        dve.wait_ge(*signal(st + "_se", u + 1))
                        link(V.tensor_tensor(rsm[:, u % 2, :], rsm[:, u % 2, :], rs2[:, u % 2, :], ADD))
                    link(V.reciprocal(rin[:, u % 2, :], rsm[:, u % 2, :]))
                    for h in range(4):
                        V.tensor_scalar(prob[:, u % 2, h, 0:w], prob[:, u % 2, h, 0:w], rin[:, u % 2, h:h + 1], None, MUL)\
                            .then_inc(S(st + "_pn"), 1)

                def leave(u):
                    dve.wait_ge(*signal(st + "_pv", u + 1))
                    yout(u, Q[4 + u % 2]).then_inc(S(st + "_yo"), 1)

                maxima(0, units[0])
                for u, blocks in enumerate(units):
                    if u + 1 < len(units):
                        maxima(u + 1, units[u + 1])
                    divide(u, blocks)
                    if u >= 1:
                        leave(u - 1)
                leave(len(units) - 1)

            dve.wait_ge(*signal("vec_ps", 1))
            V.tensor_copy(vec[:, 0:VEC0], Q[4][:, 0:VEC0])
            V.tensor_copy(vec[:, P:P + VEC1], Q[4][:, P:P + VEC1]).then_inc(S("vec_ok"), 1)
            for j in range(4):
                dve.wait_ge(*signal("x_ps", j + 1))
                V.tensor_copy(pairs(xT, j), Q[j][:, :]).then_inc(S("x_ok"), 1)
            split_lo(dve, 0)
            dve.wait_ge(*signal("vec_ok", 1))
            dve.wait_ge(*signal("x_ok", 4))
            norm("n1", V_FFN1)

            dve.wait_ge(*signal("small_in", 16 * SMALL_LOADS))
            V.tensor_scalar(bif[:, 2:4], bif[:, 0:2], 1.0 / 15, None, MUL).then_inc(S("if_b"), 1)
            V.tensor_scalar(nsink[:, 0:16], nsink[:, 0:16], -1.0, None, MUL)
            R = slice(64, P)
            TWO_PI = 2 * np.pi
            c1 = 6.28125
            c2 = float(np.float32(np.round((TWO_PI - c1) * 2 ** 21) / 2 ** 21))
            c3 = float(np.float32(TWO_PI - c1 - c2))
            MAGIC = 12582912.0
            link(V.tensor_copy(ang[R, :], posi[R, :]))
            link(V.tensor_scalar(ang[R, :], ang[R, :], cst[R, C_INV:C_INV + 1], None, MUL))
            link(V.tensor_scalar(turn[R, :], ang[R, :], float(1 / TWO_PI), MAGIC, MUL, ADD))
            link(V.tensor_scalar(turn[R, :], turn[R, :], MAGIC, None, SUB))
            for c in (c1, c2, c3):
                link(V.scalar_tensor_tensor(ang[R, :], turn[R, :], -c, ang[R, :], MUL, ADD))
            link(V.tensor_scalar(quarter[R, :], ang[R, :], float(np.pi / 2), None, ADD))
            link(V.tensor_scalar(tmpr[R, :], quarter[R, :], float(np.pi), TWO_PI, ALU.is_gt, MUL))
            link(V.tensor_tensor(quarter[R, :], quarter[R, :], tmpr[R, :], SUB))
            BOUND = 3.1415925
            V.tensor_scalar(rope_c[R, :], quarter[R, :], BOUND, -BOUND, MIN, MAX)
            V.tensor_scalar(rope_s[R, :], ang[R, :], BOUND, -BOUND, MIN, MAX).then_inc(S("angles"), 1)

            feed_forward("f1u", "f1d")
            norm("n2", V_MIX)

            def with_bias(dst_of, v, name):
                s, n = SLAB0[name], ACC0[name]

                def evac(i, r):
                    slab_used(dve, s + r, i)
                    for m in range(2):
                        c = i * 4 + r * 2 + m
                        ins = V.tensor_scalar(dst_of(c), L[(n + r) % 2][:, m * T:(m + 1) * T],
                                              vec[:, bass.ds(c + v, 1)], None, ADD)
                    ins.then_inc(free_sem(n + r), 1)
                return evac

            stage_loop("wq", 4, with_bias(lambda c: aq[:, :, :].rearrange("p c t -> p (c t)")[:, bass.ds(c * T, T)], V_BQ, "wq"))
            s, n = SLAB0["wkv"], ACC0["wkv"]
            split_lo(dve, s + 1)
            slab_used(dve, s)
            for c in range(2):
                for e in range(2):
                    for to in range(2):
                        ins = V.tensor_scalar(akd[64 * to:64 * to + 64, 2 * c + e, :],
                                              L[n % 2][64 * e:64 * e + 64, c * T:(c + 1) * T],
                                              col(V_BK + c, 64 * e, 64 * e + 64), None, ADD)
            ins.then_inc(free_sem(n), 1)
            split_lo(dve, s + 2)
            slab_used(dve, s + 1)
            V.tensor_tensor(av[:, :, :], L[(n + 1) % 2][:, :].rearrange("p (b c) -> p b c", b=TB),
                            bav[:, :].rearrange("p (a c) -> p a c", a=1).broadcast_to([P, TB, 256]), ADD).then_inc(free_sem(n + 1), 1)
            padf = pad[:, :, :].rearrange("p c t -> p (c t)")
            stage_loop("wmqk", 4, with_bias(lambda c: padf[:, bass.ds(c * (T + 3) + 3, T)], V_BMQK, "wmqk"))
            s_mv, n_mv = SLAB0["wmv"], ACC0["wmv"]

            def values_out(i, r):
                slab_used(dve, s_mv + r, i)
                for b in range(TB):
                    ins = V.tensor_tensor(mv[:, b, bass.ds(i * 512 + r * 256, 256)], L[(n_mv + r) % 2][:, b * 256:(b + 1) * 256],
                                          bmv[:, bass.ds(i * 512 + r * 256, 256)], ADD)
                ins.then_inc(free_sem(n_mv + r), 1)
            stage_loop("wmv", 4, values_out)
            stage_loop("wmo", 4, lambda i, r: None)

            qkf = qk[:, :, :].rearrange("p c t -> p (c t)")
            dve.wait_ge(*signal("pad0", 1))
            acc_freed(dve, ACC0["wmqk"] + 2)
            acc_freed(dve, ACC0["wmqk"] + 3)

            def conv(i, r):
                for j in range(4):
                    o = qkf[:, bass.ds((i * 2 + r) * T, T)]
                    x = padf[:, bass.ds((i * 2 + r) * (T + 3) + j, T)]
                    w = vec[:, bass.ds(V_MCONV + j * 8 + r + i * 2, 1)]
                    if j == 0:
                        ins = V.tensor_scalar(o, x, w, None, MUL)
                    else:
                        dve.wait_ge(*signal("conv", 8 * i + 4 * r + j))
                        ins = V.scalar_tensor_tensor(o, x, w, o, MUL, ADD)
                    ins.then_inc(S("conv"), 1)
            stage_loop("wg", 8, conv)

            dve.wait_ge(*signal("if_ps", 1))
            V.tensor_copy(gtok[:, :, :].rearrange("p b c -> p (b c)"), Q[5][:, 0:32]).then_inc(S("if_tok"), 1)

            def y_first(u, bank):
                g, blk = u // 2, u % 2
                return V.tensor_copy(aq[:, 2 * g:2 * g + 2, blk * P:(blk + 1) * P],
                                     bank[:, 0:256].rearrange("p (c q) -> p c q", c=2))

            attention("at", [1, 2] * 4, prob1, 0.125,
                      lambda b: cst[:, C_OWN:C_OWN + P] if b == 1 else cst[:, C_PREV:C_PREV + 256], y_first,
                      sink=lambda u, h: nsink[:, 4 * (u // 2) + h:4 * (u // 2) + h + 1])
            dve.wait_ge(*signal("at_yo", 8))
            lows("at", aq, ah, al, 4)

            dve.wait_ge(*signal("m_e", 2))
            link(V.tensor_tensor_scan(Gc[:, :], cst[0:8, C_ONE:C_ONE + 1].broadcast_to([8, T]), lse[:, :], 0.0, MUL, ADD))
            V.scalar_tensor_tensor(ai[:, :], ti[:, 0:T], 15.0, Gc[:, :], MUL, ADD).then_inc(S("m_a"), 1)
            dve.wait_ge(*signal("m_a", 1))
            V.tensor_tensor_scan(Mx[:, :], cst[0:8, C_ONE:C_ONE + 1].broadcast_to([8, T]), ai[:, :], 0.0, MUL, MAX)\
                .then_inc(S("m_M"), 1)
            dve.wait_ge(*signal("m_M", 1))
            V.tensor_tensor(gm[:, :], Gc[:, :], Mx[:, :], SUB).then_inc(S("m_gm"), 1)
            dve.wait_ge(*signal("m_acol", 1))
            V.tensor_copy(acol[:, :, :].rearrange("p b h -> p (b h)"), Q[5][:, 0:16]).then_inc(S("m_acolr"), 1)
            dve.wait_ge(*signal("m_acolr", 1))
            for h in range(8):
                dve.wait_ge(*signal("mm_sp", h // 2 + 1))
                for b in range(TB):
                    a = acol[:, b, h:h + 1]
                    V.tensor_scalar(wm[:, h, b * 256:b * 256 + T - b * P], Q[h // 2][:, (h % 2) * T + b * P:(h % 2) * T + T],
                                    a, a, MAX, SUB).then_inc(S("m_D"), 1)
            for h in range(8):
                dve.wait_ge(*signal("m_qkT", h + 1))
                dve.wait_ge(*signal("m_mask", h // 2 + 1))
                V.scalar_tensor_tensor(wm[:, h, :], Q[h % 4][:, 0:384], 0.125, wm[:, h, :], MUL, MUL)\
                    .then_inc(S("m_S"), 1)
            for j in range(4):
                dve.wait_ge(*signal("m_num", 2 * j + 2))
                V.tensor_copy(pairs(xn, j), Q[j][:, :]).then_inc(S("m_nu"), 1)
            dve.wait_ge(*signal("m_num", 8))
            dve.wait_ge(*signal("m_en", 1))
            link(V.scalar_tensor_tensor(rden[:, :], Q[5][0:8, 0:T], -1.0, en[:, :], MUL, MAX))
            link(V.tensor_tensor(rden[:, :], rden[:, :], Q[5][0:8, 0:T], MAX))
            link(V.reciprocal(rden[:, :], rden[:, :]))
            link(V.tensor_tensor(gm[:, :], rden[:, :], rden[:, :], MUL))
            dve.wait_ge(*signal("m_ss", 1))
            V.scalar_tensor_tensor(gm[:, :], Q[4][0:8, 0:T], 1.0 / P, gm[:, :], MUL, MUL).then_inc(S("m_v"), 1)
            dve.wait_ge(*signal("m_sd", 1))
            link(V.reciprocal(en[:, :], gm[:, :]))
            V.tensor_tensor(rden[:, :], rden[:, :], en[:, :], MUL).then_inc(S("m_r"), 1)
            for j in range(4):
                dve.wait_ge(*signal("mf_sp", j + 1))
                link(V.tensor_tensor(pairs(xn, j), Q[j][:, :], pairs(xn, j), MUL))
                for h in (2 * j, 2 * j + 1):
                    ins = V.scalar_tensor_tensor(xn[:, h, :], xn[:, h, :], col(V_HEAD + h), sigo[:, h, :], MUL, MUL)
                ins.then_inc(S("mo_y"), 1)
            lows("mo", xn, bh, bl, 4)

            s_p, n_p = SLAB0["proj"], ACC0["proj"]

            def merge(i, last):
                split_lo(dve, s_p + 1, i)
                slab_used(dve, s_p, i)
                V.tensor_tensor(mga[:, :], L[n_p % 2][:, :], rpair(gate, i), MUL).then_inc(free_sem(n_p), 1)
                if last:
                    split_lo(dve, s_p + 2 * i + 2)
                else:
                    split_lo(dve, s_p + 2, i)
                slab_used(dve, s_p + 1, i)
                V.tensor_tensor(mgb[:, :], L[(n_p + 1) % 2][:, :], rpair(gate, i + 4), MUL).then_inc(free_sem(n_p + 1), 1)
                acc_freed(dve, n_p, i)
                acc_freed(dve, n_p + 1, i)
                V.tensor_tensor(mgs[:, :], mga[:, :], mgb[:, :], ADD).then_inc(S("mg"), 1)
                dve.wait_ge(*signal("mg_hi", i + 1))
                V.tensor_tensor(rpair(cl, i), mgs[:, :], f(rpair(ch, i)), SUB).then_inc(S("mg_lo"), 1)
            looped(dve, 4, merge)
            stage_loop("wo", 4, add_to_x("wo", SLAB0["wo"], ACC0["wo"]))
            norm("n3", V_FFN2)
            feed_forward("f2u", "f2d")
            norm("n4", V_FINAL, dst=xT, parts_=False)
            norm("n5", V_MIX2)

            s, n = SLAB0["w2"], ACC0["w2"]

            def acc(k):
                return L[(n + k) % 2]
            for k in range(8):
                split_lo(dve, s + k + 1)
                if k in (4, 5):
                    continue
                slab_used(dve, s + k)
                if k == 0:
                    ins = V.tensor_scalar(pairs(gq, 0), acc(k)[:, :], 0.125, None, MUL)
                elif k == 1:
                    ins = V.tensor_copy(pairs(gk, 0), acc(k)[:, :])
                elif k in (2, 3):
                    ins = V.tensor_copy(gv[:, :, (k - 2) * 256:(k - 1) * 256], acc(k)[:, :].rearrange("p (b c) -> p b c", b=TB))
                elif k == 6:
                    ins = V.tensor_copy(pairs(cq, 0), acc(k)[:, :])
                else:
                    V.tensor_copy(kpe[64:P, :], acc(k)[64:P, T:512])
                    ins = V.tensor_copy(ckv[:, :], acc(k)[:, 0:T])
                ins.then_inc(free_sem(n + k), 1)
            dve.wait_ge(*signal("alr_ps", 1))
            V.tensor_copy(alr[0:16, :], Q[0][0:16, 0:T]).then_inc(S("alr"), 1)
            dve.wait_ge(*signal("gl_z", 1))
            for c in range(2):
                ins = V.tensor_scalar(zg[:, c * T:(c + 1) * T], Q[1][:, c * T:(c + 1) * T], col(V_GATEB + c), None, ADD)
            ins.then_inc(S("gl_zr"), 1)
            dve.wait_ge(*signal("gl_l", 3))
            link(V.scalar_tensor_tensor(zg[:, :], zg[:, :], 0.0, lg[:, :], MIN, SUB))
            for c in range(2):
                V.tensor_tensor_scan(cum[:, c * T:(c + 1) * T], cst[:, C_RESET:C_RESET + T], zg[:, c * T:(c + 1) * T],
                                     0.0, MUL, ADD).then_inc(S("gl_cum"), 1)
            dve.wait_ge(*signal("gl_cum", 2))
            c8 = cum[:, :].rearrange("p (n c) -> p n c", n=8)
            V.tensor_tensor(zg[:, :].rearrange("p (n c) -> p n c", n=8), c8, c8[:, :, 63:64].broadcast_to([P, 8, 64]), SUB)\
                .then_inc(S("gl_d"), 1)
            for k, (o, x) in enumerate(((qd, gq), (ki, gk), (ke, gk))):
                dve.wait_ge(*signal("gl_e", k + 1))
                ins = V.tensor_tensor(pairs(o, 0), pairs(x, 0), eg[:, k, :], MUL)
            ins.then_inc(S("gl_ke"), 1)
            dve.wait_ge(*signal("gl_att", 1))
            dve.wait_ge(*signal("att0", 1))
            gmask = cst[:, C_GLA:C_GLA + P].bitcast(i32).rearrange("p (a c) -> p a c", a=1).broadcast_to([P, 4, P])
            for e in range(2):
                V.copy_predicated(att[:, e, :].rearrange("p (a c) -> p a c", a=4), gmask,
                                  Q[2 + e][:, :].rearrange("p (a c) -> p a c", a=4)).then_inc(S("gl_am"), 1)
            for k in range(3):
                dve.wait_ge(*signal("gl_dS", k + 1))
                bank = (Q[4], Q[5], Q[1])[k]
                if k >= 1:
                    dve.wait_ge(*signal("gl_S", k))
                for e in range(2):
                    p0 = 64 * e
                    for c in range(2):
                        o = stt_[p0:p0 + 64, k, c, :]
                        x = bank[p0:p0 + 64, c * 256 + e * P:c * 256 + (e + 1) * P]
                        if k == 0:
                            ins = V.tensor_copy(o, x)
                        else:
                            ins = V.scalar_tensor_tensor(o, stt_[p0:p0 + 64, k - 1, c, :], dec[p0:p0 + 64, 4 * c + k:4 * c + k + 1],
                                                         x, MUL, ADD)
                ins.then_inc(S("gl_S"), 1)
            dve.wait_ge(*signal("gl_o", 1))
            for e in range(2):
                ins = V.tensor_copy(xn[:, e:4:2, :], Q[4 + e][:, :].rearrange("p (c t) -> p c t", c=2))
            ins.then_inc(S("gl_or"), 1)
            dve.wait_ge(*signal("gl_sd", 1))
            V.reciprocal(r8[:, 0:T], st8[:, 0:T]).then_inc(S("gl_r"), 1)
            dve.wait_ge(*signal("gl_or", 1))
            for j in range(2):
                dve.wait_ge(*signal("gf_sp", j + 1))
                link(V.tensor_tensor(pairs(xn, j), Q[2 + j][:, :], pairs(xn, j), MUL))
                V.scalar_tensor_tensor(pairs(xn, j), pairs(xn, j), col(V_GLA), pairs(sog, j), MUL, MUL).then_inc(S("go_y"), 1)
            dve.wait_ge(*signal("la_sd", 1))
            link(V.reciprocal(rstd[:, :], std[:, :]))
            for c in range(2):
                V.scalar_tensor_tensor(cq[:, c, :], cq[:, c, :], col(V_QA + c), rstd[:, 0:T], MUL, MUL).then_inc(S("la_n"), 1)
            V.scalar_tensor_tensor(ckv[:, :], ckv[:, :], col(V_KVA), rstd[:, T:512], MUL, MUL).then_inc(S("la_n"), 1)
            lows("go", xn, oh, ol, 2)
            dve.wait_ge(*signal("la_hi", 1))
            V.tensor_tensor(cql[:, 0:2, :], cq[:, :, :], f(cqh[:, 0:2, :]), SUB).then_inc(S("la_lo"), 2)
            dve.wait_ge(*signal("la_hi", 2))
            V.tensor_tensor(cql[:, 2, :], ckv[:, :], f(cqh[:, 2, :]), SUB).then_inc(S("la_lo"), 1)
            split_lo(dve, SLAB0["ukv"])
            V.tensor_copy(kh[64:P, :, :], kpe[64:P, :].rearrange("p (a t) -> p a t", a=1).broadcast_to([64, 8, T]))\
                .then_inc(S("kpe_in"), 1)
            n = ACC0["uq"]
            for j in range(4):
                dve.wait_ge(*signal("uq_ps", j + 1))
                V.tensor_copy(pairs(qh, j), L[(n + j) % 2][:, :]).then_inc(free_sem(n + j), 1)
            n = ACC0["ukv"]
            for j in range(4):
                dve.wait_ge(*signal("uk_ps", j + 1))
                V.tensor_copy(kh[0:64, 2 * j:2 * j + 2, :].rearrange("p c t -> p (c t)"), L[(n + j) % 2][0:64, :])\
                    .then_inc(free_sem(n + j), 1)
            for b in range(TB):
                dve.wait_ge(*signal("w_used", 2 * SLAB0["uq"] + 2 * b + 2))
                V.tensor_copy(vm[:, b, :], L[(n + 4 + b) % 2][:, :]).then_inc(free_sem(n + 4 + b), 1)
            split_lo(dve, SLAB0["wo2"])
            dve.wait_ge(*signal("ml_sd", 1))
            V.reciprocal(r8[:, :], st8[:, :]).then_inc(S("ml_r"), 1)
            for part, t, g, b0 in (("mqf", qh, V_MLAQ, 2), ("mkf", kh, V_MLAK, 4)):
                acc_freed(dve, ACC0["uq"] + 2 if part == "mqf" else ACC0["ukv"] + 2)
                acc_freed(dve, ACC0["uq"] + 3 if part == "mqf" else ACC0["ukv"] + 3)
                if part == "mkf":
                    dve.wait_ge(*signal("kpe_in", 1))
                for j in range(4):
                    dve.wait_ge(*signal(part + "_sp", j + 1))
                    V.scalar_tensor_tensor(pairs(t, j), pairs(t, j), col(g), Q[b0 + j % 2][:, :], MUL, MUL)\
                        .then_inc(S(part + "_use"), 1)
            dve.wait_ge(*signal("rope", 1))
            tr = xn[64:96, :, :]
            cosb = rope_c[64:96, :].rearrange("p (a t) -> p a t", a=1).broadcast_to([32, 8, T])
            sinb = rope_s[96:P, :].rearrange("p (a t) -> p a t", a=1).broadcast_to([32, 8, T])
            dve.wait_ge(*signal("go_lo", 2))
            for part, t in (("mqf", qh), ("mkf", kh)):
                dve.wait_ge(*signal(part + "_use", 4))
                link(V.tensor_tensor(t[64:96, :, :], t[64:96, :, :], cosb, MUL))
                link(V.tensor_tensor(tr, t[96:P, :, :], sinb, MUL))
                ins = V.tensor_tensor(t[64:96, :, :], t[64:96, :, :], tr, ADD)
                if part == "mqf":
                    link(ins)
            ins.then_inc(S("ml_k"), 1)

            def y_second(u, bank):
                g, blk = u // 2, u % 2
                return V.tensor_copy(xn[:, 4 + 2 * g:6 + 2 * g, blk * P:(blk + 1) * P],
                                     bank[:, 0:256].rearrange("p (c q) -> p c q", c=2))
            dve.wait_ge(*signal("ml_k", 1))
            attention("ml", [1, 2] * 2, prob2, 96 ** -0.5,
                      lambda b: cst[:, C_OWN2:C_OWN2 + P] if b == 1 else cst[:, C_OWN2 - P:C_OWN2 + P], y_second)
            dve.wait_ge(*signal("ml_yo", 4))
            lows("lo", xn, oh, ol, 2, j0=2)
            stage_loop("wo2", 4, add_to_x("wo2", SLAB0["wo2"], ACC0["wo2"]))

            for j in range(4):
                dve.wait_ge(*signal("mem_ps", j + 1))
                V.tensor_copy(pairs(mT, j), Q[j][:, :]).then_inc(S("mem_ok"), 1)
            norm("n6", V_XA)

            def heads_out(name, j0):
                n_, s_ = ACC0[name], SLAB0[name]

                def evac(i, r):
                    slab_used(dve, s_ + r, i)
                    V.tensor_copy(pairs(xq, j0 + r), L[(n_ + r) % 2][:, :]).then_inc(free_sem(n_ + r), 1)
                return evac
            stage_loop("xq", 2, heads_out("xq", 0))
            norm("n7", V_MEM, src=mT, xh=mh, xl=ml)
            stage_loop("xk", 2, heads_out("xk", 2))
            n_v, s_v = ACC0["xv"], SLAB0["xv"]

            def mem_values(i, r):
                slab_used(dve, s_v + r, i)
                V.tensor_copy(xv[:, :, r * 256:(r + 1) * 256], L[(n_v + r) % 2][:, :].rearrange("p (b c) -> p b c", b=TB))\
                    .then_inc(free_sem(n_v + r), 1)
            stage_loop("xv", 2, mem_values)
            dve.wait_ge(*signal("xx_sd", 1))
            V.reciprocal(rx8[:, 0:T], sx8[:, 0:T]).then_inc(S("xx_r"), 1)
            acc_freed(dve, ACC0["xk"])
            acc_freed(dve, ACC0["xk"] + 1)
            for j in range(4):
                dve.wait_ge(*signal("xf_sp", j + 1))
                V.scalar_tensor_tensor(pairs(xq, j), pairs(xq, j), col(V_XQ if j < 2 else V_XK), Q[2 + j % 2][:, :], MUL, MUL)\
                    .then_inc(S("xf_use"), 1)

            def y_third(u, bank):
                return V.tensor_copy(xn[:, 0:4, u * P:(u + 1) * P], bank[:, :].rearrange("p (c q) -> p c q", c=4))
            attention("xa", [2, 2], prob3, 128 ** -0.5, lambda b: cst[:, C_ZERO:C_ZERO + 256], y_third)
            dve.wait_ge(*signal("xa_yo", 2))
            lows("xo", xn, ah, al, 2)
            stage_loop("xo", 4, add_to_x("xo", SLAB0["xo"], ACC0["xo"]))
            norm("n8", V_FFN3)
            dve.wait_ge(*signal("gpad0", 1))
            feed_forward("f3u", "f3d", conv=True)
            for k in range(2):
                dve.wait_ge(*signal("res_ps", 2 * k + 2))
                V.tensor_copy(res[:, k, 512:1024], Q[2 * k + 1][:, :]).then_inc(S("resd"), 1)

        @block.gpsimd
        def _(pool):
            G = nc.gpsimd
            pool.wait_ge(*signal("sines", 1))
            G.tensor_scalar(rope_s[64:P, :], rope_s[64:P, :], cst[64:P, C_SIGN:C_SIGN + 1], None, MUL).then_inc(S("rope"), 1)
            pool.wait_ge(*signal("rope", 1))
            pool.wait_ge(*signal("n2_sum", 1))
            G.memset(pad[:, :, 0:3], 0.0).then_inc(S("pad0"), 1)
            for j in range(4):
                pool.wait_ge(*signal("m_w", j + 1))
                for c in (0, 256):
                    v = wm[:, 2 * j:2 * j + 2, c:c + P]
                    ins = G.affine_select(out=v, in_=v, pattern=[[0, 2], [1, P]], compare_op=ALU.is_ge, fill=0.0,
                                          base=0, channel_multiplier=-1)
                ins.then_inc(S("m_mask"), 1)
            pool.wait_ge(*signal("n4_sum", 1))
            G.memset(att[:, :, :], 0.0).then_inc(S("att0"), 1)
            pool.wait_ge(*signal("n8_sum", 1))
            G.memset(gpad[:, :, 0:2], 0.0).then_inc(S("gpad0"), 1)


def kernel(**inputs):
    import concourse.bacc as _bacc
    from concourse.bass_utils import run_bass_kernel_spmd as _run

    nc = _bacc.Bacc("TRN2", target_bir_lowering=False, num_devices=1)
    arrays, A = {}, {}
    for name, a in inputs.items():
        a = np.ascontiguousarray(a)
        arrays[f"in_{name}"] = a
        A[name] = nc.dram_tensor(f"in_{name}", a.shape, mybir.dt.from_np(a.dtype), kind="ExternalInput").ap()
    c = shape_constants()
    arrays["shape_constants"] = c
    consts = nc.dram_tensor("shape_constants", c.shape, mybir.dt.float32, kind="ExternalInput").ap()
    out = nc.dram_tensor("out", (1, T, D), mybir.dt.float32, kind="ExternalOutput").ap()
    build(nc, A, consts, out)
    r = _run(nc, [arrays], core_ids=[0])
    return r.results[0]["out"]
```

```python
import numpy as np
import concourse.bass as bass
from concourse import mybir
from contextlib import ExitStack

P = 128
T = 256
TB = T // P
D = 1024
DC = D // P
FF = 2816
FC = FF // P
FP = FC // 2
SLAB = 11 * 256
VEC_LOADS, SMALL_LOADS = 27, 9
EPS = 1e-6
NEG = -1.0e30

C_ID, C_ONE = 0, 128
C_PREV, C_OWN, C_ZERO, C_OWN2 = 256, 384, 512, 768
C_RESET, C_GLA, C_HOT = 896, 1152, 1280
C_INV, C_SIGN, C_EPS = 1344, 1345, 1346
C_ALL = 1347

V_FFN1, V_MIX, V_FFN2, V_FINAL, V_MIX2, V_XA, V_MEM, V_FFN3 = 0, 8, 16, 24, 32, 40, 48, 56
V_BQ, V_BK, V_BMQK, V_BMO, V_BG = 64, 72, 74, 82, 90
V_HEAD, V_GATEB, V_GLA, V_QA, V_KVA, V_XQ, V_XK, V_MLAQ, V_MLAK = 106, 114, 116, 117, 119, 120, 121, 122, 123
VEC0 = 124
V_FCW, V_FCB, V_MCONV = 128, 128 + 3 * FC, 128 + 4 * FC
VEC1 = 4 * FC + 32
V_FIN32 = 248

I_AQ, I_AK, I_AV, I_MQK, I_MV, I_MO, I_MI, I_G = 0, 1024, 1280, 1536, 2560, 3584, 4608, 4624
J_Q, J_K, J_V, J_ALR, J_OG, J_CQ, J_CKV, J_PE = 0, 256, 512, 1024, 1040, 1552, 1808, 1936

STAGES = [("f1u", 22, 22), ("f1d", 8, 4), ("wq", 4, 4), ("wkv", 2, 2), ("wmqk", 4, 4), ("wmv", 4, 4),
          ("wmo", 4, 4), ("wg", 8, 8), ("pa", 4, 4), ("pm", 4, 4), ("wo", 4, 4), ("f2u", 22, 22), ("f2d", 8, 4),
          ("w2", 8, 8), ("uq", 1, 4), ("ukv", 1, 6), ("wo2", 4, 4), ("xq", 2, 2), ("xk", 2, 2),
          ("xv", 2, 2), ("xo", 4, 4), ("f3u", 22, 22), ("f3d", 8, 4)]


def first_numbers():
    slab, acc, s, n = {}, {}, 0, 0
    for name, slabs, accs in STAGES:
        slab[name], acc[name] = s, n
        s, n = s + slabs, n + accs
    return slab, acc, s


def shared_signals():
    kinds = [
        ("norm", ("hi", "lo", "sq", "ps", "ss", "sd", "rc", "sp", "rs"), (4, 4, 4, 3, 1, 1, 1, 1, 1),
         [(f"n{k}", 1) for k in (1, 2, 3, 5, 6, 7, 8)]),
        ("softmax", ("mx", "ex", "pn", "sc", "tp", "pt", "pv", "yo"), (4, 4, 4, 1, 1, 1, 1, 1), [("at", 8), ("ml", 4), ("xa", 2)]),
        ("ff", ("hh", "hl", "si", "sr"), (1, 1, 1, 1), [("f1u", FP), ("f2u", FP), ("f3u", FP)]),
    ]
    found = {}
    for kind, signals, each, stages in kinds:
        for sig, n in zip(signals, each):
            base = 0
            for st, units in stages:
                found[f"{st}_{sig}"] = (f"{kind}_{sig}", base)
                base += n * units
    return found


SHARED = shared_signals()
MIX = 20


def shape_constants():
    c = np.zeros((P, C_ALL), np.float32)
    i = np.arange(P)
    c[i, C_ID + i] = 1
    c[:, C_ONE:C_ONE + P] = 1
    q, k = i[:, None], i[None, :]
    c[:, C_PREV:C_PREV + P] = np.where(k > q, 0, NEG)
    c[:, C_OWN:C_OWN + P] = np.where(k <= q, 0, NEG)
    c[:, C_OWN2:C_OWN2 + P] = np.where(k <= q, 0, NEG)
    c[:, C_RESET:C_RESET + T] = np.arange(T) % 64 != 0
    c[:, C_GLA:C_GLA + P] = (q // 64 == k // 64) & (q <= k)
    for h in range(8):
        c[:, C_HOT + h * 8 + h] = 1
    c[:, C_INV] = np.float32(10000.0) ** (-(i % 16).astype(np.float32) / np.float32(16))
    c[:, C_SIGN] = np.where((i // 16) % 2 == 0, -1, 1)
    c[:, C_EPS] = EPS
    return c


def build(nc, A, consts, out):
    f32, f32r, i32 = mybir.dt.float32, mybir.dt.float32r, mybir.dt.int32
    ALU, ACT = mybir.AluOpType, mybir.ActivationFunctionType
    MUL, ADD, SUB, MAX, MIN = ALU.mult, ALU.add, ALU.subtract, ALU.max, ALU.min
    SLAB0, ACC0, SLABS = first_numbers()
    ctx = ExitStack()
    with ctx:
        def sb(name, shape, dt=f32, scope=ctx):
            return scope.enter_context(nc.sbuf_tensor(name, shape, dt))

        sems = {}

        def S(name):
            name = SHARED.get(name, (name, 0))[0]
            if name not in sems:
                sems[name] = ctx.enter_context(nc.semaphore("s_" + name))
            return sems[name]

        def signal(name, count):
            return S(name), SHARED.get(name, (name, 0))[1] + count

        raw = sb("raw", [P, 2, SLAB])
        wh = sb("wh", [P, 2, SLAB], f32r)
        wl = sb("wl", [P, 2, SLAB], f32r)
        xT = sb("xT", [P, DC, T])
        ah = sb("ah", [P, DC, T], f32r)
        al = sb("al", [P, DC, T], f32r)
        xn = sb("xn", [P, DC, T])
        sq = sb("sq", [P, 4, 512])
        cst = sb("cst", [P, C_ALL])
        vec = sb("vec", [P, 256])
        std = sb("std", [P, 512])
        rstd = sb("rstd", [P, 512])
        bav = sb("bav", [P, 256])
        bmv = sb("bmv", [P, 1024])
        nsink = sb("nsink", [P, 32])
        wif = sb("wif", [P, DC, 16])
        walr = sb("walr", [P, DC, 16])
        w2g = sb("w2g", [16, 256])
        bif = sb("bif", [8, 4])
        stmp = sb("stmp", [P, 2, 512])
        vv = sb("vv", [P, 4])
        root = sb("root", [P, 4])
        rcol = sb("rcol", [P, 4])
        g1raw = sb("g1raw", [8, P])
        rope_c = sb("rope_c", [P, T])
        rope_s = sb("rope_s", [P, T])
        rmx = sb("rmx", [P, 2, 4])
        rsm = sb("rsm", [P, 2, 4])
        rs2 = sb("rs2", [P, 2, 4])
        rin = sb("rin", [P, 2, 4])

        with ExitStack() as sc:
            xraw = sb("xraw", [P, TB, D], scope=sc)
        with ExitStack() as sc:
            hh = sb("hh", [P, FC, T], f32r, scope=sc)
            hl = sb("hl", [P, FC, T], f32r, scope=sc)
            sil = sb("sil", [P, 512], scope=sc)
            hid = sb("hid", [P, 512], scope=sc)
            gpad = sb("gpad", [P, 2, T + 2], scope=sc)
            gcv = sb("gcv", [P, 512], scope=sc)
            vraw = sb("vraw", [P, 2, P], scope=sc)
            posi = sb("posi", [P, T], i32, scope=sc)
            ang = sb("ang", [P, T], scope=sc)
            turn = sb("turn", [P, T], scope=sc)
            tmpr = sb("tmpr", [P, T], scope=sc)
            quarter = sb("quarter", [P, T], scope=sc)
        with ExitStack() as sc:
            sigo = sb("sigo", [P, 8, T], scope=sc)
            gate = sb("gate", [P, 16, T], scope=sc)
            with ExitStack() as s2:
                aq = sb("aq", [P, 8, T], scope=s2)
                mv = sb("mv", [P, TB, D], scope=s2)
                akd = sb("akd", [P, 4, T], scope=s2)
                av = sb("av", [P, TB, 256], scope=s2)
                pad = sb("pad", [P, 8, T + 3], scope=s2)
                gtok = sb("gtok", [P, TB, 16], scope=s2)
                acol = sb("acol", [P, TB, 8], scope=s2)
                ti = sb("ti", [8, 512], scope=s2)
                lse = sb("lse", [8, T], scope=s2)
                Gc = sb("Gc", [8, T], scope=s2)
                ai = sb("ai", [8, T], scope=s2)
                Mx = sb("Mx", [8, T], scope=s2)
                gm = sb("gm", [8, T], scope=s2)
                en = sb("en", [8, T], scope=s2)
                rden = sb("rden", [8, T], scope=s2)
                with ExitStack() as s3:
                    prob1 = sb("prob1", [P, 2, 4, T], scope=s3)
                    probT1 = sb("probT1", [P, 2, 512], scope=s3)
                with ExitStack() as s3:
                    wm = sb("wm", [P, 8, 384], scope=s3)
            with ExitStack() as s2:
                bh = sb("bh", [P, DC, T], f32r, scope=s2)
                bl = sb("bl", [P, DC, T], f32r, scope=s2)
                ch = sb("ch", [P, DC, T], f32r, scope=s2)
                cl = sb("cl", [P, DC, T], f32r, scope=s2)
                mgb = sb("mgb", [P, 512], scope=s2)
                mgs = sb("mgs", [P, 512], scope=s2)
        with ExitStack() as sc:
            cq = sb("cq", [P, 2, T], scope=sc)
            ckv = sb("ckv", [P, T], scope=sc)
            kpe = sb("kpe", [P, T], scope=sc)
            oh = sb("oh", [P, DC, T], f32r, scope=sc)
            ol = sb("ol", [P, DC, T], f32r, scope=sc)
            st8 = sb("st8", [8, 512], scope=sc)
            r8 = sb("r8", [8, 512], scope=sc)
            with ExitStack() as s2:
                gq = sb("gq", [P, 2, T], scope=s2)
                gk = sb("gk", [P, 2, T], scope=s2)
                gv = sb("gv", [P, TB, 512], scope=s2)
                sog = sb("sog", [P, 4, T], scope=s2)
                alr = sb("alr", [16, T], scope=s2)
                zg = sb("zg", [P, 512], scope=s2)
                lg = sb("lg", [P, 512], scope=s2)
                cum = sb("cum", [P, 512], scope=s2)
                eg = sb("eg", [P, 3, 512], scope=s2)
                qd = sb("qd", [P, 2, T], scope=s2)
                ki = sb("ki", [P, 2, T], scope=s2)
                ke = sb("ke", [P, 2, T], scope=s2)
                ketok = sb("ketok", [P, TB, 256], scope=s2)
                att = sb("att", [P, 2, 512], scope=s2)
                dec = sb("dec", [P, 8], scope=s2)
                stt_ = sb("stt_", [P, 3, 2, P], scope=s2)
            with ExitStack() as s2:
                qh = sb("qh", [P, 8, T], scope=s2)
                kh = sb("kh", [P, 8, T], scope=s2)
                vm = sb("vm", [P, TB, 512], scope=s2)
                cqh = sb("cqh", [P, 3, T], f32r, scope=s2)
                cql = sb("cql", [P, 3, T], f32r, scope=s2)
                prob2 = sb("prob2", [P, 2, 4, T], scope=s2)
                probT2 = sb("probT2", [P, 2, 512], scope=s2)
        with ExitStack() as sc:
            memraw = sb("memraw", [P, TB, D], scope=sc)
            mT = sb("mT", [P, DC, T], scope=sc)
            mh = sb("mh", [P, DC, T], f32r, scope=sc)
            ml = sb("ml", [P, DC, T], f32r, scope=sc)
            xq = sb("xq", [P, 8, T], scope=sc)
            xv = sb("xv", [P, TB, 512], scope=sc)
            sx8 = sb("sx8", [8, 512], scope=sc)
            rx8 = sb("rx8", [8, 512], scope=sc)
            prob3 = sb("prob3", [P, 2, 4, T], scope=sc)
            probT3 = sb("probT3", [P, 2, 512], scope=sc)
        with ExitStack() as sc:
            res = sb("res", [P, TB, D], scope=sc)

        L = [ctx.enter_context(nc.psum_tensor(f"acc{i}", [P, 512], f32)) for i in range(2)]
        Q = [ctx.enter_context(nc.psum_tensor(f"part{i}", [P, 512], f32)) for i in range(6)]

        ident = cst[:, C_ID:C_ID + P]
        ones = cst[:, C_ONE:C_ONE + P]
        eps = cst[:, C_EPS:C_EPS + 1]

        def sel(h):
            return cst[0:8, C_ID + h:C_ID + h + 1].broadcast_to([8, P])

        def hot(h, rows=P):
            return cst[0:rows, C_HOT + h * 8:C_HOT + (h + 1) * 8]

        def col(n, lo=0, hi=P):
            return vec[lo:hi, n:n + 1]

        def pairs(t, j):
            return t[:, 2 * j:2 * j + 2, :].rearrange("p c t -> p (c t)")

        def rpair(t, j):
            return t[:, :, :].rearrange("p c t -> p (c t)")[:, bass.ds(j * 512, 512)]

        def f(ap):
            return ap.bitcast(f32)

        def two_t(ap):
            return ap.rearrange("p (c t) -> p c t", c=2)

        qk = pad[:, :, 3:T + 3]

        factor = rstd[:, 0:T].rearrange("p (a t) -> p a t", a=1).broadcast_to([P, 2, T])

        def loaded(eng, s, i=0):
            eng.wait_ge(*signal(f"raw{s % 2}", 16 * (s // 2 + 1) + 16 * i))

        def lo_ready(eng, s, i, half):
            eng.wait_ge(*signal("w_lo", 2 * s + half + 1 + 4 * i))

        def slab_used(eng, s, i=0, half=1):
            eng.wait_ge(*signal("w_used", 2 * s + half + 1 + 4 * i))

        def acc_freed(eng, n, i=0):
            eng.wait_ge(*signal(f"acc_free{n % 2}", n // 2 + 1 + i))

        def free_sem(n):
            return S(f"acc_free{n % 2}")

        def halves(nk):
            return (0, (nk + 1) // 2), ((nk + 1) // 2, nk)

        def looped(eng, n, body, peel=False):
            if peel:
                body(0, False)
            if n > 2:
                with eng.Fori(1 if peel else 0, n - 1) as i:
                    body(i, False)
            else:
                for i in range(1 if peel else 0, n - 1):
                    body(i, False)
            body(n - 1, True)

        def columns(name):
            return {"f1d": 11, "f2d": 11, "f3d": 11, "xo": 4}.get(name, 8), 256

        EXTRA = {SLAB0["w2"] + 7: "pe", SLAB0["uq"]: "uq", SLAB0["ukv"]: "ukv"}
        STAGE_OF = {SLAB0[n] + k: n for n, c, _ in STAGES for k in range(c)}

        def shape_of(s):
            return columns(STAGE_OF[s]) if s in STAGE_OF else None

        def parts(kind, t, slot):
            r = raw[:, slot, :]
            w = t[:, slot, :]
            if kind == "pe":
                d = w[:, 0:2048].rearrange("p (k c) -> p k c", k=8)
                s = r[:, 0:8 * 160].rearrange("p (k c) -> p k c", k=8)
                return [(d[:, :, 0:160], s), (d[:, :, 160:192], s[:, :, 128:160]),
                        (d[:, :, 192:224], s[:, :, 128:160]), (d[:, :, 224:240], s[:, :, 144:160]),
                        (d[:, :, 240:256], s[:, :, 128:144])]
            if kind == "uq":
                d = w[:, 0:2048].rearrange("p (k c) -> p k c", k=16)
                s = r[:, 0:1536].rearrange("p (k c) -> p k c", k=16)
                return [(d[:, :, 0:96], s), (d[:, :, 96:112], s[:, :, 80:96]), (d[:, :, 112:128], s[:, :, 64:80])]
            return [(w[:, 0:512], r[:, 0:512]), (w[:, 512:1024], r[:, 512:1024])]

        def split_hi(act, s, i=0):
            if s >= SLABS:
                return
            loaded(act, s, i)
            slot = s % 2
            if s in EXTRA:
                slab_used(act, s - 2)
                todo = parts(EXTRA[s], wh, slot)
                for n, (d, r) in enumerate(todo):
                    ins = nc.scalar.activation(d, r, ACT.Copy)
                ins.then_inc(S("w_hi"), 2)
                return
            nk, nw = shape_of(s)
            for half, (a, b) in enumerate(halves(nk)):
                if s >= 2:
                    slab_used(act, s - 2, i, half if shape_of(s - 2) == (nk, nw) and s - 2 not in EXTRA else 1)
                nc.scalar.activation(wh[:, slot, a * nw:b * nw], raw[:, slot, a * nw:b * nw],
                                     ACT.Copy).then_inc(S("w_hi"), 1)

        def split_lo(dve, s, i=0):
            if s >= SLABS:
                return
            slot = s % 2
            if s in EXTRA:
                dve.wait_ge(*signal("w_hi", 2 * s + 2))
                for (d, r), (h, _) in zip(parts(EXTRA[s], wl, slot), parts(EXTRA[s], wh, slot)):
                    ins = nc.vector.tensor_tensor(d, r, f(h), SUB)
                ins.then_inc(S("w_lo"), 2)
                return
            nk, nw = shape_of(s)
            for half, (a, b) in enumerate(halves(nk)):
                dve.wait_ge(*signal("w_hi", 2 * s + half + 1 + 4 * i))
                nc.vector.tensor_tensor(wl[:, slot, a * nw:b * nw], raw[:, slot, a * nw:b * nw],
                                        f(wh[:, slot, a * nw:b * nw]), SUB).then_inc(S("w_lo"), 1)

        block = ctx.enter_context(nc.Block())

        @block.sync
        def _(sp):
            sp.dma_start(cst[:, 0:256], consts[:, 0:256]).then_inc(S("ident"), 16)
            sp.dma_start(xraw[:, :, :], A["x"][0].rearrange("(b p) c -> p b c", p=P)).then_inc(S("x_in"), 16)
            win = A["w_in"][0].rearrange("(k p) c -> p k c", p=P)
            win2 = A["w_in_2"][0].rearrange("(k p) c -> p k c", p=P)

            def load(s, i, src, kind=None):
                if s >= 2:
                    sp.wait_ge(*signal("w_lo", 2 * s - 2 + 4 * i))
                nk, nw = shape_of(s)
                if kind == "pe":
                    d = raw[:, s % 2, 0:8 * 160].rearrange("p (k c) -> p k c", k=8)
                elif kind == "uq":
                    d = raw[:, s % 2, 0:1536].rearrange("p (k c) -> p k c", k=2)
                elif kind == "ukv":
                    d = raw[:, s % 2, 0:1024]
                else:
                    d = raw[:, s % 2, 0:nk * nw].rearrange("p (k c) -> p k c", k=nk)
                sp.dma_start(d, src).then_inc(S(f"raw{s % 2}"), 16)

            def many(name, w, first):
                s0, count = SLAB0[name], dict((n, c) for n, c, _ in STAGES)[name]

                def body(i):
                    for r in range(2):
                        load(s0 + r, i, w[:, :, bass.ds(first + i * 512 + r * 256, 256)])
                if count > 2:
                    with sp.Fori(0, count // 2) as i:
                        body(i)
                else:
                    body(0)

            def gains_and_biases():
                rows = [(V_MIX, "mix_norm"), (V_FFN2, "ffn2_norm"),
                        (V_MIX2, "norm_mix_2"), (V_XA, "norm_xa_2"), (V_MEM, "norm_mem_2"), (V_FFN3, "norm_ffn_2"),
                        (V_GATEB, "gla_gate_b_2"), (V_GLA, "gla_out_norm_2"), (V_QA, "mla_q_a_norm_2"),
                        (V_KVA, "mla_kv_a_norm_2"), (V_XQ, "xa_q_norm_2"), (V_XK, "xa_k_norm_2")]
                todo = []
                for v, name in rows:
                    n = A[name].shape[1] // P
                    todo.append((vraw[v:v + n, 0, :], A[name][0].rearrange("(c p) -> c p", p=P)))
                todo.append((vraw[V_FINAL:V_FINAL + 8, 0, :], A["final_norm"].rearrange("(c p) -> c p", p=P)))
                todo.append((vraw[V_HEAD:V_HEAD + 8, 0, :], A["mlstm_head_norm"][0]))
                b = A["b_in"][0]
                for v, lo, n in ((V_BQ, I_AQ, 10), (V_BMQK, I_MQK, 8), (V_BMO, I_MO, 8), (V_BG, I_G, 16)):
                    todo.append((vraw[v:v + n, 0, :], b[lo:lo + n * P].rearrange("(c p) -> c p", p=P)))
                for v, name in ((V_MLAQ, "mla_q_norm_2"), (V_MLAK, "mla_k_norm_2")):
                    g = A[name]
                    todo += [(vraw[v:v + 1, 0, 0:96], g), (vraw[v:v + 1, 0, 96:112], g[:, 80:96]),
                             (vraw[v:v + 1, 0, 112:128], g[:, 64:80])]
                todo.append((vraw[0:3 * FC, 1, :], A["ffn_conv_w_2"][0].rearrange("j (c p) -> (j c) p", p=P)))
                todo.append((vraw[3 * FC:4 * FC, 1, :], A["ffn_conv_b_2"][0].rearrange("(c p) -> c p", p=P)))
                todo.append((vraw[4 * FC:4 * FC + 32, 1, :], A["mlstm_conv"][0].rearrange("j (c p) -> (j c) p", p=P)))
                for d, s in todo:
                    sp.dma_start(d, s).then_inc(S("vec_in"), 16)
                assert len(todo) == VEC_LOADS

            def feed_forward(up, down, gate_w, up_w, down_w):
                g = gate_w.rearrange("(k p) c -> p k c", p=P)
                u = up_w.rearrange("(k p) c -> p k c", p=P)
                s0 = SLAB0[up]
                if s0 == 0:
                    load(0, 0, g[:, :, 0:256])
                    load(1, 0, u[:, :, 0:256])
                    sp.dma_start(cst[:, 256:C_ALL], consts[:, 256:C_ALL]).then_inc(S("consts"), 16)
                    gains_and_biases()
                with sp.Fori(1 if s0 == 0 else 0, FP) as i:
                    for r, w in ((0, g), (1, u)):
                        sp.wait_ge(*signal("w_lo", 2 * (s0 + r) - 2 + 4 * i))
                        d = raw[:, (s0 + r) % 2, 0:2048].rearrange("p (k c) -> p k c", k=8)
                        sp.dma_start(d, w[:, :, bass.ds(i * 256, 256)]).then_inc(S(f"raw{(s0 + r) % 2}"), 16)
                d = down_w.rearrange("(k p) c -> p k c", p=P)
                s0 = SLAB0[down]
                with sp.Fori(0, 4) as i:
                    for r in range(2):
                        load(s0 + r, i, d[:, 11 * r:11 * r + 11, bass.ds(i * 256, 256)])

            feed_forward("f1u", "f1d", A["ffn1_w_gate"][0], A["ffn1_w_up"][0], A["ffn1_w_down"][0])
            many("wq", win, I_AQ)
            many("wkv", win, I_AK)
            many("wmqk", win, I_MQK)
            many("wmv", win, I_MV)
            many("wmo", win, I_MO)
            many("wg", win, I_G)
            many("pa", A["w_proj_attn"][0].rearrange("(k p) c -> p k c", p=P), 0)
            many("pm", A["w_proj_mlstm"][0].rearrange("(k p) c -> p k c", p=P), 0)
            many("wo", A["w_out"][0].rearrange("(k p) c -> p k c", p=P), 0)
            feed_forward("f2u", "f2d", A["ffn2_w_gate"][0], A["ffn2_w_up"][0], A["ffn2_w_down"][0])
            s0 = SLAB0["w2"]
            for k, c in enumerate((J_Q, J_K, J_V, J_V + 256, J_OG, J_OG + 256, J_CQ)):
                load(s0 + k, 0, win2[:, :, c:c + 256])
            load(s0 + 7, 0, win2[:, :, J_CKV:J_CKV + 160], "pe")
            load(SLAB0["uq"], 0, A["mla_w_uq_2"][0].rearrange("(k p) c -> p k c", p=P), "uq")
            load(SLAB0["ukv"], 0, A["mla_w_ukv_2"][0], "ukv")
            many("wo2", A["w_out_2"][0].rearrange("(k p) c -> p k c", p=P), 0)
            many("xq", A["xa_w_q_2"][0].rearrange("(k p) c -> p k c", p=P), 0)
            acc_freed(sp, ACC0["wo2"] + 2)
            acc_freed(sp, ACC0["wo2"] + 3)
            sp.dma_start(memraw[:, :, :], A["mem_2"][0].rearrange("(b p) c -> p b c", p=P)).then_inc(S("mem_in"), 16)
            kv = A["xa_w_kv_2"][0].rearrange("(k p) c -> p k c", p=P)
            many("xk", kv, 0)
            many("xv", kv, 512)
            many("xo", A["xa_w_o_2"][0].rearrange("(k p) c -> p k c", p=P), 0)
            feed_forward("f3u", "f3d", A["ffn_w_gate_2"][0], A["ffn_w_up_2"][0], A["ffn_w_down_2"][0])
            for tb in range(TB):
                sp.wait_ge(*signal("resa", tb + 1))
                sp.wait_ge(*signal("resd", tb + 1))
                sp.dma_start(out[0, tb * P:(tb + 1) * P, :], res[:, tb, :]).then_inc(S("stored"), 16)
            sp.wait_ge(*signal("stored", 16 * TB))

        @block.tensor
        def _(pe):
            mm = nc.tensor.matmul

            def normed_input(st):
                return lambda k: k % 2 == 0 and pe.wait_ge(*signal(st + "_lo", k // 2 + 1))

            def norm_sums(st):
                pe.wait_ge(*signal(st + "_ps", 3))
                if st == "n5":
                    pe.wait_ge(*signal("n5_ps2", 3))
                for c in range(2):
                    for b in range(TB):
                        t = slice(c * T + b * P, c * T + (b + 1) * P)
                        ins = mm(Q[0][:, T + b:T + b + 1], sq[:, 0, t], ones[:, 0:1],
                                 start=c + b == 0, stop=c == 1, skip_group_check=True)
                        if st == "n5":
                            ins = mm(Q[0][:, T + 2 + b:T + 3 + b], xn[:, c, b * P:(b + 1) * P], ones[:, 0:1],
                                     start=False, stop=c == 1, skip_group_check=True)
                ins.then_inc(S(st + "_ss"), 1)

            def norm_spread(st):
                pe.wait_ge(*signal(st + "_rc", 1))
                for n in range(2 if st == "n5" else 1):
                    for b in range(TB):
                        ins = mm(Q[n][:, b * P:(b + 1) * P], rcol[:, 2 * n + b:2 * n + b + 1].broadcast_to([P, P]), ident,
                                 start=b == 0, stop=b == 1, skip_group_check=True)
                ins.then_inc(S(st + "_sp"), 1)

            def late(st):
                return lambda k: k == 6 and norm_spread(st)

            def open_acc(n, i=0):
                if n >= 2:
                    acc_freed(pe, n - 2, i)

            def product(s, i, nk, n, xh, xl, k0=0, first=True, last=True, tokens=False,
                        before=None):
                o, slot = L[n % 2], s % 2
                for half, (ka, kb) in enumerate(halves(nk)):
                    lo_ready(pe, s, i, half)
                    for k in range(ka, kb):
                        if before is not None:
                            before(k)
                        for m in range(2):
                            dst = o[:, m * T:(m + 1) * T]
                            st = first and k == 0 and m == 0
                            en_ = last and k == nk - 1 and m == 1
                            if tokens:
                                c = slice(k * 256, (k + 1) * 256)
                                t = slice(m * P, (m + 1) * P)
                                xa, xb = xh[:, k0 + k, t], xl[:, k0 + k, t]
                                three = ((xa, wh[:, slot, c]), (xb, wh[:, slot, c]), (xa, wl[:, slot, c]))
                            else:
                                c = slice(k * 256 + m * P, k * 256 + (m + 1) * P)
                                xa, xb = xh[:, k0 + k, :], xl[:, k0 + k, :]
                                three = ((wh[:, slot, c], xa), (wh[:, slot, c], xb), (wl[:, slot, c], xa))
                            for q, (a, b) in enumerate(three):
                                ins = mm(dst, a, b, start=st and q == 0, stop=en_ and q == 2, skip_group_check=True)
                    ins.then_inc(S("w_used"), 1)

            def opening(name, st, xh, xl, extra=None):
                s, n = SLAB0[name], ACC0[name]
                open_acc(n)
                product(s, 0, 8, n, xh, xl, before=normed_input(st))
                norm_sums(st)
                open_acc(n + 1)
                if extra is not None:
                    product(s + 1, 0, 8, n + 1, xh, xl, before=lambda k: (late(st)(k), extra(k)))
                else:
                    product(s + 1, 0, 8, n + 1, xh, xl, before=late(st))

            def two(name, xh, xl, nk=8, tokens=False, count=None):
                s, n = SLAB0[name], ACC0[name]
                count = count or dict((a, b) for a, b, _ in STAGES)[name]

                def body(i):
                    for r in range(2):
                        open_acc(n + r, i)
                        product(s + r, i, nk, n + r, xh, xl, tokens=tokens)
                if count > 2:
                    with pe.Fori(0, count // 2) as i:
                        body(i)
                else:
                    body(0)

            def feed_forward(up, down, st, then=None):
                s, n = SLAB0[up], ACC0[up]
                opening(up, st, ah, al)
                if then is not None:
                    then()
                with pe.Fori(1, FP) as i:
                    for r in range(2):
                        pe.wait_ge(free_sem(n + r), (n + r - 2) // 2 + 1 + i)
                        product(s + r, i, 8, n + r, ah, al)
                s, n = SLAB0[down], ACC0[down]
                for q in range(4):
                    open_acc(n + q)
                    for r in range(2):
                        if q == 0:
                            pe.wait_ge(*signal(up + "_hl", FP if r else 6))
                        product(s + 2 * q + r, 0, 11, n + q, hh, hl, k0=11 * r, first=r == 0, last=r == 1)

            def attention(st, units, scores, prob, probT, values, outputs):

                def do_scores(u):
                    if u >= 1:
                        pe.wait_ge(*signal(st + "_mx", 4 * u))
                    for hh_ in range(4):
                        q, k = scores(u, hh_)
                        w = k.shape[1]
                        ins = mm(Q[hh_ % 2][:, (hh_ // 2) * 256:(hh_ // 2) * 256 + w], q, k,
                                 start=True, stop=True, skip_group_check=True)
                    ins.then_inc(S(st + "_sc"), 1)

                def do_transposes(u):
                    if u >= 1:
                        pe.wait_ge(*signal(st + "_pt", u))
                    pe.wait_ge(*signal(st + "_pn", 4 * u + 4))
                    for b in range(units[u]):
                        for hh_ in range(4):
                            ins = nc.tensor.transpose(Q[2 + b][:, hh_ * P:(hh_ + 1) * P],
                                                      prob[:, u % 2, hh_, b * P:(b + 1) * P], ident)
                    ins.then_inc(S(st + "_tp"), 1)

                def do_outputs(u):
                    pe.wait_ge(*signal(st + "_pt", u + 1))
                    if u >= 2:
                        pe.wait_ge(*signal(st + "_yo", u - 1))
                    bank = Q[4 + u % 2]
                    for lo, hi, o0, hs in outputs:
                        for b in range(units[u]):
                            v = values(u, b, hs[0])
                            x = probT[:, b, :].rearrange("p (h q) -> p h q", h=4)[:, hs[0]:hs[-1] + 1:max(1, (hs[-1] - hs[0])), :] \
                                if len(hs) > 1 else probT[:, b, hs[0] * P:(hs[0] + 1) * P]
                            ins = mm(bank[lo:hi, o0:o0 + P * len(hs)], v, x, start=b == 0 and o0 == 0,
                                     stop=b == units[u] - 1, skip_group_check=True)
                    ins.then_inc(S(st + "_pv"), 1)
                return do_scores, do_transposes, do_outputs

            def in_turn(units, do_scores, do_transposes, do_outputs):
                do_scores(0)
                for u in range(units):
                    if u + 1 < units:
                        do_scores(u + 1)
                    do_transposes(u)
                    do_outputs(u)

            def head_sums(st, x, heads, bank, o0, first, rows=P):
                for j in range(heads // 2):
                    pe.wait_ge(*signal(st + "_hs", j + 1))
                    for c in range(2):
                        h = 2 * j + c
                        ins = mm(bank[0:8, o0:o0 + T], hot(h, rows), x[0:rows, j, c * T:(c + 1) * T],
                                 start=first and h == 0, stop=h == heads - 1, skip_group_check=True)
                ins.then_inc(S(st + "_ss"), 1)

            def spread(st, r, o0, heads, banks, wait):
                for j in range(heads // 2):
                    wait(j)
                    for c in range(2):
                        h = 2 * j + c
                        ins = mm(banks[j % len(banks)][:, c * T:(c + 1) * T], sel(h), r[0:8, o0:o0 + T],
                                 start=c == 0, stop=c == 1, skip_group_check=True)
                    ins.then_inc(S(st + "_sp"), 1)

            pe.wait_ge(*signal("ident", 16))
            pe.wait_ge(*signal("g1_in", 16))
            nc.tensor.transpose(Q[4][:, 0:8], g1raw[0:8, :], cst[0:8, C_ID:C_ID + 8]).then_inc(S("g1_ps"), 1)
            pe.wait_ge(*signal("x_in", 16))

            def transpose_in(src, st, banks=Q[0:4]):
                for j in range(4):
                    for c in range(2):
                        for b in range(TB):
                            o = (c * TB + b) * P
                            k = 2 * j + c
                            ins = nc.tensor.transpose(banks[j][:, o:o + P], src[:, b, k * P:(k + 1) * P], ident)
                    ins.then_inc(S(st), 1)

            transpose_in(xraw, "x_ps")

            def gains_in():
                pe.wait_ge(*signal("consts", 16))
                pe.wait_ge(*signal("vec_in", 16 * VEC_LOADS))
                pe.wait_ge(*signal("g1_ok", 1))
                nc.tensor.transpose(Q[4][:, 0:VEC0], vraw[0:VEC0, 0, :], cst[0:VEC0, C_ID:C_ID + VEC0])
                nc.tensor.transpose(Q[4][:, P:P + VEC1], vraw[0:VEC1, 1, :], cst[0:VEC1, C_ID:C_ID + VEC1])\
                    .then_inc(S("vec_ps"), 1)

            feed_forward("f1u", "f1d", "n1", then=gains_in)

            opening("wq", "n2", ah, al)
            s, n = SLAB0["wq"], ACC0["wq"]
            for k in (2, 3):
                open_acc(n + k)
                product(s + k, 0, 8, n + k, ah, al)
            s, n = SLAB0["wkv"], ACC0["wkv"]
            open_acc(n)
            product(s, 0, 8, n, ah, al)
            open_acc(n + 1)
            product(s + 1, 0, 8, n + 1, ah, al, tokens=True)

            def if_products():
                pe.wait_ge(*signal("narrow", 2))
                for b in range(TB):
                    for k in range(DC):
                        ins = mm(Q[5][:, b * 16:(b + 1) * 16], xT[:, k, b * P:(b + 1) * P], wif[:, k, :],
                                 start=k == 0 and b == 0, stop=k == DC - 1, skip_group_check=True)
                ins.then_inc(S("if_ps"), 1)

            def if_transposes():
                pe.wait_ge(*signal("if_tok", 1))
                for g in range(2):
                    for b in range(TB):
                        ins = nc.tensor.transpose(Q[4][0:8, g * T + b * P:g * T + (b + 1) * P],
                                                  gtok[:, b, g * 8:(g + 1) * 8], ident)
                ins.then_inc(S("if_T"), 1)

            def a_scores(u, h):
                g, blk = u // 2, u % 2
                p0, hd = 64 * (h % 2), 4 * g + h
                return (aq[p0:p0 + 64, hd // 2, blk * P:(blk + 1) * P],
                        akd[p0:p0 + 64, g, 0:(blk + 1) * P])

            at_scores, at_transposes, at_outputs = attention(
                "at", [1, 2] * 4, a_scores, prob1, probT1,
                lambda u, b, h: av[:, b, (u // 2) * 64:(u // 2 + 1) * 64],
                [(0, 64, 0, [0, 2]), (64, P, 0, [1, 3])])

            def m_spread():
                pe.wait_ge(*signal("m_M", 1))
                pe.wait_ge(*signal("at_yo", 8))
                for b in range(TB):
                    ins = nc.tensor.transpose(Q[5][:, b * 8:(b + 1) * 8], ai[0:8, b * P:(b + 1) * P], cst[0:8, C_ID:C_ID + 8])
                ins.then_inc(S("m_acol"), 1)
                pe.wait_ge(*signal("at_pt", 8))
                spread("mm", Mx, 0, 8, Q[0:4], lambda j: None)

            s, n = SLAB0["wmqk"], ACC0["wmqk"]
            pe.wait_ge(*signal("keys", 1))
            acc_freed(pe, ACC0["wkv"] + 1)
            for m in range(MIX):
                u, odd = divmod(m, 2)
                if not odd and u < 8:
                    at_scores(u)
                if not odd and 1 <= u <= 8:
                    if u == 1:
                        pe.wait_ge(*signal("if_use", 1))
                    at_outputs(u - 1)
                if m == 0:
                    if_products()
                open_acc(n + m)
                product(s + m, 0, 8, n + m, ah, al, tokens=4 <= m < 8,
                        before=(lambda k: k == 4 and at_transposes(u)) if odd and u < 8 else None)
                if m == 0:
                    if_transposes()
                elif m == 17:
                    m_spread()

            def m_scores(h):
                p0 = 64 * (h % 2)
                pe.wait_ge(*signal("m_qk", 1))
                if h < 4:
                    pe.wait_ge(*signal("m_D", 4 * (h + 1)))
                else:
                    pe.wait_ge(*signal("m_S", h - 3))
                bank = Q[h % 4]
                for b in range(TB):
                    ks = qk[p0:p0 + 64, 4 + h // 2, b * P:(b + 1) * P]
                    qs = qk[p0:p0 + 64, h // 2, b * P:T]
                    ins = mm(bank[:, b * 256:b * 256 + T - b * P], ks, qs, start=b == 0, stop=True, skip_group_check=True)
                ins.then_inc(S("m_qkT"), 1)

            def m_numerators(h):
                pe.wait_ge(*signal("m_S", max(h + 1, h // 2 + 5)))
                bank = Q[h // 2]
                for b in range(TB):
                    sc_ = wm[:, h, b * 256:b * 256 + T - b * P]
                    ins = mm(bank[:, (h % 2) * T + b * P:(h % 2) * T + T], mv[:, b, h * P:(h + 1) * P], sc_,
                             start=b == 0 and h % 2 == 0, stop=b == 1, skip_group_check=True)
                    if h == 0 and b == 0:
                        pe.wait_ge(*signal("m_acolr", 1))
                    den = mm(Q[5][0:8, b * P:T], hot(h), sc_, start=h == 0 and b == 0, stop=h == 7 and b == 1,
                             skip_group_check=True)
                den.then_inc(S("m_num"), 1)

            def attention_projection(k):
                open_acc(ACC0["pa"] + k)
                product(SLAB0["pa"] + k, 0, 8, ACC0["pa"] + k, ah, al)

            for h in range(4):
                m_scores(h)
            pe.wait_ge(*signal("at_lo", 4))
            attention_projection(0)
            for h in range(4, 8):
                m_scores(h)
            for h in range(8):
                m_numerators(h)
            attention_projection(1)
            head_sums("m", sq, 8, Q[4], 0, True)
            attention_projection(2)
            spread("mf", rden, 0, 8, Q[0:4], lambda j: pe.wait_ge(*signal("m_r", 1)))
            attention_projection(3)
            pe.wait_ge(*signal("mo_lo", 4))
            two("pm", bh, bl)
            pe.wait_ge(*signal("mg_lo", 4))
            two("wo", ch, cl)

            feed_forward("f2u", "f2d", "n3")

            opening("w2", "n5", ah, al)
            s, n = SLAB0["w2"], ACC0["w2"]
            for k in range(2, 8):
                open_acc(n + k)
                product(s + k, 0, 8, n + k, ah, al, tokens=k in (2, 3))
                if k == 2:
                    for c in range(DC):
                        ins = mm(Q[2][0:16, 0:T], walr[:, c, :], xT[:, c, :], start=c == 0, stop=c == DC - 1)
                    ins.then_inc(S("alr_ps"), 1)
                elif k == 4:
                    pe.wait_ge(*signal("alr", 1))
                    for c in range(2):
                        ins = mm(Q[1][:, c * T:(c + 1) * T], w2g[0:16, c * P:(c + 1) * P], alr[0:16, :],
                                 start=c == 0, stop=True, skip_group_check=True)
                    ins.then_inc(S("gl_z"), 1)
            pe.wait_ge(*signal("gl_ke", 1))
            for b in range(TB):
                for c in range(2):
                    ins = nc.tensor.transpose(Q[0][:, b * 256 + c * P:b * 256 + (c + 1) * P], ke[:, c, b * P:(b + 1) * P], ident)
            ins.then_inc(S("gl_keT"), 1)
            for c in range(2):
                for b in range(TB):
                    for e in range(2):
                        p0 = 64 * e
                        t = slice(b * P, (b + 1) * P)
                        ins = mm(Q[2 + e][:, c * 256 + b * P:c * 256 + (b + 1) * P], ki[p0:p0 + 64, c, t], qd[p0:p0 + 64, c, t],
                                 start=c == 0 and b == 0, stop=True, skip_group_check=True)
            ins.then_inc(S("gl_att"), 1)
            pe.wait_ge(*signal("gl_ketok", 1))
            pe.wait_ge(*signal("gl_zr", 1))
            for k in range(3):
                p0 = 64 * (k % 2)
                bank = (Q[4], Q[5], Q[1])[k]
                for c in range(2):
                    ins = mm(bank[:, c * 256:(c + 1) * 256], ketok[p0:p0 + 64, k // 2, c * P:(c + 1) * P],
                             gv[p0:p0 + 64, k // 2, c * 256:(c + 1) * 256], start=c == 0, stop=True, skip_group_check=True)
                ins.then_inc(S("gl_dS"), 1)
            pe.wait_ge(*signal("gl_am", 2))
            pe.wait_ge(*signal("gl_S", 3))
            for h in range(4):
                c, e = h // 2, h % 2
                p0 = 64 * e
                bank = Q[4 + e]
                for b in range(TB):
                    mm(bank[:, c * T + b * P:c * T + (b + 1) * P], gv[:, b, h * P:(h + 1) * P],
                       att[:, e, c * 256 + b * P:c * 256 + (b + 1) * P], start=c == 0 and b == 0, stop=False, skip_group_check=True)
                for k in range(1, 4):
                    ins = mm(bank[:, c * T + k * 64:c * T + (k + 1) * 64], stt_[p0:p0 + 64, k - 1, c, :],
                             qd[p0:p0 + 64, c, k * 64:(k + 1) * 64], start=False, stop=True, skip_group_check=True)
            ins.then_inc(S("gl_o"), 1)
            head_sums("gl", sq, 4, Q[0], 0, True)
            spread("gf", r8, 0, 4, Q[2:4], lambda j: pe.wait_ge(*signal("gl_r", 1)))

            pe.wait_ge(*signal("la_sq", 2))
            mm(Q[1][:, 0:T], ones, sq[:, 2, 0:T], start=True, stop=False, skip_group_check=True)
            mm(Q[1][:, 0:T], ones, sq[:, 2, T:512], start=False, stop=False, skip_group_check=True)
            mm(Q[1][:, T:512], ones, sq[:, 3, 0:T], start=False, stop=True, skip_group_check=True).then_inc(S("la_sum"), 1)
            pe.wait_ge(*signal("la_lo", 3))
            s, n = SLAB0["uq"], ACC0["uq"]
            lo_ready(pe, s, 0, 1)
            for j in range(4):
                open_acc(n + j)
                for c in range(2):
                    for k in range(2):
                        w = slice(k * 1024 + (2 * j + c) * P, k * 1024 + (2 * j + c + 1) * P)
                        dst = L[(n + j) % 2][:, c * T:(c + 1) * T]
                        mm(dst, wh[:, s % 2, w], cqh[:, k, :], start=k == 0 and c == 0, stop=False, skip_group_check=True)
                        mm(dst, wh[:, s % 2, w], cql[:, k, :], start=False, stop=False, skip_group_check=True)
                        ins = mm(dst, wl[:, s % 2, w], cqh[:, k, :], start=False, stop=k == 1, skip_group_check=True)
                ins.then_inc(S("uq_ps"), 1)
            s, n = SLAB0["ukv"], ACC0["ukv"]
            lo_ready(pe, s, 0, 1)
            for j in range(4):
                open_acc(n + j)
                for c in range(2):
                    w = slice((2 * j + c) * P, (2 * j + c + 1) * P)
                    dst = L[(n + j) % 2][:, c * T:(c + 1) * T]
                    mm(dst, wh[:, s % 2, w], cqh[:, 2, :], start=c == 0, stop=False, skip_group_check=True)
                    mm(dst, wh[:, s % 2, w], cql[:, 2, :], start=False, stop=False, skip_group_check=True)
                    ins = mm(dst, wl[:, s % 2, w], cqh[:, 2, :], start=False, stop=True, skip_group_check=True)
                ins.then_inc(S("uk_ps"), 1)
            vh = wh[:, s % 2, 0:1024].rearrange("p (h c) -> p h c", h=8)[:, :, 64:128]
            vl = wl[:, s % 2, 0:1024].rearrange("p (h c) -> p h c", h=8)[:, :, 64:128]
            for b in range(TB):
                open_acc(n + 4 + b)
                t = slice(b * P, (b + 1) * P)
                dst = L[(n + 4 + b) % 2][:, :]
                mm(dst, cqh[:, 2, t], vh, start=True, stop=False)
                mm(dst, cql[:, 2, t], vh, start=False, stop=False)
                ins = mm(dst, cqh[:, 2, t], vl, start=False, stop=True)
                ins.then_inc(S("w_used"), 2)
            head_sums("mq", sq, 8, Q[1], 0, True, rows=96)
            head_sums("mk", sq, 8, Q[1], T, False, rows=96)
            spread("mqf", r8, 0, 8, Q[2:4], lambda j: (pe.wait_ge(*signal("ml_r", 1)),
                                                       j >= 2 and pe.wait_ge(*signal("mqf_use", j - 1))))
            spread("mkf", r8, T, 8, Q[4:6], lambda j: j >= 2 and pe.wait_ge(*signal("mkf_use", j - 1)))
            pe.wait_ge(*signal("ml_k", 1))
            in_turn(4, *attention("ml", [1, 2] * 2,
                      lambda u, h: (qh[0:96, 4 * (u // 2) + h, (u % 2) * P:(u % 2 + 1) * P],
                                    kh[0:96, 4 * (u // 2) + h, 0:(u % 2 + 1) * P]),
                      prob2, probT2,
                      lambda u, b, h: vm[:, b, (4 * (u // 2) + h) * 64:(4 * (u // 2) + h + 1) * 64],
                      [(64 * (h % 2), 64 * (h % 2) + 64, (h // 2) * P, [h]) for h in range(4)]))
            pe.wait_ge(*signal("go_lo", 2))
            pe.wait_ge(*signal("lo_lo", 2))
            two("wo2", oh, ol)

            def mem_rows(k):
                if k == 4:
                    pe.wait_ge(*signal("mem_in", 16))
                    transpose_in(memraw, "mem_ps", Q[2:6])
            opening("xq", "n6", ah, al, extra=mem_rows)
            pe.wait_ge(*signal("n6_rs", 1))
            opening("xk", "n7", mh, ml)
            two("xv", mh, ml, tokens=True)
            head_sums("xx", sq, 8, Q[1], 0, True)
            spread("xf", rx8, 0, 8, Q[2:4], lambda j: (pe.wait_ge(*signal("xx_r", 1)),
                                                       j >= 2 and pe.wait_ge(*signal("xf_use", j - 1))))
            pe.wait_ge(*signal("xf_use", 4))
            in_turn(2, *attention("xa", [2, 2],
                      lambda u, h: (xq[:, h, u * P:(u + 1) * P], xq[:, 4 + h, :]),
                      prob3, probT3, lambda u, b, h: xv[:, b, h * P:(h + 1) * P],
                      [(0, P, h * P, [h]) for h in range(4)]))
            pe.wait_ge(*signal("xo_lo", 2))
            two("xo", mh, ml, nk=4)
            feed_forward("f3u", "f3d", "n8")
            for b in range(TB):
                for g in range(2):
                    if b == 0:
                        acc_freed(pe, ACC0["f3d"] + 2 * g)
                        acc_freed(pe, ACC0["f3d"] + 2 * g + 1)
                    for c in range(4):
                        ins = nc.tensor.transpose(Q[2 * b + g][:, c * P:(c + 1) * P],
                                                  xT[:, 4 * g + c, b * P:(b + 1) * P], ident)
                    ins.then_inc(S("res_ps"), 1)

        @block.scalar
        def _(act):
            A_ = nc.scalar.activation

            def norm_parts(st, g, ready, src=xT, xh=ah):
                for j in range(4):
                    ready(act, j)
                    for c in (2 * j, 2 * j + 1):
                        ins = A_(xh[:, c, :], src[:, c, :], ACT.Copy, scale=col(g + c))
                    ins.then_inc(S(st + "_hi"), 1)
                    ins = A_(sq[:, j, :], pairs(src, j), ACT.Square, scale=1.0 / 32)
                    if st == "n5":
                        for c in (2 * j, 2 * j + 1):
                            ins = A_(xn[:, c, :], src[:, c, :], ACT.Square, scale=col(V_FIN32 + c))
                    ins.then_inc(S(st + "_sq"), 1)

            def norm_root(st):
                if st == "n5":
                    act.wait_ge(*signal("n5_v", 1))
                    A_(root[:, 0:4], vv[:, 0:4], ACT.Sqrt).then_inc(S(st + "_sd"), 1)
                else:
                    act.wait_ge(*signal(st + "_ss", 1))
                    A_(root[:, 0:2], Q[0][:, T:T + 2], ACT.Sqrt, bias=eps).then_inc(S(st + "_sd"), 1)

            def from_accs(name):
                n = ACC0[name]
                return lambda e, j: acc_freed(e, n + j)

            def stage_loop(name, nslabs, evac, st=None):
                s, n = SLAB0[name], ACC0[name]

                def body(i, last):
                    for r in range(2):
                        if last and r == 1:
                            split_hi(act, s + 2 * i + 2)
                        else:
                            split_hi(act, s + r + 1, i)
                        if st is not None and isinstance(i, int) and i + r == 0:
                            norm_root(st)
                        if evac is not None:
                            slab_used(act, s + r, i)
                            evac(i, r)
                looped(act, nslabs // 2, body, peel=st is not None and nslabs > 2)

            def feed_forward(up, down, st, conv=False, then=None):
                s, n = SLAB0[up], ACC0[up]

                def body(i, last):
                    if last:
                        split_hi(act, s + 2 * i + 2)
                    else:
                        split_hi(act, s + 2, i)
                    if conv:
                        act.wait_ge(*signal(up + "_cv", 6 * i + 6))
                        A_(sil[:, :], gcv[:, :], ACT.Silu).then_inc(S(up + "_si"), 1)
                    else:
                        acc_freed(act, n, i)
                        A_(sil[:, :], sil[:, :], ACT.Silu).then_inc(S(up + "_si"), 1)
                    if last:
                        split_hi(act, s + 2 * i + 3)
                    else:
                        split_hi(act, s + 3, i)
                    acc_freed(act, n + 1, i)
                    A_(rpair(hh, i), hid[:, :], ACT.Copy).then_inc(S(up + "_hh"), 1)
                    if then is not None and isinstance(i, int) and i == 0:
                        then()
                split_hi(act, s + 1)
                norm_root(st)
                looped(act, FP, body, peel=then is not None)
                s = SLAB0[down]
                for q in range(4):
                    if q > 0:
                        split_hi(act, s + 2 * q + 1)
                    split_hi(act, s + 2 * q + 2)

            def attention(st, units, prob, probT, sinks=False):
                def exps(u):
                    for h in range(4):
                        act.wait_ge(*signal(st + "_mx", 4 * u + h + 1))
                        w = units[u] * P
                        A_(prob[:, u % 2, h, 0:w], prob[:, u % 2, h, 0:w], ACT.Exp, bias=rmx[:, u % 2, h:h + 1],
                           scale=-1.0, accum_out=rsm[:, u % 2, h:h + 1]).then_inc(S(st + "_ex"), 1)
                    if sinks:
                        act.wait_ge(*signal(st + "_sk", u + 1))
                        A_(rs2[:, u % 2, :], rs2[:, u % 2, :], ACT.Exp).then_inc(S(st + "_se"), 1)

                def transposed(u):
                    act.wait_ge(*signal(st + "_tp", u + 1))
                    if u >= 1:
                        act.wait_ge(*signal(st + "_pv", u))
                    for b in range(units[u]):
                        ins = A_(probT[:, b, :], Q[2 + b][:, :], ACT.Copy)
                    ins.then_inc(S(st + "_pt"), 1)
                return exps, transposed

            def in_turn(units, exps, transposed):
                exps(0)
                for u in range(units):
                    if u + 1 < units:
                        exps(u + 1)
                    transposed(u)

            def x_ready(e, j):
                e.wait_ge(*signal("x_ok", j + 1))

            act.dma_start(g1raw[:, :], A["ffn1_norm"][0].rearrange("(c p) -> c p", p=P)).then_inc(S("g1_in"), 16)
            split_hi(act, 0)
            act.wait_ge(*signal("g1_ok", 1))
            norm_parts("n1", V_FFN1, x_ready)
            win = A["w_in"][0].rearrange("(k p) c -> p k c", p=P)
            win2 = A["w_in_2"][0].rearrange("(k p) c -> p k c", p=P)

            def small(dst, src):
                act.dma_start(dst, src).then_inc(S("small_in"), 16)

            small(bav[:, :], A["b_in"][:, I_AV:I_AV + 256].broadcast_to([P, 256]))
            small(bmv[:, :], A["b_in"][:, I_MV:I_MV + 1024].broadcast_to([P, 1024]))
            small(nsink[:, 0:16], A["attn_sinks"].broadcast_to([P, 16]))
            small(posi[:, :], A["positions_2"].broadcast_to([P, T]))
            small(wif[:, :, :], win[:, :, I_MI:I_MI + 16])
            small(walr[:, :, :], win2[:, :, J_ALR:J_ALR + 16])
            small(w2g[:, :], A["gla_gate_w2_2"][0])
            small(bif[:, 0:1], A["b_in"][0, I_MI:I_MI + 8].rearrange("(p a) -> p a", a=1))
            small(bif[:, 1:2], A["b_in"][0, I_MI + 8:I_MI + 16].rearrange("(p a) -> p a", a=1))
            act.wait_ge(*signal("consts", 16))

            def sines():
                act.wait_ge(*signal("angles", 1))
                A_(rope_c[64:P, :], rope_c[64:P, :], ACT.Sin)
                A_(rope_s[64:P, :], rope_s[64:P, :], ACT.Sin).then_inc(S("sines"), 1)
            feed_forward("f1u", "f1d", "n1", then=sines)
            norm_parts("n2", V_MIX, from_accs("f1d"))
            stage_loop("wq", 4, None, st="n2")
            stage_loop("wkv", 2, None)

            def sigmoid(m):
                name, v, dst, k = ("wmo", V_BMO, sigo, m - 8) if m < 12 else ("wg", V_BG, gate, m - 12)
                acc_freed(act, ACC0[name] + k)
                for half in range(2):
                    c = 2 * k + half
                    ins = A_(dst[:, c, :], stmp[:, k % 2, half * T:(half + 1) * T], ACT.Sigmoid, bias=col(v + c))
                ins.then_inc(S("sig"), 1)

            exps, transposed = attention("at", [1, 2] * 4, prob1, probT1, sinks=True)
            s_mix = SLAB0["wmqk"]
            for m in range(MIX):
                u, odd = divmod(m, 2)
                split_hi(act, s_mix + m + 1)
                if not odd and u < 8:
                    exps(u)
                if m >= 9:
                    sigmoid(m - 1)
                if odd and u < 8:
                    transposed(u)
                if m == 1:
                    act.wait_ge(*signal("if_T", 1))
                    act.wait_ge(*signal("if_b", 1))
                    A_(ti[:, 0:T], Q[4][0:8, 0:T], ACT.Tanh, bias=bif[:, 2:3], scale=1.0 / 15)
                    A_(ti[:, T:512], Q[4][0:8, T:512], ACT.Tanh, bias=bif[:, 3:4], scale=1.0 / 15).then_inc(S("if_use"), 1)
                    act.wait_ge(*signal("if_use", 1))
                    A_(lse[:, :], ti[:, T:512], ACT.Exp, scale=-15.0).then_inc(S("m_e"), 1)
                    act.wait_ge(*signal("m_e", 1))
                    A_(lse[:, :], lse[:, :], ACT.Ln, bias=1.0).then_inc(S("m_e"), 1)
                elif m == 17:
                    act.wait_ge(*signal("conv", 32))
                    for j in range(4):
                        ins = A_(qk[:, 2 * j:2 * j + 2, :], qk[:, 2 * j:2 * j + 2, :], ACT.Silu)
                    ins.then_inc(S("m_qk"), 1)
                elif m == 18:
                    act.wait_ge(*signal("m_gm", 1))
                    A_(en[:, :], gm[:, :], ACT.Exp).then_inc(S("m_en"), 1)

            def m_weights(j):
                act.wait_ge(*signal("m_D", 4 * j + 4))
                v = wm[:, 2 * j:2 * j + 2, :]
                A_(v, v, ACT.Exp, scale=-1.0).then_inc(S("m_w"), 1)

            m_weights(0)
            m_weights(1)
            slab_used(act, s_mix + MIX - 1)
            for j in range(4):
                act.wait_ge(*signal("at_yo", 2 * j + 2))
                A_(pairs(ah, j), pairs(aq, j), ACT.Copy).then_inc(S("at_hi"), 1)
            m_weights(2)
            m_weights(3)
            sigmoid(MIX - 1)
            s = SLAB0["pa"]
            split_hi(act, s + 1)
            split_hi(act, s + 2)
            for j in range(4):
                act.wait_ge(*signal("m_nu", j + 1))
                A_(sq[:, j, :], pairs(xn, j), ACT.Square).then_inc(S("m_hs"), 1)
            split_hi(act, s + 3)
            act.wait_ge(*signal("m_v", 1))
            A_(gm[:, :], gm[:, :], ACT.Sqrt, bias=eps[0:8, :]).then_inc(S("m_sd"), 1)
            split_hi(act, s + 4)
            for j in range(4):
                act.wait_ge(*signal("mo_y", j + 1))
                A_(pairs(bh, j), pairs(xn, j), ACT.Copy).then_inc(S("mo_hi"), 1)
            s = SLAB0["pm"]
            for k in range(4):
                split_hi(act, s + k + 1)
                act.wait_ge(*signal("mg", k + 1))
                A_(pairs(ch, k), mgs[:, :], ACT.Copy).then_inc(S("mg_hi"), 1)
            stage_loop("wo", 4, None)
            norm_parts("n3", V_FFN2, from_accs("wo"))
            feed_forward("f2u", "f2d", "n3")
            norm_parts("n5", V_MIX2, from_accs("f2d"))

            s, n = SLAB0["w2"], ACC0["w2"]
            for k in range(8):
                split_hi(act, s + k + 1)
                if k == 0:
                    norm_root("n5")
                elif k in (4, 5):
                    acc_freed(act, n + k)
                    A_(pairs(sog, k - 4), stmp[:, k % 2, :], ACT.Silu).then_inc(S("sog"), 1)
                elif k == 6:
                    act.wait_ge(*signal("gl_zr", 1))
                    A_(lg[:, :], zg[:, :], ACT.Abs).then_inc(S("gl_l"), 1)
                    act.wait_ge(*signal("gl_l", 1))
                    A_(lg[:, :], lg[:, :], ACT.Exp, scale=-1.0).then_inc(S("gl_l"), 1)
                    act.wait_ge(*signal("gl_l", 2))
                    A_(lg[:, :], lg[:, :], ACT.Ln, bias=1.0).then_inc(S("gl_l"), 1)
            act.wait_ge(*signal("gl_cum", 2))
            A_(eg[:, 0, :], cum[:, :], ACT.Exp, scale=1.0 / 16).then_inc(S("gl_e"), 1)
            A_(eg[:, 1, :], cum[:, :], ACT.Exp, scale=-1.0 / 16).then_inc(S("gl_e"), 1)
            ends = cum[:, :].rearrange("p (n c) -> p n c", n=8)[:, :, 63]
            A_(dec[:, :], ends, ACT.Exp, scale=1.0 / 16)
            act.wait_ge(*signal("gl_d", 1))
            A_(eg[:, 2, :], zg[:, :], ACT.Exp, scale=-1.0 / 16).then_inc(S("gl_e"), 1)
            act.wait_ge(*signal("gl_keT", 1))
            A_(ketok[:, :, :].rearrange("p b c -> p (b c)"), Q[0][:, :], ACT.Copy).then_inc(S("gl_ketok"), 1)
            for j in range(2):
                act.wait_ge(*signal("gl_or", 1))
                A_(sq[:, j, :], pairs(xn, j), ACT.Square).then_inc(S("gl_hs"), 1)
            acc_freed(act, n + 6)
            A_(sq[:, 2, :], pairs(cq, 0), ACT.Square).then_inc(S("la_sq"), 1)
            acc_freed(act, n + 7)
            A_(sq[:, 3, 0:T], ckv[:, :], ACT.Square).then_inc(S("la_sq"), 1)
            act.wait_ge(*signal("gl_ss", 1))
            A_(st8[:, 0:T], Q[0][0:8, 0:T], ACT.Sqrt, bias=eps[0:8, :], scale=1.0 / P).then_inc(S("gl_sd"), 1)
            act.wait_ge(*signal("la_sum", 1))
            A_(std[:, 0:T], Q[1][:, 0:T], ACT.Sqrt, bias=eps, scale=1.0 / 256)
            A_(std[:, T:512], Q[1][:, T:512], ACT.Sqrt, bias=eps, scale=1.0 / P).then_inc(S("la_sd"), 1)
            for j in range(2):
                act.wait_ge(*signal("go_y", j + 1))
                A_(pairs(oh, j), pairs(xn, j), ACT.Copy).then_inc(S("go_hi"), 1)
            act.wait_ge(*signal("la_n", 3))
            A_(cqh[:, 0:2, :], cq[:, :, :], ACT.Copy).then_inc(S("la_hi"), 1)
            A_(cqh[:, 2, :], ckv[:, :], ACT.Copy).then_inc(S("la_hi"), 1)
            split_hi(act, SLAB0["ukv"])
            for part, dst in (("mq", qh), ("mk", kh)):
                n = ACC0["uq"] if part == "mq" else ACC0["ukv"]
                if part == "mk":
                    act.wait_ge(*signal("mq_ss", 1))
                for j in range(4):
                    acc_freed(act, n + j)
                    if part == "mk":
                        act.wait_ge(*signal("kpe_in", 1))
                    A_(sq[0:96, j, :], dst[0:96, 2 * j:2 * j + 2, :].rearrange("p c t -> p (c t)"), ACT.Square)\
                        .then_inc(S(part + "_hs"), 1)
            split_hi(act, SLAB0["wo2"])
            act.wait_ge(*signal("mk_ss", 1))
            A_(st8[:, :], Q[1][0:8, :], ACT.Sqrt, bias=eps[0:8, :], scale=1.0 / 96).then_inc(S("ml_sd"), 1)
            in_turn(4, *attention("ml", [1, 2] * 2, prob2, probT2))
            for j in range(2):
                act.wait_ge(*signal("ml_yo", 2 * j + 2))
                A_(pairs(oh, 2 + j), pairs(xn, 2 + j), ACT.Copy).then_inc(S("lo_hi"), 1)
            stage_loop("wo2", 4, None)

            norm_parts("n6", V_XA, from_accs("wo2"))
            stage_loop("xq", 2, None, st="n6")
            norm_parts("n7", V_MEM, lambda e, j: e.wait_ge(*signal("mem_ok", j + 1)), src=mT, xh=mh)
            stage_loop("xk", 2, None, st="n7")
            stage_loop("xv", 2, None)
            for j in range(4):
                acc_freed(act, ACC0["xq"] + j)
                A_(sq[:, j, :], pairs(xq, j), ACT.Square).then_inc(S("xx_hs"), 1)
            act.wait_ge(*signal("xx_ss", 1))
            A_(sx8[:, 0:T], Q[1][0:8, 0:T], ACT.Sqrt, bias=eps[0:8, :], scale=1.0 / P).then_inc(S("xx_sd"), 1)
            in_turn(2, *attention("xa", [2, 2], prob3, probT3))
            for j in range(2):
                act.wait_ge(*signal("xa_yo", 2))
                A_(pairs(mh, j), pairs(xn, j), ACT.Copy).then_inc(S("xo_hi"), 1)
            stage_loop("xo", 4, None)
            norm_parts("n8", V_FFN3, from_accs("xo"))
            feed_forward("f3u", "f3d", "n8", conv=True)
            for k in range(2):
                act.wait_ge(*signal("res_ps", 2 * k + 1))
                A_(res[:, k, 0:512], Q[2 * k][:, :], ACT.Copy).then_inc(S("resa"), 1)

        @block.vector
        def _(dve):
            V = nc.vector
            steps = [0]

            def link(ins, n=1):
                ins.then_inc(S("dve_step"), 1)
                steps[0] += 1
                dve.wait_ge(*signal("dve_step", steps[0]))

            def norm_lows(st, g, src=xT, xh=ah, xl=al):
                for j in range(4):
                    dve.wait_ge(*signal(st + "_hi", j + 1))
                    for c in (2 * j, 2 * j + 1):
                        ins = V.scalar_tensor_tensor(xl[:, c, :], src[:, c, :], col(g + c), f(xh[:, c, :]), MUL, SUB)
                    ins.then_inc(S(st + "_lo"), 1)

            def norm_factor(st):
                n = 2
                if st == "n5":
                    n = 4
                    dve.wait_ge(*signal("n5_ss", 1))
                    link(V.tensor_scalar(vv[:, 2:4], Q[0][:, T:T + 2], EPS, None, ADD))
                    V.scalar_tensor_tensor(vv[:, 0:2], vv[:, 2:4], EPS, Q[0][:, T + 2:T + 4], MUL, ADD).then_inc(S("n5_v"), 1)
                dve.wait_ge(*signal(st + "_sd", 1))
                V.reciprocal(rcol[:, 0:n], root[:, 0:n]).then_inc(S(st + "_rc"), 1)
                dve.wait_ge(*signal(st + "_rc", 1))
                dve.wait_ge(*signal(st + "_sp", 1))
                if st == "n5":
                    V.tensor_copy(std[:, 0:T], Q[1][:, 0:T])
                V.tensor_copy(rstd[:, 0:T], Q[0][:, 0:T]).then_inc(S(st + "_rs"), 1)
                dve.wait_ge(*signal(st + "_rs", 1))

            def lows(st, src, xh, xl, n, j0=0):
                for j in range(n):
                    dve.wait_ge(*signal(st + "_hi", j + 1))
                    V.tensor_tensor(pairs(xl, j0 + j), pairs(src, j0 + j), f(pairs(xh, j0 + j)), SUB)\
                        .then_inc(S(st + "_lo"), 1)

            def stage_loop(name, nslabs, evac, st=None):
                s, n = SLAB0[name], ACC0[name]

                def body(i, last):
                    for r in range(2):
                        if last and r == 1:
                            split_lo(dve, s + 2 * i + 2)
                        else:
                            split_lo(dve, s + r + 1, i)
                        if st is not None and isinstance(i, int) and i + r == 0:
                            norm_factor(st)
                        evac(i, r)
                looped(dve, nslabs // 2, body, peel=st is not None and nslabs > 2)

            def feed_forward(up, down, st, conv=False, then=None):
                s, n = SLAB0[up], ACC0[up]

                def body(i, last):
                    slab_used(dve, s, i)
                    gdst = gpad[:, :, 2:T + 2] if conv else two_t(sil[:, :])
                    V.tensor_tensor(gdst, two_t(L[n % 2][:, :]), factor, MUL).then_inc(free_sem(n), 1)
                    if conv:
                        for j in range(3):
                            for m in range(2):
                                w = vec[:, bass.ds(V_FCW + j * FC + m + i * 2, 1)]
                                o, x = gcv[:, m * T:(m + 1) * T], gpad[:, m, j:j + T]
                                if j == 0:
                                    if m == 0:
                                        acc_freed(dve, n, i)
                                    ins = V.tensor_scalar(o, x, w, vec[:, bass.ds(V_FCB + m + i * 2, 1)], MUL, ADD)
                                else:
                                    dve.wait_ge(*signal(up + "_cv", 6 * i + 2 * j + m - 1))
                                    ins = V.scalar_tensor_tensor(o, x, w, o, MUL, ADD)
                                ins.then_inc(S(up + "_cv"), 1)
                    if last:
                        split_lo(dve, s + 2 * i + 2)
                    else:
                        split_lo(dve, s + 2, i)
                    slab_used(dve, s + 1, i)
                    dve.wait_ge(*signal(up + "_sr", i + 1))
                    V.tensor_tensor(hid[:, :], L[(n + 1) % 2][:, :], sil[:, :], MUL).then_inc(free_sem(n + 1), 1)
                    if last:
                        split_lo(dve, s + 2 * i + 3)
                    else:
                        split_lo(dve, s + 3, i)
                    dve.wait_ge(*signal(up + "_hh", i + 1))
                    V.tensor_tensor(rpair(hl, i), hid[:, :], f(rpair(hh, i)), SUB).then_inc(S(up + "_hl"), 1)
                    if then is not None and isinstance(i, int) and i == 0:
                        then()
                split_lo(dve, s + 1)
                norm_factor(st)
                looped(dve, FP, body, peel=then is not None)
                s, n = SLAB0[down], ACC0[down]
                for q in range(4):
                    if q > 0:
                        split_lo(dve, s + 2 * q + 1)
                    split_lo(dve, s + 2 * q + 2)
                    slab_used(dve, s + 2 * q + 1)
                    V.scalar_tensor_tensor(pairs(xT, q), L[(n + q) % 2][:, :], 1.0 if conv else 0.5, pairs(xT, q),
                                           MUL, ADD).then_inc(free_sem(n + q), 1)

            def add_to_x(name, s, n):
                def evac(i, r):
                    slab_used(dve, s + r, i)
                    V.tensor_tensor(rpair(xT, i * 2 + r), L[(n + r) % 2][:, :], rpair(xT, i * 2 + r), ADD)\
                        .then_inc(free_sem(n + r), 1)
                return evac

            def attention(st, units, prob, scale, mask, yout, sink=None):
                def maxima(u):
                    dve.wait_ge(*signal(st + "_sc", u + 1))
                    if u >= 2:
                        dve.wait_ge(*signal(st + "_tp", u - 1))
                    w = units[u] * P
                    for h in range(4):
                        V.tensor_tensor_reduce(out=prob[:, u % 2, h, 0:w], in0=Q[h % 2][:, (h // 2) * 256:(h // 2) * 256 + w],
                                               in1=mask(units[u]), scale=-scale, scalar=sink(u, h) if sink else 3.0e38,
                                               op0=ADD, op1=MIN, accum_out=rmx[:, u % 2, h:h + 1]).then_inc(S(st + "_mx"), 1)
                    if sink:
                        dve.wait_ge(*signal(st + "_mx", 4 * u + 4))
                        g = u // 2
                        V.tensor_tensor(rs2[:, u % 2, :], rmx[:, u % 2, :], nsink[:, 4 * g:4 * g + 4], SUB)\
                            .then_inc(S(st + "_sk"), 1)

                def divide(u):
                    w = units[u] * P
                    dve.wait_ge(*signal(st + "_ex", 4 * u + 4))
                    if sink:
                        dve.wait_ge(*signal(st + "_se", u + 1))
                        link(V.tensor_tensor(rsm[:, u % 2, :], rsm[:, u % 2, :], rs2[:, u % 2, :], ADD))
                    link(V.reciprocal(rin[:, u % 2, :], rsm[:, u % 2, :]))
                    for h in range(4):
                        V.tensor_scalar(prob[:, u % 2, h, 0:w], prob[:, u % 2, h, 0:w], rin[:, u % 2, h:h + 1], None, MUL)\
                            .then_inc(S(st + "_pn"), 1)

                def leave(u):
                    dve.wait_ge(*signal(st + "_pv", u + 1))
                    yout(u, Q[4 + u % 2]).then_inc(S(st + "_yo"), 1)
                return maxima, divide, leave

            def in_turn(units, maxima, divide, leave):
                maxima(0)
                for u in range(units):
                    if u + 1 < units:
                        maxima(u + 1)
                    divide(u)
                    if u >= 1:
                        leave(u - 1)
                leave(units - 1)

            dve.wait_ge(*signal("g1_ps", 1))
            V.tensor_copy(vec[:, 0:8], Q[4][:, 0:8]).then_inc(S("g1_ok"), 1)
            for j in range(4):
                dve.wait_ge(*signal("x_ps", j + 1))
                V.tensor_copy(pairs(xT, j), Q[j][:, :]).then_inc(S("x_ok"), 1)
            dve.wait_ge(*signal("g1_ok", 1))
            dve.wait_ge(*signal("x_ok", 4))
            split_lo(dve, 0)
            norm_lows("n1", V_FFN1)

            def narrow_inputs():
                dve.wait_ge(*signal("vec_ps", 1))
                V.tensor_copy(vec[:, 8:VEC0], Q[4][:, 8:VEC0])
                link(V.tensor_copy(vec[:, P:P + VEC1], Q[4][:, P:P + VEC1]))
                V.tensor_scalar(vec[:, V_FIN32:V_FIN32 + 8], vec[:, V_FINAL:V_FINAL + 8], 1.0 / 32, None, MUL)
                link(V.tensor_tensor(vec[:, V_MIX2:V_MIX2 + 8], vec[:, V_MIX2:V_MIX2 + 8], vec[:, V_FINAL:V_FINAL + 8], MUL))
                dve.wait_ge(*signal("small_in", 16 * SMALL_LOADS))
                for w, g in ((wif, V_MIX), (walr, V_MIX2)):
                    gc = vec[:, g:g + 8].rearrange("p (c a) -> p c a", a=1).broadcast_to([P, 8, 16])
                    V.tensor_tensor(w[:, :, :], w[:, :, :], gc, MUL).then_inc(S("narrow"), 1)
                V.tensor_scalar(bif[:, 2:4], bif[:, 0:2], 1.0 / 15, None, MUL).then_inc(S("if_b"), 1)
                V.tensor_scalar(nsink[:, 0:16], nsink[:, 0:16], -1.0, None, MUL)
                R = slice(64, P)
                TWO_PI = 2 * np.pi
                c1 = 6.28125
                c2 = float(np.float32(np.round((TWO_PI - c1) * 2 ** 21) / 2 ** 21))
                c3 = float(np.float32(TWO_PI - c1 - c2))
                MAGIC = 12582912.0
                link(V.tensor_copy(ang[R, :], posi[R, :]))
                link(V.tensor_scalar(ang[R, :], ang[R, :], cst[R, C_INV:C_INV + 1], None, MUL))
                link(V.tensor_scalar(turn[R, :], ang[R, :], float(1 / TWO_PI), MAGIC, MUL, ADD))
                link(V.tensor_scalar(turn[R, :], turn[R, :], MAGIC, None, SUB))
                for c in (c1, c2, c3):
                    link(V.scalar_tensor_tensor(ang[R, :], turn[R, :], -c, ang[R, :], MUL, ADD))
                link(V.tensor_scalar(quarter[R, :], ang[R, :], float(np.pi / 2), None, ADD))
                link(V.tensor_scalar(tmpr[R, :], quarter[R, :], float(np.pi), TWO_PI, ALU.is_gt, MUL))
                link(V.tensor_tensor(quarter[R, :], quarter[R, :], tmpr[R, :], SUB))
                BOUND = 3.1415925
                V.tensor_scalar(rope_c[R, :], quarter[R, :], BOUND, -BOUND, MIN, MAX)
                V.tensor_scalar(rope_s[R, :], ang[R, :], BOUND, -BOUND, MIN, MAX).then_inc(S("angles"), 1)

            feed_forward("f1u", "f1d", "n1", then=narrow_inputs)
            norm_lows("n2", V_MIX)

            def scaled_out(name, k, dst):
                slab_used(dve, SLAB0[name] + k)
                V.tensor_tensor(dst, two_t(L[(ACC0[name] + k) % 2][:, :]), factor, MUL).then_inc(free_sem(ACC0[name] + k), 1)

            def with_bias(name, dst, v):
                def evac(i, r):
                    k = 2 * i + r
                    scaled_out(name, k, dst(k))
                    acc_freed(dve, ACC0[name] + k)
                    for m in range(2):
                        ins = V.tensor_scalar(dst(k)[:, m, :], dst(k)[:, m, :], col(v + 2 * k + m), None, ADD)
                    ins.then_inc(S("biased"), 1)
                return evac

            def straight(name, nslabs, evac, st=None):
                for k in range(nslabs):
                    split_lo(dve, SLAB0[name] + k + 1)
                    if k == 0 and st is not None:
                        norm_factor(st)
                    evac(k // 2, k % 2)

            straight("wq", 4, with_bias("wq", lambda k: aq[:, 2 * k:2 * k + 2, :], V_BQ), st="n2")
            s, n = SLAB0["wkv"], ACC0["wkv"]
            split_lo(dve, s + 1)
            scaled_out("wkv", 0, two_t(stmp[:, 0, :]))
            acc_freed(dve, n)
            for c in range(2):
                for e in range(2):
                    for to in range(2):
                        ins = V.tensor_scalar(akd[64 * to:64 * to + 64, 2 * c + e, :],
                                              stmp[64 * e:64 * e + 64, 0, c * T:(c + 1) * T],
                                              col(V_BK + c, 64 * e, 64 * e + 64), None, ADD)
            ins.then_inc(S("keys"), 1)
            split_lo(dve, s + 2)
            slab_used(dve, s + 1)
            for b in range(TB):
                ins = V.scalar_tensor_tensor(av[:, b, :], L[(n + 1) % 2][:, b * 256:(b + 1) * 256], rcol[:, b:b + 1],
                                             bav[:, :], MUL, ADD)
            ins.then_inc(free_sem(n + 1), 1)

            def y_first(u, bank):
                g, blk = u // 2, u % 2
                return V.tensor_copy(aq[:, 2 * g:2 * g + 2, blk * P:(blk + 1) * P],
                                     bank[:, 0:256].rearrange("p (c q) -> p c q", c=2))

            maxima, divide, leave = attention(
                "at", [1, 2] * 4, prob1, 0.125,
                lambda b: cst[:, C_OWN:C_OWN + P] if b == 1 else cst[:, C_PREV:C_PREV + 256], y_first,
                sink=lambda u, h: nsink[:, 4 * (u // 2) + h:4 * (u // 2) + h + 1])

            conv_in = with_bias("wmqk", lambda k: pad[:, 2 * k:2 * k + 2, 3:T + 3], V_BMQK)

            def values_out(k):
                slab_used(dve, SLAB0["wmv"] + k)
                for b in range(TB):
                    ins = V.scalar_tensor_tensor(mv[:, b, k * 256:(k + 1) * 256],
                                                 L[(ACC0["wmv"] + k) % 2][:, b * 256:(b + 1) * 256],
                                                 rcol[:, b:b + 1], bmv[:, k * 256:(k + 1) * 256], MUL, ADD)
                ins.then_inc(free_sem(ACC0["wmv"] + k), 1)

            def for_sigmoid(m):
                name, k = ("wmo", m - 8) if m < 12 else ("wg", m - 12)
                if m >= 10:
                    dve.wait_ge(*signal("sig", m - 9))
                scaled_out(name, k, two_t(stmp[:, k % 2, :]))

            def conv(c):
                part = std[:, (c % 2) * T:(c % 2 + 1) * T]
                for j in range(4):
                    x, w = pad[:, c, j:j + T], col(V_MCONV + j * 8 + c)
                    if j == 0:
                        ins = V.tensor_scalar(part, x, w, None, MUL)
                    else:
                        dve.wait_ge(*signal("conv", 4 * c + j))
                        ins = V.scalar_tensor_tensor(pad[:, c, 3:T + 3] if j == 3 else part, x, w, part, MUL, ADD)
                    ins.then_inc(S("conv"), 1)

            def m_gates():
                dve.wait_ge(*signal("m_e", 2))
                link(V.tensor_tensor_scan(Gc[:, :], cst[0:8, C_ONE:C_ONE + 1].broadcast_to([8, T]), lse[:, :], 0.0, MUL, ADD))
                V.scalar_tensor_tensor(ai[:, :], ti[:, 0:T], 15.0, Gc[:, :], MUL, ADD).then_inc(S("m_a"), 1)
                dve.wait_ge(*signal("m_a", 1))
                V.tensor_tensor_scan(Mx[:, :], cst[0:8, C_ONE:C_ONE + 1].broadcast_to([8, T]), ai[:, :], 0.0, MUL, MAX)\
                    .then_inc(S("m_M"), 1)
                dve.wait_ge(*signal("m_M", 1))
                V.tensor_tensor(gm[:, :], Gc[:, :], Mx[:, :], SUB).then_inc(S("m_gm"), 1)

            def m_exponents(heads):
                for h in heads:
                    dve.wait_ge(*signal("mm_sp", h // 2 + 1))
                    for b in range(TB):
                        a = acol[:, b, h:h + 1]
                        V.tensor_scalar(wm[:, h, b * 256:b * 256 + T - b * P], Q[h // 2][:, (h % 2) * T + b * P:(h % 2) * T + T],
                                        a, a, MAX, SUB).then_inc(S("m_D"), 1)

            s_mix = SLAB0["wmqk"]
            for m in range(MIX):
                u, odd = divmod(m, 2)
                if not odd and u < 8:
                    maxima(u)
                if m == 0:
                    dve.wait_ge(*signal("if_ps", 1))
                    for b in range(TB):
                        ins = V.tensor_scalar(gtok[:, b, :], Q[5][:, b * 16:(b + 1) * 16], rcol[:, b:b + 1], None, MUL)
                    ins.then_inc(S("if_tok"), 1)
                split_lo(dve, s_mix + m + 1)
                if not odd and u < 8:
                    divide(u)
                if not odd and 1 <= u <= 8:
                    leave(u - 1)
                if m == 0:
                    dve.wait_ge(*signal("pad0", 1))
                if m < 4:
                    conv_in(m // 2, m % 2)
                elif m < 8:
                    values_out(m - 4)
                else:
                    for_sigmoid(m)
                if m == 3:
                    m_gates()
                    dve.wait_ge(*signal("biased", 8))
                elif 8 <= m < 16:
                    conv(m - 8)
                elif m == 18:
                    dve.wait_ge(*signal("m_acol", 1))
                    V.tensor_copy(acol[:, :, :].rearrange("p b h -> p (b h)"), Q[5][:, 0:16]).then_inc(S("m_acolr"), 1)
                    dve.wait_ge(*signal("m_acolr", 1))
                    m_exponents(range(0, 4))
                elif m == 19:
                    m_exponents(range(4, 8))

            def m_weighted(h):
                dve.wait_ge(*signal("m_qkT", h + 1))
                dve.wait_ge(*signal("m_mask", h // 2 + 1))
                V.scalar_tensor_tensor(wm[:, h, :], Q[h % 4][:, 0:384], 0.125, wm[:, h, :], MUL, MUL)\
                    .then_inc(S("m_S"), 1)

            def attention_out(k):
                slab_used(dve, SLAB0["pa"] + k)
                V.tensor_tensor(pairs(gate, k), L[(ACC0["pa"] + k) % 2][:, :], pairs(gate, k), MUL)\
                    .then_inc(free_sem(ACC0["pa"] + k), 1)

            lows("at", aq, ah, al, 4)
            for h in range(4):
                m_weighted(h)
            dve.wait_ge(*signal("sig", 12))
            split_lo(dve, SLAB0["pa"] + 1)
            attention_out(0)
            for h in range(4, 8):
                m_weighted(h)
            for j in range(4):
                dve.wait_ge(*signal("m_num", 2 * j + 2))
                V.tensor_copy(pairs(xn, j), Q[j][:, :]).then_inc(S("m_nu"), 1)
            split_lo(dve, SLAB0["pa"] + 2)
            dve.wait_ge(*signal("m_num", 8))
            dve.wait_ge(*signal("m_en", 1))
            link(V.scalar_tensor_tensor(rden[:, :], Q[5][0:8, 0:T], -1.0, en[:, :], MUL, MAX))
            link(V.tensor_tensor(rden[:, :], rden[:, :], Q[5][0:8, 0:T], MAX))
            link(V.reciprocal(rden[:, :], rden[:, :]))
            link(V.tensor_tensor(gm[:, :], rden[:, :], rden[:, :], MUL))
            attention_out(1)
            dve.wait_ge(*signal("m_ss", 1))
            V.scalar_tensor_tensor(gm[:, :], Q[4][0:8, 0:T], 1.0 / P, gm[:, :], MUL, MUL).then_inc(S("m_v"), 1)
            split_lo(dve, SLAB0["pa"] + 3)
            dve.wait_ge(*signal("m_sd", 1))
            link(V.reciprocal(en[:, :], gm[:, :]))
            V.tensor_tensor(rden[:, :], rden[:, :], en[:, :], MUL).then_inc(S("m_r"), 1)
            attention_out(2)
            for j in range(4):
                dve.wait_ge(*signal("mf_sp", j + 1))
                link(V.tensor_tensor(pairs(xn, j), Q[j][:, :], pairs(xn, j), MUL))
                for h in (2 * j, 2 * j + 1):
                    ins = V.scalar_tensor_tensor(xn[:, h, :], xn[:, h, :], col(V_HEAD + h), sigo[:, h, :], MUL, MUL)
                ins.then_inc(S("mo_y"), 1)
            split_lo(dve, SLAB0["pm"])
            lows("mo", xn, bh, bl, 4)
            attention_out(3)
            acc_freed(dve, ACC0["pa"] + 2)
            acc_freed(dve, ACC0["pa"] + 3)
            for k in range(4):
                s, n = SLAB0["pm"] + k, ACC0["pm"] + k
                split_lo(dve, s + 1)
                slab_used(dve, s)
                V.tensor_tensor(mgb[:, :], L[n % 2][:, :], pairs(gate, 4 + k), MUL).then_inc(free_sem(n), 1)
                acc_freed(dve, n)
                V.tensor_tensor(mgs[:, :], mgb[:, :], pairs(gate, k), ADD).then_inc(S("mg"), 1)
                dve.wait_ge(*signal("mg_hi", k + 1))
                V.tensor_tensor(pairs(cl, k), mgs[:, :], f(pairs(ch, k)), SUB).then_inc(S("mg_lo"), 1)
            stage_loop("wo", 4, add_to_x("wo", SLAB0["wo"], ACC0["wo"]))
            norm_lows("n3", V_FFN2)
            feed_forward("f2u", "f2d", "n3")
            norm_lows("n5", V_MIX2)

            s, n = SLAB0["w2"], ACC0["w2"]

            def acc(k):
                return L[(n + k) % 2]
            for k in range(8):
                split_lo(dve, s + k + 1)
                if k == 0:
                    norm_factor("n5")
                slab_used(dve, s + k)
                if k == 0:
                    ins = V.scalar_tensor_tensor(gq[:, :, :], two_t(acc(k)[:, :]), 0.125, factor, MUL, MUL)
                elif k == 1:
                    ins = V.tensor_tensor(gk[:, :, :], two_t(acc(k)[:, :]), factor, MUL)
                elif k in (2, 3):
                    for b in range(TB):
                        ins = V.tensor_scalar(gv[:, b, (k - 2) * 256:(k - 1) * 256], acc(k)[:, b * 256:(b + 1) * 256],
                                              rcol[:, b:b + 1], None, MUL)
                elif k in (4, 5):
                    ins = V.tensor_tensor(two_t(stmp[:, k % 2, :]), two_t(acc(k)[:, :]), factor, MUL)
                elif k == 6:
                    ins = V.tensor_tensor(cq[:, :, :], two_t(acc(k)[:, :]), factor, MUL)
                else:
                    V.tensor_tensor(kpe[64:P, :], acc(k)[64:P, T:512], rstd[64:P, 0:T], MUL)
                    ins = V.tensor_tensor(ckv[:, :], acc(k)[:, 0:T], rstd[:, 0:T], MUL)
                ins.then_inc(free_sem(n + k), 1)
                if k == 3:
                    dve.wait_ge(*signal("alr_ps", 1))
                    V.tensor_tensor(alr[0:16, :], Q[2][0:16, 0:T], rstd[0:16, 0:T], MUL).then_inc(S("alr"), 1)
                elif k == 4:
                    for c in range(DC):
                        V.scalar_tensor_tensor(xT[:, c, :], xT[:, c, :], col(V_FINAL + c), std[:, 0:T], MUL, MUL)
                elif k == 5:
                    dve.wait_ge(*signal("gl_z", 1))
                    for c in range(2):
                        ins = V.tensor_scalar(zg[:, c * T:(c + 1) * T], Q[1][:, c * T:(c + 1) * T], col(V_GATEB + c), None, ADD)
                    ins.then_inc(S("gl_zr"), 1)
            dve.wait_ge(*signal("gl_l", 3))
            link(V.scalar_tensor_tensor(zg[:, :], zg[:, :], 0.0, lg[:, :], MIN, SUB))
            for c in range(2):
                V.tensor_tensor_scan(cum[:, c * T:(c + 1) * T], cst[:, C_RESET:C_RESET + T], zg[:, c * T:(c + 1) * T],
                                     0.0, MUL, ADD).then_inc(S("gl_cum"), 1)
            dve.wait_ge(*signal("gl_cum", 2))
            c8 = cum[:, :].rearrange("p (n c) -> p n c", n=8)
            V.tensor_tensor(zg[:, :].rearrange("p (n c) -> p n c", n=8), c8, c8[:, :, 63:64].broadcast_to([P, 8, 64]), SUB)\
                .then_inc(S("gl_d"), 1)
            for k, (o, x) in enumerate(((qd, gq), (ki, gk), (ke, gk))):
                dve.wait_ge(*signal("gl_e", k + 1))
                ins = V.tensor_tensor(pairs(o, 0), pairs(x, 0), eg[:, k, :], MUL)
            ins.then_inc(S("gl_ke"), 1)
            dve.wait_ge(*signal("gl_att", 1))
            dve.wait_ge(*signal("att0", 1))
            gmask = cst[:, C_GLA:C_GLA + P].bitcast(i32).rearrange("p (a c) -> p a c", a=1).broadcast_to([P, 4, P])
            for e in range(2):
                V.copy_predicated(att[:, e, :].rearrange("p (a c) -> p a c", a=4), gmask,
                                  Q[2 + e][:, :].rearrange("p (a c) -> p a c", a=4)).then_inc(S("gl_am"), 1)
            for k in range(3):
                dve.wait_ge(*signal("gl_dS", k + 1))
                bank = (Q[4], Q[5], Q[1])[k]
                if k >= 1:
                    dve.wait_ge(*signal("gl_S", k))
                for e in range(2):
                    p0 = 64 * e
                    for c in range(2):
                        o = stt_[p0:p0 + 64, k, c, :]
                        x = bank[p0:p0 + 64, c * 256 + e * P:c * 256 + (e + 1) * P]
                        if k == 0:
                            ins = V.tensor_copy(o, x)
                        else:
                            ins = V.scalar_tensor_tensor(o, stt_[p0:p0 + 64, k - 1, c, :], dec[p0:p0 + 64, 4 * c + k:4 * c + k + 1],
                                                         x, MUL, ADD)
                ins.then_inc(S("gl_S"), 1)
            dve.wait_ge(*signal("gl_o", 1))
            for e in range(2):
                ins = V.tensor_copy(xn[:, e:4:2, :], Q[4 + e][:, :].rearrange("p (c t) -> p c t", c=2))
            ins.then_inc(S("gl_or"), 1)
            dve.wait_ge(*signal("gl_sd", 1))
            V.reciprocal(r8[:, 0:T], st8[:, 0:T]).then_inc(S("gl_r"), 1)
            dve.wait_ge(*signal("gl_or", 1))
            dve.wait_ge(*signal("sog", 2))
            for j in range(2):
                dve.wait_ge(*signal("gf_sp", j + 1))
                link(V.tensor_tensor(pairs(xn, j), Q[2 + j][:, :], pairs(xn, j), MUL))
                V.scalar_tensor_tensor(pairs(xn, j), pairs(xn, j), col(V_GLA), pairs(sog, j), MUL, MUL).then_inc(S("go_y"), 1)
            dve.wait_ge(*signal("la_sd", 1))
            link(V.reciprocal(rstd[:, :], std[:, :]))
            for c in range(2):
                V.scalar_tensor_tensor(cq[:, c, :], cq[:, c, :], col(V_QA + c), rstd[:, 0:T], MUL, MUL).then_inc(S("la_n"), 1)
            V.scalar_tensor_tensor(ckv[:, :], ckv[:, :], col(V_KVA), rstd[:, T:512], MUL, MUL).then_inc(S("la_n"), 1)
            lows("go", xn, oh, ol, 2)
            dve.wait_ge(*signal("la_hi", 1))
            V.tensor_tensor(cql[:, 0:2, :], cq[:, :, :], f(cqh[:, 0:2, :]), SUB).then_inc(S("la_lo"), 2)
            dve.wait_ge(*signal("la_hi", 2))
            V.tensor_tensor(cql[:, 2, :], ckv[:, :], f(cqh[:, 2, :]), SUB).then_inc(S("la_lo"), 1)
            split_lo(dve, SLAB0["ukv"])
            V.tensor_copy(kh[64:P, :, :], kpe[64:P, :].rearrange("p (a t) -> p a t", a=1).broadcast_to([64, 8, T]))\
                .then_inc(S("kpe_in"), 1)
            n = ACC0["uq"]
            for j in range(4):
                dve.wait_ge(*signal("uq_ps", j + 1))
                V.tensor_copy(pairs(qh, j), L[(n + j) % 2][:, :]).then_inc(free_sem(n + j), 1)
            n = ACC0["ukv"]
            for j in range(4):
                dve.wait_ge(*signal("uk_ps", j + 1))
                V.tensor_copy(kh[0:64, 2 * j:2 * j + 2, :].rearrange("p c t -> p (c t)"), L[(n + j) % 2][0:64, :])\
                    .then_inc(free_sem(n + j), 1)
            for b in range(TB):
                dve.wait_ge(*signal("w_used", 2 * SLAB0["uq"] + 2 * b + 2))
                V.tensor_copy(vm[:, b, :], L[(n + 4 + b) % 2][:, :]).then_inc(free_sem(n + 4 + b), 1)
            split_lo(dve, SLAB0["wo2"])
            dve.wait_ge(*signal("ml_sd", 1))
            V.reciprocal(r8[:, :], st8[:, :]).then_inc(S("ml_r"), 1)
            for part, t, g, b0 in (("mqf", qh, V_MLAQ, 2), ("mkf", kh, V_MLAK, 4)):
                acc_freed(dve, ACC0["uq"] + 2 if part == "mqf" else ACC0["ukv"] + 2)
                acc_freed(dve, ACC0["uq"] + 3 if part == "mqf" else ACC0["ukv"] + 3)
                if part == "mkf":
                    dve.wait_ge(*signal("kpe_in", 1))
                for j in range(4):
                    dve.wait_ge(*signal(part + "_sp", j + 1))
                    V.scalar_tensor_tensor(pairs(t, j), pairs(t, j), col(g), Q[b0 + j % 2][:, :], MUL, MUL)\
                        .then_inc(S(part + "_use"), 1)
            dve.wait_ge(*signal("rope", 1))
            tr = xn[64:96, :, :]
            cosb = rope_c[64:96, :].rearrange("p (a t) -> p a t", a=1).broadcast_to([32, 8, T])
            sinb = rope_s[96:P, :].rearrange("p (a t) -> p a t", a=1).broadcast_to([32, 8, T])
            dve.wait_ge(*signal("go_lo", 2))
            for part, t in (("mqf", qh), ("mkf", kh)):
                dve.wait_ge(*signal(part + "_use", 4))
                link(V.tensor_tensor(t[64:96, :, :], t[64:96, :, :], cosb, MUL))
                link(V.tensor_tensor(tr, t[96:P, :, :], sinb, MUL))
                ins = V.tensor_tensor(t[64:96, :, :], t[64:96, :, :], tr, ADD)
                if part == "mqf":
                    link(ins)
            ins.then_inc(S("ml_k"), 1)

            def y_second(u, bank):
                g, blk = u // 2, u % 2
                return V.tensor_copy(xn[:, 4 + 2 * g:6 + 2 * g, blk * P:(blk + 1) * P],
                                     bank[:, 0:256].rearrange("p (c q) -> p c q", c=2))
            dve.wait_ge(*signal("ml_k", 1))
            in_turn(4, *attention("ml", [1, 2] * 2, prob2, 96 ** -0.5,
                                  lambda b: cst[:, C_OWN2:C_OWN2 + P] if b == 1 else cst[:, C_OWN2 - P:C_OWN2 + P], y_second))
            dve.wait_ge(*signal("ml_yo", 4))
            lows("lo", xn, oh, ol, 2, j0=2)
            stage_loop("wo2", 4, add_to_x("wo2", SLAB0["wo2"], ACC0["wo2"]))

            norm_lows("n6", V_XA)

            def query_heads(i, r):
                if r == 1:
                    for j in range(4):
                        dve.wait_ge(*signal("mem_ps", j + 1))
                        V.tensor_copy(pairs(mT, j), Q[2 + j][:, :]).then_inc(S("mem_ok"), 1)
                scaled_out("xq", r, xq[:, 2 * r:2 * r + 2, :])

            straight("xq", 2, query_heads, st="n6")
            dve.wait_ge(*signal("mem_ok", 4))
            norm_lows("n7", V_MEM, src=mT, xh=mh, xl=ml)
            straight("xk", 2, lambda i, r: scaled_out("xk", r, xq[:, 4 + 2 * r:6 + 2 * r, :]), st="n7")
            n_v, s_v = ACC0["xv"], SLAB0["xv"]

            def mem_values(i, r):
                slab_used(dve, s_v + r, i)
                for b in range(TB):
                    ins = V.tensor_scalar(xv[:, b, r * 256:(r + 1) * 256], L[(n_v + r) % 2][:, b * 256:(b + 1) * 256],
                                          rcol[:, b:b + 1], None, MUL)
                ins.then_inc(free_sem(n_v + r), 1)
            stage_loop("xv", 2, mem_values)
            dve.wait_ge(*signal("xx_sd", 1))
            V.reciprocal(rx8[:, 0:T], sx8[:, 0:T]).then_inc(S("xx_r"), 1)
            acc_freed(dve, ACC0["xk"])
            acc_freed(dve, ACC0["xk"] + 1)
            for j in range(4):
                dve.wait_ge(*signal("xf_sp", j + 1))
                V.scalar_tensor_tensor(pairs(xq, j), pairs(xq, j), col(V_XQ if j < 2 else V_XK), Q[2 + j % 2][:, :], MUL, MUL)\
                    .then_inc(S("xf_use"), 1)

            def y_third(u, bank):
                return V.tensor_copy(xn[:, 0:4, u * P:(u + 1) * P], bank[:, :].rearrange("p (c q) -> p c q", c=4))
            in_turn(2, *attention("xa", [2, 2], prob3, 128 ** -0.5, lambda b: cst[:, C_ZERO:C_ZERO + 256], y_third))
            dve.wait_ge(*signal("xa_yo", 2))
            lows("xo", xn, mh, ml, 2)
            stage_loop("xo", 4, add_to_x("xo", SLAB0["xo"], ACC0["xo"]))
            norm_lows("n8", V_FFN3)
            dve.wait_ge(*signal("gpad0", 1))
            feed_forward("f3u", "f3d", "n8", conv=True)
            for k in range(2):
                dve.wait_ge(*signal("res_ps", 2 * k + 2))
                V.tensor_copy(res[:, k, 512:1024], Q[2 * k + 1][:, :]).then_inc(S("resd"), 1)

        @block.gpsimd
        def _(pool):
            G = nc.gpsimd
            def norm_pairs(st):
                for j in range(1, 4):
                    pool.wait_ge(*signal(st + "_sq", j + 1))
                    if j > 1:
                        pool.wait_ge(*signal(st + "_ps", j - 1))
                    G.tensor_tensor(sq[:, 0, :], sq[:, 0, :], sq[:, j, :], ADD).then_inc(S(st + "_ps"), 1)
                    if st == "n5":
                        if j > 1:
                            pool.wait_ge(*signal("n5_ps2", j - 1))
                        G.tensor_tensor(pairs(xn, 0), pairs(xn, 0), pairs(xn, j), ADD).then_inc(S("n5_ps2"), 1)

            def feed_forward(up):
                with pool.Fori(0, FP) as i:
                    pool.wait_ge(*signal(up + "_si", i + 1))
                    G.tensor_tensor(two_t(sil[:, :]), two_t(sil[:, :]), factor, MUL).then_inc(S(up + "_sr"), 1)

            norm_pairs("n1")
            feed_forward("f1u")
            norm_pairs("n2")
            pool.wait_ge(*signal("n2_ps", 3))
            pool.wait_ge(*signal("sines", 1))
            G.tensor_scalar(rope_s[64:P, :], rope_s[64:P, :], cst[64:P, C_SIGN:C_SIGN + 1], None, MUL).then_inc(S("rope"), 1)
            pool.wait_ge(*signal("rope", 1))
            pool.wait_ge(*signal("n2_ss", 1))
            G.memset(pad[:, :, 0:3], 0.0).then_inc(S("pad0"), 1)
            for j in range(4):
                pool.wait_ge(*signal("m_w", j + 1))
                for c in (0, 256):
                    v = wm[:, 2 * j:2 * j + 2, c:c + P]
                    ins = G.affine_select(out=v, in_=v, pattern=[[0, 2], [1, P]], compare_op=ALU.is_ge, fill=0.0,
                                          base=0, channel_multiplier=-1)
                ins.then_inc(S("m_mask"), 1)
            norm_pairs("n3")
            feed_forward("f2u")
            norm_pairs("n5")
            pool.wait_ge(*signal("n5_ss", 1))
            G.memset(att[:, :, :], 0.0).then_inc(S("att0"), 1)
            norm_pairs("n6")
            norm_pairs("n7")
            norm_pairs("n8")
            pool.wait_ge(*signal("n8_ss", 1))
            G.memset(gpad[:, :, 0:2], 0.0).then_inc(S("gpad0"), 1)
            feed_forward("f3u")


def kernel(**inputs):
    import concourse.bacc as _bacc
    from concourse.bass_utils import run_bass_kernel_spmd as _run

    nc = _bacc.Bacc("TRN2", target_bir_lowering=False, num_devices=1)
    arrays, A = {}, {}
    for name, a in inputs.items():
        a = np.ascontiguousarray(a)
        arrays[f"in_{name}"] = a
        A[name] = nc.dram_tensor(f"in_{name}", a.shape, mybir.dt.from_np(a.dtype), kind="ExternalInput").ap()
    c = shape_constants()
    arrays["shape_constants"] = c
    consts = nc.dram_tensor("shape_constants", c.shape, mybir.dt.float32, kind="ExternalInput").ap()
    out = nc.dram_tensor("out", (1, T, D), mybir.dt.float32, kind="ExternalOutput").ap()
    build(nc, A, consts, out)
    r = _run(nc, [arrays], core_ids=[0])
    return r.results[0]["out"]
```

```python
import numpy as np
import concourse.bass as bass
from concourse import mybir
from contextlib import ExitStack

P = 128
T = 256
TB = T // P
D = 1024
DC = D // P
FF = 2816
FC = FF // P
FP = FC // 2
SLAB = 11 * 256
VEC_LOADS, SMALL_LOADS = 27, 9
EPS = 1e-6
NEG = -1.0e30

C_ID, C_ONE = 0, 128
C_PREV, C_OWN, C_ZERO, C_OWN2 = 256, 384, 512, 768
C_RESET, C_GLA, C_HOT = 896, 1152, 1280
C_INV, C_SIGN, C_EPS = 1344, 1345, 1346
C_ALL = 1347

V_FFN1, V_MIX, V_FFN2, V_FINAL, V_MIX2, V_XA, V_MEM, V_FFN3 = 0, 8, 16, 24, 32, 40, 48, 56
V_BQ, V_BK, V_BMQK, V_BMO, V_BG = 64, 72, 74, 82, 90
V_HEAD, V_GATEB, V_GLA, V_QA, V_KVA, V_XQ, V_XK, V_MLAQ, V_MLAK = 106, 114, 116, 117, 119, 120, 121, 122, 123
VEC0 = 124
V_FCW, V_FCB, V_MCONV = 128, 128 + 3 * FC, 128 + 4 * FC
VEC1 = 4 * FC + 32
V_FIN32 = 248

I_AQ, I_AK, I_AV, I_MQK, I_MV, I_MO, I_MI, I_G = 0, 1024, 1280, 1536, 2560, 3584, 4608, 4624
J_Q, J_K, J_V, J_ALR, J_OG, J_CQ, J_CKV, J_PE = 0, 256, 512, 1024, 1040, 1552, 1808, 1936

STAGES = [("f1u", 22, 22), ("f1d", 8, 4), ("wq", 4, 4), ("wkv", 2, 2), ("wmqk", 4, 4), ("wmv", 4, 4),
          ("wmo", 4, 4), ("wg", 8, 8), ("pa", 4, 4), ("pm", 4, 4), ("wo", 4, 4), ("f2u", 22, 22), ("f2d", 8, 4),
          ("w2", 8, 8), ("uq", 1, 4), ("xk0", 1, 1), ("ukv", 1, 6), ("xk1", 1, 1), ("xv", 2, 2),
          ("wo2", 4, 4), ("xq", 2, 2), ("xo", 4, 4), ("f3u", 22, 22), ("f3d", 8, 4)]


def first_numbers():
    slab, acc, s, n = {}, {}, 0, 0
    for name, slabs, accs in STAGES:
        slab[name], acc[name] = s, n
        s, n = s + slabs, n + accs
    return slab, acc, s


def shared_signals():
    kinds = [
        ("norm", ("hi", "lo", "sq", "ps", "ss", "sd", "rc", "sp", "rs"), (4, 4, 4, 3, 1, 1, 1, 1, 1),
         [(f"n{k}", 1) for k in (1, 2, 3, 5, 7, 6, 8)]),
        ("softmax", ("mx", "ex", "pn", "sc", "tp", "pt", "pv", "yo"), (4, 4, 4, 1, 1, 1, 1, 1), [("at", 8), ("ml", 4), ("xa", 2)]),
        ("ff", ("hh", "hl", "si", "sr"), (1, 1, 1, 1), [("f1u", FP), ("f2u", FP), ("f3u", FP)]),
    ]
    found = {}
    for kind, signals, each, stages in kinds:
        for sig, n in zip(signals, each):
            base = 0
            for st, units in stages:
                found[f"{st}_{sig}"] = (f"{kind}_{sig}", base)
                base += n * units
    chains = {
        "mixer2_dve": [("alr", 1), ("la_n", 3), ("gl_zr", 1), ("la_lo", 3), ("gl_cum", 2), ("gl_d", 1), ("k_rot", 1),
                       ("gl_ke", 1), ("gl_am", 2)],
        "mixer2_act": [("la_sq", 2), ("kpe_sq", 1), ("la_sd", 1), ("la_hi", 2), ("gl_l", 3), ("gl_e", 3)],
        "mixer2_pe": [("la_sum", 1), ("alr_ps", 1), ("gl_z", 1)],
    }
    for sem, order in chains.items():
        base = 0
        for sig, n in order:
            found[sig] = (sem, base)
            base += n
    return found


SHARED = shared_signals()
MIX = 20


def shape_constants():
    c = np.zeros((P, C_ALL), np.float32)
    i = np.arange(P)
    c[i, C_ID + i] = 1
    c[:, C_ONE:C_ONE + P] = 1
    q, k = i[:, None], i[None, :]
    c[:, C_PREV:C_PREV + P] = np.where(k > q, 0, NEG)
    c[:, C_OWN:C_OWN + P] = np.where(k <= q, 0, NEG)
    c[:, C_OWN2:C_OWN2 + P] = np.where(k <= q, 0, NEG)
    c[:, C_RESET:C_RESET + T] = np.arange(T) % 64 != 0
    c[:, C_GLA:C_GLA + P] = (q // 64 == k // 64) & (q <= k)
    for h in range(8):
        c[:, C_HOT + h * 8 + h] = 1
    c[:, C_INV] = np.float32(10000.0) ** (-(i % 16).astype(np.float32) / np.float32(16))
    c[:, C_SIGN] = np.where((i // 16) % 2 == 0, -1, 1)
    c[:, C_EPS] = EPS
    return c


def build(nc, A, consts, out):
    f32, f32r, i32 = mybir.dt.float32, mybir.dt.float32r, mybir.dt.int32
    ALU, ACT = mybir.AluOpType, mybir.ActivationFunctionType
    MUL, ADD, SUB, MAX, MIN = ALU.mult, ALU.add, ALU.subtract, ALU.max, ALU.min
    SLAB0, ACC0, SLABS = first_numbers()
    ctx = ExitStack()
    with ctx:
        def sb(name, shape, dt=f32, scope=ctx):
            return scope.enter_context(nc.sbuf_tensor(name, shape, dt))

        sems = {}

        def S(name):
            name = SHARED.get(name, (name, 0))[0]
            if name not in sems:
                sems[name] = ctx.enter_context(nc.semaphore("s_" + name))
            return sems[name]

        def signal(name, count):
            return S(name), SHARED.get(name, (name, 0))[1] + count

        raw = sb("raw", [P, 2, SLAB])
        wh = sb("wh", [P, 2, SLAB], f32r)
        wl = sb("wl", [P, 2, SLAB], f32r)
        xT = sb("xT", [P, DC, T])
        ah = sb("ah", [P, DC, T], f32r)
        al = sb("al", [P, DC, T], f32r)
        xn = sb("xn", [P, DC, T])
        sq = sb("sq", [P, 4, 512])
        cst = sb("cst", [P, C_ALL])
        vec = sb("vec", [P, 256])
        std = sb("std", [P, 512])
        rstd = sb("rstd", [P, 512])
        bav = sb("bav", [P, 256])
        with ExitStack() as sc:
            bmv = sb("bmv", [P, 1024], scope=sc)
        keep = ctx.enter_context(ExitStack())
        rh = sb("rh", [8, 512], f32r, scope=keep)
        rl = sb("rl", [8, 512], f32r, scope=keep)
        idr = sb("idr", [8, 8], f32r)
        nsink = sb("nsink", [P, 32])
        wif = sb("wif", [P, DC, 16])
        walr = sb("walr", [P, DC, 16])
        w2g = sb("w2g", [16, 256])
        bif = sb("bif", [8, 4])
        stmp = sb("stmp", [P, 2, 512])
        vv = sb("vv", [P, 4])
        root = sb("root", [P, 4])
        rcol = sb("rcol", [P, 4])
        g1raw = sb("g1raw", [8, P])
        rope_c = sb("rope_c", [P, T])
        rope_s = sb("rope_s", [P, T])
        rmx = sb("rmx", [P, 2, 4])
        rsm = sb("rsm", [P, 2, 4])
        rs2 = sb("rs2", [P, 2, 4])
        rin = sb("rin", [P, 2, 4])

        with ExitStack() as sc:
            xraw = sb("xraw", [P, TB, D], scope=sc)
        with ExitStack() as sc:
            hh = sb("hh", [P, FC, T], f32r, scope=sc)
            hl = sb("hl", [P, FC, T], f32r, scope=sc)
            sil = sb("sil", [P, 512], scope=sc)
            hid = sb("hid", [P, 512], scope=sc)
            gpad = sb("gpad", [P, 2, T + 2], scope=sc)
            gcv = sb("gcv", [P, 512], scope=sc)
            vraw = sb("vraw", [P, 2, P], scope=sc)
            posi = sb("posi", [P, T], i32, scope=sc)
            ang = sb("ang", [P, T], scope=sc)
            turn = sb("turn", [P, T], scope=sc)
            tmpr = sb("tmpr", [P, T], scope=sc)
            quarter = sb("quarter", [P, T], scope=sc)
        with ExitStack() as sc:
            sigo = sb("sigo", [P, 8, T], scope=sc)
            gate = sb("gate", [P, 16, T], scope=sc)
            with ExitStack() as s2:
                aq = sb("aq", [P, 8, T], scope=s2)
                mv = sb("mv", [P, TB, D], scope=s2)
                akd = sb("akd", [P, 4, T], scope=s2)
                av = sb("av", [P, TB, 256], scope=s2)
                pad = sb("pad", [P, 8, T + 3], scope=s2)
                gtok = sb("gtok", [P, TB, 16], scope=s2)
                acol = sb("acol", [P, TB, 8], scope=s2)
                ti = sb("ti", [8, 512], scope=s2)
                lse = sb("lse", [8, T], scope=s2)
                Gc = sb("Gc", [8, T], scope=s2)
                ai = sb("ai", [8, T], scope=s2)
                Mx = sb("Mx", [8, T], scope=s2)
                gm = sb("gm", [8, T], scope=s2)
                en = sb("en", [8, T], scope=s2)
                rden = sb("rden", [8, T], scope=s2)
                with ExitStack() as s3:
                    prob1 = sb("prob1", [P, 2, 4, T], scope=s3)
                    probT1 = sb("probT1", [P, 2, 512], scope=s3)
                with ExitStack() as s3:
                    wm = sb("wm", [P, 8, 384], scope=s3)
            with ExitStack() as s2:
                bh = sb("bh", [P, DC, T], f32r, scope=s2)
                bl = sb("bl", [P, DC, T], f32r, scope=s2)
                ch = sb("ch", [P, DC, T], f32r, scope=s2)
                cl = sb("cl", [P, DC, T], f32r, scope=s2)
                mgb = sb("mgb", [P, 512], scope=s2)
                mgs = sb("mgs", [P, 512], scope=s2)
        with ExitStack() as sc:
            xq = sb("xq", [P, 8, T], scope=sc)
            xv = sb("xv", [P, TB, 512], scope=sc)
            with ExitStack() as s1:
                cq = sb("cq", [P, 2, T], scope=s1)
                ckv = sb("ckv", [P, T], scope=s1)
                kpe = sb("kpe", [P, T], scope=s1)
                kr = sb("kr", [P, 3, T], scope=s1)
                gk1 = sb("gk1", [P, 1], scope=s1)
                r8 = sb("r8", [8, 512], scope=s1)
                gs8 = sb("gs8", [8, 512], scope=s1)
                cqh = sb("cqh", [P, 3, T], f32r, scope=s1)
                cql = sb("cql", [P, 3, T], f32r, scope=s1)
                kh = sb("kh", [P, 8, T], scope=s1)
                vm = sb("vm", [P, TB, 512], scope=s1)
                with ExitStack() as s2:
                    qh = sb("qh", [P, 8, T], scope=s2)
                with ExitStack() as s2:
                    memraw = sb("memraw", [P, TB, D], scope=s2)
                keep = s1.enter_context(ExitStack())
                hold = sb("hold", [P, 8, T], scope=keep)
                sog = sb("sog", [P, 4, T], scope=keep)
                with ExitStack() as s2:
                    gq = sb("gq", [P, 2, T], scope=s2)
                    gk = sb("gk", [P, 2, T], scope=s2)
                    gv = sb("gv", [P, TB, 512], scope=s2)
                    zg = sb("zg", [P, 512], scope=s2)
                    lg = sb("lg", [P, 512], scope=s2)
                    cum = sb("cum", [P, 512], scope=s2)
                    ketok = sb("ketok", [P, TB, 256], scope=s2)
                    att = sb("att", [P, 2, 512], scope=s2)
                    dec = sb("dec", [P, 8], scope=s2)
                    stt_ = sb("stt_", [P, 3, 2, P], scope=s2)
                prob2 = sb("prob2", [P, 2, 4, T], scope=s1)
                probT2 = sb("probT2", [P, 2, 512], scope=s1)
            with ExitStack() as s1:
                mh = sb("mh", [P, DC, T], f32r, scope=s1)
                ml = sb("ml", [P, DC, T], f32r, scope=s1)
                sx8 = sb("sx8", [8, 512], scope=s1)
                rx8 = sb("rx8", [8, 512], scope=s1)
                prob3 = sb("prob3", [P, 2, 4, T], scope=s1)
                probT3 = sb("probT3", [P, 2, 512], scope=s1)
        with ExitStack() as sc:
            res = sb("res", [P, TB, D], scope=sc)

        L = [ctx.enter_context(nc.psum_tensor(f"acc{i}", [P, 512], f32)) for i in range(2)]
        Q = [ctx.enter_context(nc.psum_tensor(f"part{i}", [P, 512], f32)) for i in range(6)]

        ident = cst[:, C_ID:C_ID + P]
        ones = cst[:, C_ONE:C_ONE + P]
        eps = cst[:, C_EPS:C_EPS + 1]

        def sel(h):
            return idr[0:8, h:h + 1].broadcast_to([8, P])

        def hot(h, rows=P):
            return cst[0:rows, C_HOT + h * 8:C_HOT + (h + 1) * 8]

        def col(n, lo=0, hi=P):
            return vec[lo:hi, n:n + 1]

        def pairs(t, j):
            return t[:, 2 * j:2 * j + 2, :].rearrange("p c t -> p (c t)")

        def rpair(t, j):
            return t[:, :, :].rearrange("p c t -> p (c t)")[:, bass.ds(j * 512, 512)]

        def f(ap):
            return ap.bitcast(f32)

        def two_t(ap):
            return ap.rearrange("p (c t) -> p c t", c=2)

        qk = pad[:, :, 3:T + 3]
        alr = kr[0:16, 0, :]
        qd, ki, ke = gq, two_t(cum[:, :]), two_t(zg[:, :])

        factor = rstd[:, 0:T].rearrange("p (a t) -> p a t", a=1).broadcast_to([P, 2, T])

        def loaded(eng, s, i=0):
            eng.wait_ge(*signal(f"raw{s % 2}", 16 * (s // 2 + 1) + 16 * i))

        def lo_ready(eng, s, i, half):
            eng.wait_ge(*signal("w_lo", 2 * s + half + 1 + 4 * i))

        def slab_used(eng, s, i=0, half=1):
            eng.wait_ge(*signal("w_used", 2 * s + half + 1 + 4 * i))

        def acc_freed(eng, n, i=0):
            eng.wait_ge(*signal(f"acc_free{n % 2}", n // 2 + 1 + i))

        def free_sem(n):
            return S(f"acc_free{n % 2}")

        def halves(nk):
            return (0, (nk + 1) // 2), ((nk + 1) // 2, nk)

        def looped(eng, n, body, peel=False):
            if peel:
                body(0, False)
            if n > 2:
                with eng.Fori(1 if peel else 0, n - 1) as i:
                    body(i, False)
            else:
                for i in range(1 if peel else 0, n - 1):
                    body(i, False)
            body(n - 1, True)

        def columns(name):
            return {"f1d": 11, "f2d": 11, "f3d": 11, "xo": 4}.get(name, 8), 256

        EXTRA = {SLAB0["w2"] + 1: "pe", SLAB0["uq"]: "uq", SLAB0["ukv"]: "ukv"}
        STAGE_OF = {SLAB0[n] + k: n for n, c, _ in STAGES for k in range(c)}

        def shape_of(s):
            return columns(STAGE_OF[s]) if s in STAGE_OF else None

        def parts(kind, t, slot):
            r = raw[:, slot, :]
            w = t[:, slot, :]
            if kind == "pe":
                d = w[:, 0:2048].rearrange("p (k c) -> p k c", k=8)
                s = r[:, 0:8 * 160].rearrange("p (k c) -> p k c", k=8)
                return [(d[:, :, 0:160], s), (d[:, :, 160:192], s[:, :, 128:160]),
                        (d[:, :, 192:224], s[:, :, 128:160]), (d[:, :, 224:240], s[:, :, 144:160]),
                        (d[:, :, 240:256], s[:, :, 128:144])]
            if kind == "uq":
                d = w[:, 0:2048].rearrange("p (k c) -> p k c", k=16)
                s = r[:, 0:1536].rearrange("p (k c) -> p k c", k=16)
                return [(d[:, :, 0:96], s), (d[:, :, 96:112], s[:, :, 80:96]), (d[:, :, 112:128], s[:, :, 64:80])]
            return [(w[:, 0:512], r[:, 0:512]), (w[:, 512:1024], r[:, 512:1024])]

        def split_hi(act, s, i=0):
            if s >= SLABS:
                return
            loaded(act, s, i)
            slot = s % 2
            if s in EXTRA:
                slab_used(act, s - 2)
                todo = parts(EXTRA[s], wh, slot)
                for n, (d, r) in enumerate(todo):
                    ins = nc.scalar.activation(d, r, ACT.Copy)
                ins.then_inc(S("w_hi"), 2)
                return
            nk, nw = shape_of(s)
            for half, (a, b) in enumerate(halves(nk)):
                if s >= 2:
                    slab_used(act, s - 2, i, half if shape_of(s - 2) == (nk, nw) and s - 2 not in EXTRA else 1)
                nc.scalar.activation(wh[:, slot, a * nw:b * nw], raw[:, slot, a * nw:b * nw],
                                     ACT.Copy).then_inc(S("w_hi"), 1)

        def split_lo(dve, s, i=0):
            if s >= SLABS:
                return
            slot = s % 2
            if s in EXTRA:
                dve.wait_ge(*signal("w_hi", 2 * s + 2))
                for (d, r), (h, _) in zip(parts(EXTRA[s], wl, slot), parts(EXTRA[s], wh, slot)):
                    ins = nc.vector.tensor_tensor(d, r, f(h), SUB)
                ins.then_inc(S("w_lo"), 2)
                return
            nk, nw = shape_of(s)
            for half, (a, b) in enumerate(halves(nk)):
                dve.wait_ge(*signal("w_hi", 2 * s + half + 1 + 4 * i))
                nc.vector.tensor_tensor(wl[:, slot, a * nw:b * nw], raw[:, slot, a * nw:b * nw],
                                        f(wh[:, slot, a * nw:b * nw]), SUB).then_inc(S("w_lo"), 1)

        block = ctx.enter_context(nc.Block())

        @block.sync
        def _(sp):
            sp.dma_start(cst[:, 0:256], consts[:, 0:256]).then_inc(S("ident"), 16)
            sp.dma_start(xraw[:, :, :], A["x"][0].rearrange("(b p) c -> p b c", p=P)).then_inc(S("x_in"), 16)
            win = A["w_in"][0].rearrange("(k p) c -> p k c", p=P)
            win2 = A["w_in_2"][0].rearrange("(k p) c -> p k c", p=P)

            def load(s, i, src, kind=None):
                if s >= 2:
                    sp.wait_ge(*signal("w_lo", 2 * s - 2 + 4 * i))
                nk, nw = shape_of(s)
                if kind == "pe":
                    d = raw[:, s % 2, 0:8 * 160].rearrange("p (k c) -> p k c", k=8)
                elif kind == "uq":
                    d = raw[:, s % 2, 0:1536].rearrange("p (k c) -> p k c", k=2)
                elif kind == "ukv":
                    d = raw[:, s % 2, 0:1024]
                else:
                    d = raw[:, s % 2, 0:nk * nw].rearrange("p (k c) -> p k c", k=nk)
                sp.dma_start(d, src).then_inc(S(f"raw{s % 2}"), 16)

            def many(name, w, first):
                s0, count = SLAB0[name], dict((n, c) for n, c, _ in STAGES)[name]

                def body(i):
                    for r in range(2):
                        load(s0 + r, i, w[:, :, bass.ds(first + i * 512 + r * 256, 256)])
                if count > 2:
                    with sp.Fori(0, count // 2) as i:
                        body(i)
                else:
                    body(0)

            def gains_and_biases():
                rows = [(V_MIX, "mix_norm"), (V_FFN2, "ffn2_norm"),
                        (V_MIX2, "norm_mix_2"), (V_XA, "norm_xa_2"), (V_MEM, "norm_mem_2"), (V_FFN3, "norm_ffn_2"),
                        (V_GATEB, "gla_gate_b_2"), (V_GLA, "gla_out_norm_2"), (V_QA, "mla_q_a_norm_2"),
                        (V_KVA, "mla_kv_a_norm_2"), (V_XQ, "xa_q_norm_2"), (V_XK, "xa_k_norm_2")]
                todo = []
                for v, name in rows:
                    n = A[name].shape[1] // P
                    todo.append((vraw[v:v + n, 0, :], A[name][0].rearrange("(c p) -> c p", p=P)))
                todo.append((vraw[V_FINAL:V_FINAL + 8, 0, :], A["final_norm"].rearrange("(c p) -> c p", p=P)))
                todo.append((vraw[V_HEAD:V_HEAD + 8, 0, :], A["mlstm_head_norm"][0]))
                b = A["b_in"][0]
                for v, lo, n in ((V_BQ, I_AQ, 10), (V_BMQK, I_MQK, 8), (V_BMO, I_MO, 8), (V_BG, I_G, 16)):
                    todo.append((vraw[v:v + n, 0, :], b[lo:lo + n * P].rearrange("(c p) -> c p", p=P)))
                for v, name in ((V_MLAQ, "mla_q_norm_2"), (V_MLAK, "mla_k_norm_2")):
                    g = A[name]
                    todo += [(vraw[v:v + 1, 0, 0:96], g), (vraw[v:v + 1, 0, 96:112], g[:, 80:96]),
                             (vraw[v:v + 1, 0, 112:128], g[:, 64:80])]
                todo.append((vraw[0:3 * FC, 1, :], A["ffn_conv_w_2"][0].rearrange("j (c p) -> (j c) p", p=P)))
                todo.append((vraw[3 * FC:4 * FC, 1, :], A["ffn_conv_b_2"][0].rearrange("(c p) -> c p", p=P)))
                todo.append((vraw[4 * FC:4 * FC + 32, 1, :], A["mlstm_conv"][0].rearrange("j (c p) -> (j c) p", p=P)))
                for d, s in todo:
                    sp.dma_start(d, s).then_inc(S("vec_in"), 16)
                assert len(todo) == VEC_LOADS

            def feed_forward(up, down, gate_w, up_w, down_w):
                g = gate_w.rearrange("(k p) c -> p k c", p=P)
                u = up_w.rearrange("(k p) c -> p k c", p=P)
                s0 = SLAB0[up]
                if s0 == 0:
                    load(0, 0, g[:, :, 0:256])
                    load(1, 0, u[:, :, 0:256])
                    sp.dma_start(cst[:, 256:C_ALL], consts[:, 256:C_ALL]).then_inc(S("consts"), 16)
                    gains_and_biases()
                with sp.Fori(1 if s0 == 0 else 0, FP) as i:
                    for r, w in ((0, g), (1, u)):
                        sp.wait_ge(*signal("w_lo", 2 * (s0 + r) - 2 + 4 * i))
                        d = raw[:, (s0 + r) % 2, 0:2048].rearrange("p (k c) -> p k c", k=8)
                        sp.dma_start(d, w[:, :, bass.ds(i * 256, 256)]).then_inc(S(f"raw{(s0 + r) % 2}"), 16)
                d = down_w.rearrange("(k p) c -> p k c", p=P)
                s0 = SLAB0[down]
                with sp.Fori(0, 4) as i:
                    for r in range(2):
                        load(s0 + r, i, d[:, 11 * r:11 * r + 11, bass.ds(i * 256, 256)])

            feed_forward("f1u", "f1d", A["ffn1_w_gate"][0], A["ffn1_w_up"][0], A["ffn1_w_down"][0])
            many("wq", win, I_AQ)
            many("wkv", win, I_AK)
            many("wmqk", win, I_MQK)
            many("wmv", win, I_MV)
            many("wmo", win, I_MO)
            many("wg", win, I_G)
            many("pa", A["w_proj_attn"][0].rearrange("(k p) c -> p k c", p=P), 0)
            many("pm", A["w_proj_mlstm"][0].rearrange("(k p) c -> p k c", p=P), 0)
            many("wo", A["w_out"][0].rearrange("(k p) c -> p k c", p=P), 0)
            feed_forward("f2u", "f2d", A["ffn2_w_gate"][0], A["ffn2_w_up"][0], A["ffn2_w_down"][0])
            s0 = SLAB0["w2"]
            for k, c in enumerate((J_CQ, None, J_Q, J_K, J_V, J_V + 256, J_OG, J_OG + 256)):
                if k == 1:
                    load(s0 + k, 0, win2[:, :, J_CKV:J_CKV + 160], "pe")
                else:
                    load(s0 + k, 0, win2[:, :, c:c + 256])
                if k == 3:
                    sp.wait_ge(*signal("n5_ss", 1))
                    sp.dma_start(memraw[:, :, :], A["mem_2"][0].rearrange("(b p) c -> p b c", p=P)).then_inc(S("mem_in"), 16)
            kv = A["xa_w_kv_2"][0].rearrange("(k p) c -> p k c", p=P)
            load(SLAB0["uq"], 0, A["mla_w_uq_2"][0].rearrange("(k p) c -> p k c", p=P), "uq")
            load(SLAB0["xk0"], 0, kv[:, :, 0:256])
            load(SLAB0["ukv"], 0, A["mla_w_ukv_2"][0], "ukv")
            load(SLAB0["xk1"], 0, kv[:, :, 256:512])
            many("xv", kv, 512)
            many("wo2", A["w_out_2"][0].rearrange("(k p) c -> p k c", p=P), 0)
            many("xq", A["xa_w_q_2"][0].rearrange("(k p) c -> p k c", p=P), 0)
            many("xo", A["xa_w_o_2"][0].rearrange("(k p) c -> p k c", p=P), 0)
            feed_forward("f3u", "f3d", A["ffn_w_gate_2"][0], A["ffn_w_up_2"][0], A["ffn_w_down_2"][0])
            for tb in range(TB):
                sp.wait_ge(*signal("resa", tb + 1))
                sp.wait_ge(*signal("resd", tb + 1))
                sp.dma_start(out[0, tb * P:(tb + 1) * P, :], res[:, tb, :]).then_inc(S("stored"), 16)
            sp.wait_ge(*signal("stored", 16 * TB))

        @block.tensor
        def _(pe):
            mm = nc.tensor.matmul

            def normed_input(st):
                return lambda k: k % 2 == 0 and pe.wait_ge(*signal(st + "_lo", k // 2 + 1))

            def norm_sums(st):
                pe.wait_ge(*signal(st + "_ps", 3))
                if st == "n5":
                    pe.wait_ge(*signal("n5_ps2", 3))
                for c in range(2):
                    for b in range(TB):
                        t = slice(c * T + b * P, c * T + (b + 1) * P)
                        ins = mm(Q[0][:, T + b:T + b + 1], sq[:, 0, t], ones[:, 0:1],
                                 start=c + b == 0, stop=c == 1, skip_group_check=True)
                        if st == "n5":
                            ins = mm(Q[0][:, T + 2 + b:T + 3 + b], xn[:, c, b * P:(b + 1) * P], ones[:, 0:1],
                                     start=False, stop=c == 1, skip_group_check=True)
                ins.then_inc(S(st + "_ss"), 1)

            def norm_spread(st):
                pe.wait_ge(*signal(st + "_rc", 1))
                for n in range(2 if st == "n5" else 1):
                    for b in range(TB):
                        ins = mm(Q[n][:, b * P:(b + 1) * P], rcol[:, 2 * n + b:2 * n + b + 1].broadcast_to([P, P]), ident,
                                 start=b == 0, stop=b == 1, skip_group_check=True)
                ins.then_inc(S(st + "_sp"), 1)

            def late(st):
                return lambda k: k == 6 and norm_spread(st)

            def open_acc(n, i=0):
                if n >= 2:
                    acc_freed(pe, n - 2, i)

            def product(s, i, nk, n, xh, xl, k0=0, first=True, last=True, tokens=False,
                        before=None):
                o, slot = L[n % 2], s % 2
                for half, (ka, kb) in enumerate(halves(nk)):
                    lo_ready(pe, s, i, half)
                    for k in range(ka, kb):
                        if before is not None:
                            before(k)
                        for m in range(2):
                            dst = o[:, m * T:(m + 1) * T]
                            st = first and k == 0 and m == 0
                            en_ = last and k == nk - 1 and m == 1
                            if tokens:
                                c = slice(k * 256, (k + 1) * 256)
                                t = slice(m * P, (m + 1) * P)
                                xa, xb = xh[:, k0 + k, t], xl[:, k0 + k, t]
                                three = ((xa, wh[:, slot, c]), (xb, wh[:, slot, c]), (xa, wl[:, slot, c]))
                            else:
                                c = slice(k * 256 + m * P, k * 256 + (m + 1) * P)
                                xa, xb = xh[:, k0 + k, :], xl[:, k0 + k, :]
                                three = ((wh[:, slot, c], xa), (wh[:, slot, c], xb), (wl[:, slot, c], xa))
                            for q, (a, b) in enumerate(three):
                                ins = mm(dst, a, b, start=st and q == 0, stop=en_ and q == 2, skip_group_check=True)
                    ins.then_inc(S("w_used"), 1)

            def opening(name, st, xh, xl, extra=None):
                s, n = SLAB0[name], ACC0[name]
                open_acc(n)
                product(s, 0, 8, n, xh, xl, before=normed_input(st))
                norm_sums(st)
                open_acc(n + 1)
                if extra is not None:
                    product(s + 1, 0, 8, n + 1, xh, xl, before=lambda k: (late(st)(k), extra(k)))
                else:
                    product(s + 1, 0, 8, n + 1, xh, xl, before=late(st))

            def two(name, xh, xl, nk=8, tokens=False, count=None):
                s, n = SLAB0[name], ACC0[name]
                count = count or dict((a, b) for a, b, _ in STAGES)[name]

                def body(i):
                    for r in range(2):
                        open_acc(n + r, i)
                        product(s + r, i, nk, n + r, xh, xl, tokens=tokens)
                if count > 2:
                    with pe.Fori(0, count // 2) as i:
                        body(i)
                else:
                    body(0)

            def feed_forward(up, down, st, then=None):
                s, n = SLAB0[up], ACC0[up]
                opening(up, st, ah, al)
                if then is not None:
                    then()
                with pe.Fori(1, FP) as i:
                    for r in range(2):
                        pe.wait_ge(free_sem(n + r), (n + r - 2) // 2 + 1 + i)
                        product(s + r, i, 8, n + r, ah, al)
                s, n = SLAB0[down], ACC0[down]
                for q in range(4):
                    open_acc(n + q)
                    for r in range(2):
                        if q == 0:
                            pe.wait_ge(*signal(up + "_hl", FP if r else 6))
                        product(s + 2 * q + r, 0, 11, n + q, hh, hl, k0=11 * r, first=r == 0, last=r == 1)

            def attention(st, units, scores, prob, probT, values, outputs):

                def do_scores(u):
                    if u >= 1:
                        pe.wait_ge(*signal(st + "_mx", 4 * u))
                    for hh_ in range(4):
                        q, k = scores(u, hh_)
                        w = k.shape[1]
                        ins = mm(Q[hh_ % 2][:, (hh_ // 2) * 256:(hh_ // 2) * 256 + w], q, k,
                                 start=True, stop=True, skip_group_check=True)
                    ins.then_inc(S(st + "_sc"), 1)

                def do_transposes(u):
                    if u >= 1:
                        pe.wait_ge(*signal(st + "_pt", u))
                    pe.wait_ge(*signal(st + "_pn", 4 * u + 4))
                    for b in range(units[u]):
                        for hh_ in range(4):
                            ins = nc.tensor.transpose(Q[2 + b][:, hh_ * P:(hh_ + 1) * P],
                                                      prob[:, u % 2, hh_, b * P:(b + 1) * P], ident)
                    ins.then_inc(S(st + "_tp"), 1)

                def do_outputs(u):
                    pe.wait_ge(*signal(st + "_pt", u + 1))
                    if u >= 2:
                        pe.wait_ge(*signal(st + "_yo", u - 1))
                    bank = Q[4 + u % 2]
                    for lo, hi, o0, hs in outputs:
                        for b in range(units[u]):
                            v = values(u, b, hs[0])
                            x = probT[:, b, :].rearrange("p (h q) -> p h q", h=4)[:, hs[0]:hs[-1] + 1:max(1, (hs[-1] - hs[0])), :] \
                                if len(hs) > 1 else probT[:, b, hs[0] * P:(hs[0] + 1) * P]
                            ins = mm(bank[lo:hi, o0:o0 + P * len(hs)], v, x, start=b == 0 and o0 == 0,
                                     stop=b == units[u] - 1, skip_group_check=True)
                    ins.then_inc(S(st + "_pv"), 1)
                return do_scores, do_transposes, do_outputs

            def in_turn(units, do_scores, do_transposes, do_outputs):
                do_scores(0)
                for u in range(units):
                    if u + 1 < units:
                        do_scores(u + 1)
                    do_transposes(u)
                    do_outputs(u)

            def head_sums(st, x, heads, bank, o0, first, rows=P):
                for j in range(heads // 2):
                    pe.wait_ge(*signal(st + "_hs", j + 1))
                    for c in range(2):
                        h = 2 * j + c
                        ins = mm(bank[0:8, o0:o0 + T], hot(h, rows), x[0:rows, j, c * T:(c + 1) * T],
                                 start=first and h == 0, stop=h == heads - 1, skip_group_check=True)
                ins.then_inc(S(st + "_ss"), 1)

            def spread(st, o0, heads, banks, wait):
                for j in range(heads // 2):
                    wait(j)
                    for c in range(2):
                        h = 2 * j + c
                        for x in (rh, rl):
                            ins = mm(banks[j % len(banks)][:, c * T:(c + 1) * T], sel(h), x[0:8, o0:o0 + T],
                                     start=c == 0 and x is rh, stop=c == 1 and x is rl, skip_group_check=True)
                    ins.then_inc(S(st + "_sp"), 1)

            pe.wait_ge(*signal("ident", 16))
            pe.wait_ge(*signal("g1_in", 16))
            nc.tensor.transpose(Q[4][:, 0:8], g1raw[0:8, :], cst[0:8, C_ID:C_ID + 8]).then_inc(S("g1_ps"), 1)
            pe.wait_ge(*signal("x_in", 16))

            def transpose_in(src, st, banks=Q[0:4]):
                for j in range(4):
                    for c in range(2):
                        for b in range(TB):
                            o = (c * TB + b) * P
                            k = 2 * j + c
                            ins = nc.tensor.transpose(banks[j][:, o:o + P], src[:, b, k * P:(k + 1) * P], ident)
                    ins.then_inc(S(st), 1)

            transpose_in(xraw, "x_ps")

            def gains_in():
                pe.wait_ge(*signal("consts", 16))
                pe.wait_ge(*signal("vec_in", 16 * VEC_LOADS))
                pe.wait_ge(*signal("g1_ok", 1))
                nc.tensor.transpose(Q[4][:, 0:VEC0], vraw[0:VEC0, 0, :], cst[0:VEC0, C_ID:C_ID + VEC0])
                nc.tensor.transpose(Q[4][:, P:P + VEC1], vraw[0:VEC1, 1, :], cst[0:VEC1, C_ID:C_ID + VEC1])\
                    .then_inc(S("vec_ps"), 1)

            feed_forward("f1u", "f1d", "n1", then=gains_in)

            opening("wq", "n2", ah, al)
            s, n = SLAB0["wq"], ACC0["wq"]
            for k in (2, 3):
                open_acc(n + k)
                product(s + k, 0, 8, n + k, ah, al)
            s, n = SLAB0["wkv"], ACC0["wkv"]
            open_acc(n)
            product(s, 0, 8, n, ah, al)
            open_acc(n + 1)
            product(s + 1, 0, 8, n + 1, ah, al, tokens=True)

            def if_products():
                pe.wait_ge(*signal("narrow", 2))
                for b in range(TB):
                    for k in range(DC):
                        ins = mm(Q[5][:, b * 16:(b + 1) * 16], xT[:, k, b * P:(b + 1) * P], wif[:, k, :],
                                 start=k == 0 and b == 0, stop=k == DC - 1, skip_group_check=True)
                ins.then_inc(S("if_ps"), 1)

            def if_transposes():
                pe.wait_ge(*signal("if_tok", 1))
                for g in range(2):
                    for b in range(TB):
                        ins = nc.tensor.transpose(Q[4][0:8, g * T + b * P:g * T + (b + 1) * P],
                                                  gtok[:, b, g * 8:(g + 1) * 8], ident)
                ins.then_inc(S("if_T"), 1)

            def a_scores(u, h):
                g, blk = u // 2, u % 2
                p0, hd = 64 * (h % 2), 4 * g + h
                return (aq[p0:p0 + 64, hd // 2, blk * P:(blk + 1) * P],
                        akd[p0:p0 + 64, g, 0:(blk + 1) * P])

            at_scores, at_transposes, at_outputs = attention(
                "at", [1, 2] * 4, a_scores, prob1, probT1,
                lambda u, b, h: av[:, b, (u // 2) * 64:(u // 2 + 1) * 64],
                [(0, 64, 0, [0, 2]), (64, P, 0, [1, 3])])

            def m_spread():
                pe.wait_ge(*signal("m_M", 1))
                pe.wait_ge(*signal("at_yo", 8))
                for b in range(TB):
                    ins = nc.tensor.transpose(Q[5][:, b * 8:(b + 1) * 8], ai[0:8, b * P:(b + 1) * P], cst[0:8, C_ID:C_ID + 8])
                ins.then_inc(S("m_acol"), 1)
                pe.wait_ge(*signal("at_pt", 8))
                pe.wait_ge(*signal("m_Mr", 1))
                spread("mm", 0, 8, Q[0:4], lambda j: None)

            s, n = SLAB0["wmqk"], ACC0["wmqk"]
            pe.wait_ge(*signal("keys", 1))
            acc_freed(pe, ACC0["wkv"] + 1)
            for m in range(MIX):
                u, odd = divmod(m, 2)
                if not odd and u < 8:
                    at_scores(u)
                if not odd and 1 <= u <= 8:
                    if u == 1:
                        pe.wait_ge(*signal("if_use", 1))
                    at_outputs(u - 1)
                if m == 0:
                    if_products()
                open_acc(n + m)
                product(s + m, 0, 8, n + m, ah, al, tokens=4 <= m < 8,
                        before=(lambda k: k == 4 and at_transposes(u)) if odd and u < 8 else None)
                if m == 0:
                    if_transposes()
                elif m == 17:
                    m_spread()

            def m_scores(h):
                p0 = 64 * (h % 2)
                pe.wait_ge(*signal("m_qk", 1))
                if h < 4:
                    pe.wait_ge(*signal("m_D", 4 * (h + 1)))
                else:
                    pe.wait_ge(*signal("m_S", h - 3))
                bank = Q[h % 4]
                for b in range(TB):
                    ks = qk[p0:p0 + 64, 4 + h // 2, b * P:(b + 1) * P]
                    qs = qk[p0:p0 + 64, h // 2, b * P:T]
                    ins = mm(bank[:, b * 256:b * 256 + T - b * P], ks, qs, start=b == 0, stop=True, skip_group_check=True)
                ins.then_inc(S("m_qkT"), 1)

            def m_numerators(h):
                pe.wait_ge(*signal("m_S", max(h + 1, h // 2 + 5)))
                bank = Q[h // 2]
                for b in range(TB):
                    sc_ = wm[:, h, b * 256:b * 256 + T - b * P]
                    ins = mm(bank[:, (h % 2) * T + b * P:(h % 2) * T + T], mv[:, b, h * P:(h + 1) * P], sc_,
                             start=b == 0 and h % 2 == 0, stop=b == 1, skip_group_check=True)
                    if h == 0 and b == 0:
                        pe.wait_ge(*signal("m_acolr", 1))
                    den = mm(Q[5][0:8, b * P:T], hot(h), sc_, start=h == 0 and b == 0, stop=h == 7 and b == 1,
                             skip_group_check=True)
                den.then_inc(S("m_num"), 1)

            def attention_projection(k):
                open_acc(ACC0["pa"] + k)
                product(SLAB0["pa"] + k, 0, 8, ACC0["pa"] + k, ah, al)

            for h in range(4):
                m_scores(h)
            pe.wait_ge(*signal("at_lo", 4))
            attention_projection(0)
            for h in range(4, 8):
                m_scores(h)
            for h in range(8):
                m_numerators(h)
            attention_projection(1)
            head_sums("m", sq, 8, Q[4], 0, True)
            attention_projection(2)
            spread("mf", 0, 8, Q[0:4], lambda j: pe.wait_ge(*signal("m_r", 1)))
            attention_projection(3)
            pe.wait_ge(*signal("mo_lo", 4))
            two("pm", bh, bl)
            pe.wait_ge(*signal("mg_lo", 4))
            two("wo", ch, cl)

            feed_forward("f2u", "f2d", "n3")

            opening("w2", "n5", ah, al)
            s, n = SLAB0["w2"], ACC0["w2"]

            def mem_rows(k):
                if k == 4:
                    pe.wait_ge(*signal("mem_in", 16))
                    pe.wait_ge(*signal("la_sd", 1))
                    transpose_in(memraw, "mem_ps", Q[2:6])

            for k in range(2, 8):
                open_acc(n + k)
                product(s + k, 0, 8, n + k, ah, al, tokens=k in (4, 5), before=mem_rows if k == 6 else None)
                if k == 2:
                    pe.wait_ge(*signal("la_sq", 2))
                    mm(Q[3][:, 0:T], ones, sq[:, 2, 0:T], start=True, stop=False, skip_group_check=True)
                    mm(Q[3][:, 0:T], ones, sq[:, 2, T:512], start=False, stop=False, skip_group_check=True)
                    mm(Q[3][:, T:512], ones, sq[:, 3, 0:T], start=False, stop=True, skip_group_check=True).then_inc(S("la_sum"), 1)
                    for c in range(DC):
                        ins = mm(Q[2][0:16, 0:T], walr[:, c, :], xT[:, c, :], start=c == 0, stop=c == DC - 1)
                    ins.then_inc(S("alr_ps"), 1)
                elif k == 4:
                    pe.wait_ge(*signal("alr", 1))
                    for c in range(2):
                        ins = mm(Q[1][:, c * T:(c + 1) * T], w2g[0:16, c * P:(c + 1) * P], alr,
                                 start=c == 0, stop=True, skip_group_check=True)
                    ins.then_inc(S("gl_z"), 1)

            pe.wait_ge(*signal("la_lo", 3))
            s, n = SLAB0["uq"], ACC0["uq"]
            lo_ready(pe, s, 0, 1)
            for j in range(4):
                open_acc(n + j)
                for c in range(2):
                    for k in range(2):
                        w = slice(k * 1024 + (2 * j + c) * P, k * 1024 + (2 * j + c + 1) * P)
                        dst = L[(n + j) % 2][:, c * T:(c + 1) * T]
                        mm(dst, wh[:, s % 2, w], cqh[:, k, :], start=k == 0 and c == 0, stop=False, skip_group_check=True)
                        mm(dst, wh[:, s % 2, w], cql[:, k, :], start=False, stop=False, skip_group_check=True)
                        ins = mm(dst, wl[:, s % 2, w], cqh[:, k, :], start=False, stop=k == 1, skip_group_check=True)
                if j < 3:
                    ins.then_inc(S("uq_ps"), 1)
                else:
                    ins.then_inc(S("w_used"), 2)

            open_acc(ACC0["xk0"])
            product(SLAB0["xk0"], 0, 8, ACC0["xk0"], ah, al, before=normed_input("n7"))
            norm_sums("n7")

            s, n = SLAB0["ukv"], ACC0["ukv"]
            lo_ready(pe, s, 0, 1)
            for j in range(4):
                open_acc(n + j)
                for c in range(2):
                    w = slice((2 * j + c) * P, (2 * j + c + 1) * P)
                    dst = L[(n + j) % 2][:, c * T:(c + 1) * T]
                    mm(dst, wh[:, s % 2, w], cqh[:, 2, :], start=c == 0, stop=False, skip_group_check=True)
                    mm(dst, wh[:, s % 2, w], cql[:, 2, :], start=False, stop=False, skip_group_check=True)
                    ins = mm(dst, wl[:, s % 2, w], cqh[:, 2, :], start=False, stop=True, skip_group_check=True)
                ins.then_inc(S("uk_ps"), 1)
            vh = wh[:, s % 2, 0:1024].rearrange("p (h c) -> p h c", h=8)[:, :, 64:128]
            vl = wl[:, s % 2, 0:1024].rearrange("p (h c) -> p h c", h=8)[:, :, 64:128]
            for b in range(TB):
                open_acc(n + 4 + b)
                t = slice(b * P, (b + 1) * P)
                dst = L[(n + 4 + b) % 2][:, :]
                mm(dst, cqh[:, 2, t], vh, start=True, stop=False)
                mm(dst, cql[:, 2, t], vh, start=False, stop=False)
                ins = mm(dst, cqh[:, 2, t], vl, start=False, stop=True)
                if b == 0:
                    ins.then_inc(S("uv_ps"), 1)
                else:
                    ins.then_inc(S("w_used"), 2)

            pe.wait_ge(*signal("gl_ke", 1))
            for b in range(TB):
                for c in range(2):
                    ins = nc.tensor.transpose(Q[1][:, b * 256 + c * P:b * 256 + (c + 1) * P], ke[:, c, b * P:(b + 1) * P], ident)
            ins.then_inc(S("gl_keT"), 1)
            pe.wait_ge(*signal("n7_sq", 4))
            for c in range(2):
                for b in range(TB):
                    for e in range(2):
                        p0 = 64 * e
                        t = slice(b * P, (b + 1) * P)
                        ins = mm(Q[2 + e][:, c * 256 + b * P:c * 256 + (b + 1) * P], ki[p0:p0 + 64, c, t], qd[p0:p0 + 64, c, t],
                                 start=c == 0 and b == 0, stop=True, skip_group_check=True)
            ins.then_inc(S("gl_att"), 1)

            head_sums("mq", sq, 8, Q[4], 0, True, rows=96)
            pe.wait_ge(*signal("kpe_sq", 1))
            mm(Q[4][0:8, T:512], ones[64:96, 0:8], kr[64:96, 1, :], start=False, stop=False, skip_group_check=True)
            head_sums("mk", xn[:, :, :].rearrange("p (j c) t -> p j (c t)", c=2), 8, Q[4], T, False, rows=64)

            def gl_increment(k):
                p0 = 64 * (k % 2)
                bank = (Q[5], Q[1], Q[2])[k]
                for c in range(2):
                    ins = mm(bank[:, c * 256:(c + 1) * 256], ketok[p0:p0 + 64, k // 2, c * P:(c + 1) * P],
                             gv[p0:p0 + 64, k // 2, c * 256:(c + 1) * 256], start=c == 0, stop=True, skip_group_check=True)
                ins.then_inc(S("gl_dS"), 1)

            pe.wait_ge(*signal("gl_ketok", 1))
            gl_increment(0)
            gl_increment(1)

            open_acc(ACC0["xk1"])
            product(SLAB0["xk1"], 0, 8, ACC0["xk1"], ah, al, before=late("n7"))

            pe.wait_ge(*signal("gl_am", 2))
            gl_increment(2)
            pe.wait_ge(*signal("gl_S", 3))
            for h in range(4):
                c, e = h // 2, h % 2
                p0 = 64 * e
                bank = (Q[3], Q[5])[e]
                for b in range(TB):
                    mm(bank[:, c * T + b * P:c * T + (b + 1) * P], gv[:, b, h * P:(h + 1) * P],
                       att[:, e, c * 256 + b * P:c * 256 + (b + 1) * P], start=c == 0 and b == 0, stop=False, skip_group_check=True)
                for k in range(1, 4):
                    ins = mm(bank[:, c * T + k * 64:c * T + (k + 1) * 64], stt_[p0:p0 + 64, k - 1, c, :],
                             qd[p0:p0 + 64, c, k * 64:(k + 1) * 64], start=False, stop=True, skip_group_check=True)
            ins.then_inc(S("gl_o"), 1)

            spread("mqf", 0, 8, Q[1:3], lambda j: (pe.wait_ge(*signal("ml_r", 1)),
                                                       j >= 2 and pe.wait_ge(*signal("mqf_use", j - 1))))
            pe.wait_ge(*signal("n7_rs", 1))
            spread("mkf", T, 8, (Q[4], Q[0]), lambda j: j >= 2 and pe.wait_ge(*signal("mkf_use", j - 1)))
            pe.wait_ge(*signal("gl_or", 1))
            head_sums("gl", sq, 4, Q[3], 0, True)

            m_sc, m_tp, m_out = attention(
                "ml", [1, 2] * 2,
                lambda u, h: (qh[0:96, 4 * (u // 2) + h, (u % 2) * P:(u % 2 + 1) * P],
                              kh[0:96, 4 * (u // 2) + h, 0:(u % 2 + 1) * P]),
                prob2, probT2,
                lambda u, b, h: vm[:, b, (4 * (u // 2) + h) * 64:(4 * (u // 2) + h + 1) * 64],
                [(64 * (h % 2), 64 * (h % 2) + 64, (h // 2) * P, [h]) for h in range(4)])

            def mem_values(k):
                open_acc(ACC0["xv"] + k)
                product(SLAB0["xv"] + k, 0, 8, ACC0["xv"] + k, ah, al, tokens=True)

            pe.wait_ge(*signal("ml_k", 1))
            m_sc(0)
            mem_values(0)
            pe.wait_ge(*signal("gl_r", 1))
            m_tp(0)
            m_sc(1)
            spread("gf", 0, 4, (Q[5], Q[4]), lambda j: None)
            mem_values(1)
            pe.wait_ge(*signal("go_y", 2))
            m_out(0)
            m_tp(1)
            pe.wait_ge(*signal("ml_k", 2))
            m_sc(2)
            m_out(1)
            m_tp(2)
            m_sc(3)
            m_out(2)
            m_tp(3)
            m_out(3)

            s, n = SLAB0["wo2"], ACC0["wo2"]
            for k in range(4):
                open_acc(n + k)
                product(s + k, 0, 8, n + k, ah, al, before=None if k else lambda c: c % 2 == 0 and
                        pe.wait_ge(*signal("go_lo" if c < 4 else "lo_lo", c // 2 % 2 + 1)))

            opening("xq", "n6", mh, ml)
            head_sums("xx", sq, 8, Q[1], 0, True)
            spread("xf", 0, 8, Q[2:4], lambda j: (pe.wait_ge(*signal("xx_r", 1)),
                                                       j >= 2 and pe.wait_ge(*signal("xf_use", j - 1))))
            pe.wait_ge(*signal("xf_use", 4))
            in_turn(2, *attention("xa", [2, 2],
                      lambda u, h: (xq[:, h, u * P:(u + 1) * P], xq[:, 4 + h, :]),
                      prob3, probT3, lambda u, b, h: xv[:, b, h * P:(h + 1) * P],
                      [(0, P, h * P, [h]) for h in range(4)]))
            pe.wait_ge(*signal("xo_lo", 2))
            two("xo", mh, ml, nk=4)
            feed_forward("f3u", "f3d", "n8")
            for b in range(TB):
                for g in range(2):
                    if b == 0:
                        acc_freed(pe, ACC0["f3d"] + 2 * g)
                        acc_freed(pe, ACC0["f3d"] + 2 * g + 1)
                    for c in range(4):
                        ins = nc.tensor.transpose(Q[2 * b + g][:, c * P:(c + 1) * P],
                                                  xT[:, 4 * g + c, b * P:(b + 1) * P], ident)
                    ins.then_inc(S("res_ps"), 1)

        @block.scalar
        def _(act):
            A_ = nc.scalar.activation

            def norm_parts(st, g, ready, src=xT, xh=ah):
                for j in range(4):
                    ready(act, j)
                    for c in (2 * j, 2 * j + 1):
                        ins = A_(xh[:, c, :], src[:, c, :], ACT.Copy, scale=col(g + c))
                    ins.then_inc(S(st + "_hi"), 1)
                    ins = A_(sq[:, j, :], pairs(src, j), ACT.Square, scale=1.0 / 32)
                    if st == "n5":
                        for c in (2 * j, 2 * j + 1):
                            ins = A_(xn[:, c, :], src[:, c, :], ACT.Square, scale=col(V_FIN32 + c))
                    ins.then_inc(S(st + "_sq"), 1)

            def norm_root(st):
                if st == "n5":
                    act.wait_ge(*signal("n5_v", 1))
                    A_(root[:, 0:4], vv[:, 0:4], ACT.Sqrt).then_inc(S(st + "_sd"), 1)
                else:
                    act.wait_ge(*signal(st + "_ss", 1))
                    A_(root[:, 0:2], Q[0][:, T:T + 2], ACT.Sqrt, bias=eps).then_inc(S(st + "_sd"), 1)

            def from_accs(name):
                n = ACC0[name]
                return lambda e, j: acc_freed(e, n + j)

            def stage_loop(name, nslabs, evac, st=None):
                s, n = SLAB0[name], ACC0[name]

                def body(i, last):
                    for r in range(2):
                        if last and r == 1:
                            split_hi(act, s + 2 * i + 2)
                        else:
                            split_hi(act, s + r + 1, i)
                        if st is not None and isinstance(i, int) and i + r == 0:
                            norm_root(st)
                        if evac is not None:
                            slab_used(act, s + r, i)
                            evac(i, r)
                looped(act, nslabs // 2, body, peel=st is not None and nslabs > 2)

            def feed_forward(up, down, st, conv=False, then=None):
                s, n = SLAB0[up], ACC0[up]

                def body(i, last):
                    if last:
                        split_hi(act, s + 2 * i + 2)
                    else:
                        split_hi(act, s + 2, i)
                    if conv:
                        act.wait_ge(*signal(up + "_cv", 6 * i + 6))
                        A_(sil[:, :], gcv[:, :], ACT.Silu).then_inc(S(up + "_si"), 1)
                    else:
                        acc_freed(act, n, i)
                        A_(sil[:, :], sil[:, :], ACT.Silu).then_inc(S(up + "_si"), 1)
                    if last:
                        split_hi(act, s + 2 * i + 3)
                    else:
                        split_hi(act, s + 3, i)
                    acc_freed(act, n + 1, i)
                    A_(rpair(hh, i), hid[:, :], ACT.Copy).then_inc(S(up + "_hh"), 1)
                    if then is not None and isinstance(i, int) and i == 0:
                        then()
                split_hi(act, s + 1)
                norm_root(st)
                looped(act, FP, body, peel=then is not None)
                s = SLAB0[down]
                for q in range(4):
                    if q > 0:
                        split_hi(act, s + 2 * q + 1)
                    split_hi(act, s + 2 * q + 2)

            def attention(st, units, prob, probT, sinks=False):
                def exps(u):
                    for h in range(4):
                        act.wait_ge(*signal(st + "_mx", 4 * u + h + 1))
                        w = units[u] * P
                        A_(prob[:, u % 2, h, 0:w], prob[:, u % 2, h, 0:w], ACT.Exp, bias=rmx[:, u % 2, h:h + 1],
                           scale=-1.0, accum_out=rsm[:, u % 2, h:h + 1]).then_inc(S(st + "_ex"), 1)
                    if sinks:
                        act.wait_ge(*signal(st + "_sk", u + 1))
                        A_(rs2[:, u % 2, :], rs2[:, u % 2, :], ACT.Exp).then_inc(S(st + "_se"), 1)

                def transposed(u):
                    act.wait_ge(*signal(st + "_tp", u + 1))
                    if u >= 1:
                        act.wait_ge(*signal(st + "_pv", u))
                    for b in range(units[u]):
                        ins = A_(probT[:, b, :], Q[2 + b][:, :], ACT.Copy)
                    ins.then_inc(S(st + "_pt"), 1)
                return exps, transposed

            def in_turn(units, exps, transposed):
                exps(0)
                for u in range(units):
                    if u + 1 < units:
                        exps(u + 1)
                    transposed(u)

            def x_ready(e, j):
                e.wait_ge(*signal("x_ok", j + 1))

            act.dma_start(g1raw[:, :], A["ffn1_norm"][0].rearrange("(c p) -> c p", p=P)).then_inc(S("g1_in"), 16)
            split_hi(act, 0)
            act.wait_ge(*signal("g1_ok", 1))
            norm_parts("n1", V_FFN1, x_ready)
            win = A["w_in"][0].rearrange("(k p) c -> p k c", p=P)
            win2 = A["w_in_2"][0].rearrange("(k p) c -> p k c", p=P)

            def small(dst, src):
                act.dma_start(dst, src).then_inc(S("small_in"), 16)

            small(bav[:, :], A["b_in"][:, I_AV:I_AV + 256].broadcast_to([P, 256]))
            small(bmv[:, :], A["b_in"][:, I_MV:I_MV + 1024].broadcast_to([P, 1024]))
            small(nsink[:, 0:16], A["attn_sinks"].broadcast_to([P, 16]))
            small(posi[:, :], A["positions_2"].broadcast_to([P, T]))
            small(wif[:, :, :], win[:, :, I_MI:I_MI + 16])
            small(walr[:, :, :], win2[:, :, J_ALR:J_ALR + 16])
            small(w2g[:, :], A["gla_gate_w2_2"][0])
            small(bif[:, 0:1], A["b_in"][0, I_MI:I_MI + 8].rearrange("(p a) -> p a", a=1))
            small(bif[:, 1:2], A["b_in"][0, I_MI + 8:I_MI + 16].rearrange("(p a) -> p a", a=1))
            act.wait_ge(*signal("consts", 16))

            def sines():
                act.wait_ge(*signal("angles", 1))
                A_(rope_c[64:P, :], rope_c[64:P, :], ACT.Sin)
                A_(rope_s[64:P, :], rope_s[64:P, :], ACT.Sin).then_inc(S("sines"), 1)
            feed_forward("f1u", "f1d", "n1", then=sines)
            norm_parts("n2", V_MIX, from_accs("f1d"))
            stage_loop("wq", 4, None, st="n2")
            stage_loop("wkv", 2, None)

            def sigmoid(m):
                name, v, dst, k = ("wmo", V_BMO, sigo, m - 8) if m < 12 else ("wg", V_BG, gate, m - 12)
                acc_freed(act, ACC0[name] + k)
                for half in range(2):
                    c = 2 * k + half
                    ins = A_(dst[:, c, :], stmp[:, k % 2, half * T:(half + 1) * T], ACT.Sigmoid, bias=col(v + c))
                ins.then_inc(S("sig"), 1)

            exps, transposed = attention("at", [1, 2] * 4, prob1, probT1, sinks=True)
            s_mix = SLAB0["wmqk"]
            for m in range(MIX):
                u, odd = divmod(m, 2)
                split_hi(act, s_mix + m + 1)
                if not odd and u < 8:
                    exps(u)
                if m >= 9:
                    sigmoid(m - 1)
                if odd and u < 8:
                    transposed(u)
                if m == 1:
                    act.wait_ge(*signal("if_T", 1))
                    act.wait_ge(*signal("if_b", 1))
                    A_(ti[:, 0:T], Q[4][0:8, 0:T], ACT.Tanh, bias=bif[:, 2:3], scale=1.0 / 15)
                    A_(ti[:, T:512], Q[4][0:8, T:512], ACT.Tanh, bias=bif[:, 3:4], scale=1.0 / 15).then_inc(S("if_use"), 1)
                    act.wait_ge(*signal("if_use", 1))
                    A_(lse[:, :], ti[:, T:512], ACT.Exp, scale=-15.0).then_inc(S("m_e"), 1)
                    act.wait_ge(*signal("m_e", 1))
                    A_(lse[:, :], lse[:, :], ACT.Ln, bias=1.0).then_inc(S("m_e"), 1)
                elif m == 17:
                    act.wait_ge(*signal("conv", 32))
                    for j in range(4):
                        ins = A_(qk[:, 2 * j:2 * j + 2, :], qk[:, 2 * j:2 * j + 2, :], ACT.Silu)
                    ins.then_inc(S("m_qk"), 1)
                elif m == 18:
                    act.wait_ge(*signal("m_gm", 1))
                    A_(en[:, :], gm[:, :], ACT.Exp).then_inc(S("m_en"), 1)

            def m_weights(j):
                act.wait_ge(*signal("m_D", 4 * j + 4))
                v = wm[:, 2 * j:2 * j + 2, :]
                A_(v, v, ACT.Exp, scale=-1.0).then_inc(S("m_w"), 1)

            m_weights(0)
            m_weights(1)
            slab_used(act, s_mix + MIX - 1)
            for j in range(4):
                act.wait_ge(*signal("at_yo", 2 * j + 2))
                A_(pairs(ah, j), pairs(aq, j), ACT.Copy).then_inc(S("at_hi"), 1)
            m_weights(2)
            m_weights(3)
            sigmoid(MIX - 1)
            s = SLAB0["pa"]
            split_hi(act, s + 1)
            split_hi(act, s + 2)
            for j in range(4):
                act.wait_ge(*signal("m_nu", j + 1))
                A_(sq[:, j, :], pairs(xn, j), ACT.Square).then_inc(S("m_hs"), 1)
            split_hi(act, s + 3)
            act.wait_ge(*signal("m_v", 1))
            A_(gm[:, :], gm[:, :], ACT.Sqrt, bias=eps[0:8, :]).then_inc(S("m_sd"), 1)
            split_hi(act, s + 4)
            for j in range(4):
                act.wait_ge(*signal("mo_y", j + 1))
                A_(pairs(bh, j), pairs(xn, j), ACT.Copy).then_inc(S("mo_hi"), 1)
            s = SLAB0["pm"]
            for k in range(4):
                split_hi(act, s + k + 1)
                act.wait_ge(*signal("mg", k + 1))
                A_(pairs(ch, k), mgs[:, :], ACT.Copy).then_inc(S("mg_hi"), 1)
            stage_loop("wo", 4, None)
            norm_parts("n3", V_FFN2, from_accs("wo"))
            feed_forward("f2u", "f2d", "n3")
            norm_parts("n5", V_MIX2, from_accs("f2d"))

            s, n = SLAB0["w2"], ACC0["w2"]
            for k in range(8):
                split_hi(act, s + k + 1)
                if k == 0:
                    norm_root("n5")
                elif k == 2:
                    acc_freed(act, n)
                    A_(sq[:, 2, :], pairs(cq, 0), ACT.Square).then_inc(S("la_sq"), 1)
                    acc_freed(act, n + 1)
                    A_(sq[:, 3, 0:T], ckv[:, :], ACT.Square).then_inc(S("la_sq"), 1)
                    A_(kr[64:96, 1, :], kpe[64:96, :], ACT.Square).then_inc(S("kpe_sq"), 1)
                elif k == 3:
                    act.wait_ge(*signal("la_sum", 1))
                    A_(sq[:, 0, 0:T], Q[3][:, 0:T], ACT.Sqrt, bias=eps, scale=1.0 / 256)
                    A_(sq[:, 0, T:512], Q[3][:, T:512], ACT.Sqrt, bias=eps, scale=1.0 / P).then_inc(S("la_sd"), 1)
                elif k == 4:
                    act.wait_ge(*signal("la_n", 3))
                    A_(cqh[:, 0:2, :], cq[:, :, :], ACT.Copy).then_inc(S("la_hi"), 1)
                    A_(cqh[:, 2, :], ckv[:, :], ACT.Copy).then_inc(S("la_hi"), 1)
                elif k == 5:
                    act.wait_ge(*signal("gl_zr", 1))
                    A_(lg[:, :], zg[:, :], ACT.Abs).then_inc(S("gl_l"), 1)
                    act.wait_ge(*signal("gl_l", 1))
                    A_(lg[:, :], lg[:, :], ACT.Exp, scale=-1.0).then_inc(S("gl_l"), 1)
                    act.wait_ge(*signal("gl_l", 2))
                    A_(lg[:, :], lg[:, :], ACT.Ln, bias=1.0).then_inc(S("gl_l"), 1)
                elif k == 6:
                    act.wait_ge(*signal("gl_cum", 2))
                    ends = cum[:, :].rearrange("p (n c) -> p n c", n=8)[:, :, 63]
                    A_(dec[:, :], ends, ACT.Exp, scale=1.0 / 16)
                    A_(lg[:, :], cum[:, :], ACT.Exp, scale=1.0 / 16).then_inc(S("gl_e"), 1)
                    act.wait_ge(*signal("gl_e", 1))
                    act.wait_ge(*signal("gl_d", 1))
                    A_(cum[:, :], cum[:, :], ACT.Exp, scale=-1.0 / 16).then_inc(S("gl_e"), 1)
                    A_(zg[:, :], zg[:, :], ACT.Exp, scale=-1.0 / 16).then_inc(S("gl_e"), 1)
                elif k == 7:
                    acc_freed(act, n + 6)
                    A_(pairs(sog, 0), stmp[:, 0, :], ACT.Silu).then_inc(S("sog"), 1)
            slab_used(act, s + 7)
            split_hi(act, SLAB0["xk0"])
            for j in range(4):
                act.wait_ge(*signal("mem_ps", j + 1))
                for c in range(2):
                    ins = A_(ah[:, 2 * j + c, :], Q[2 + j][:, c * T:(c + 1) * T], ACT.Copy, scale=col(V_MEM + 2 * j + c))
                ins.then_inc(S("n7_hi"), 1)
                A_(sq[:, j, :], Q[2 + j][:, :], ACT.Square, scale=1.0 / 32).then_inc(S("n7_sq"), 1)
            acc_freed(act, n + 7)
            A_(pairs(sog, 1), stmp[:, 1, :], ACT.Silu).then_inc(S("sog"), 1)
            split_hi(act, SLAB0["ukv"])
            act.wait_ge(*signal("n7_ss", 1))
            for j in range(4):
                acc_freed(act, ACC0["uq"] + j)
                A_(sq[0:96, j, :], qh[0:96, 2 * j:2 * j + 2, :].rearrange("p c t -> p (c t)"), ACT.Square)\
                    .then_inc(S("mq_hs"), 1)
            split_hi(act, SLAB0["xk1"])
            act.wait_ge(*signal("gl_keT", 1))
            A_(ketok[:, :, :].rearrange("p b c -> p (b c)"), Q[1][:, :], ACT.Copy).then_inc(S("gl_ketok"), 1)
            for j in range(4):
                acc_freed(act, ACC0["ukv"] + j)
                A_(xn[0:64, 2 * j:2 * j + 2, :], kh[0:64, 2 * j:2 * j + 2, :], ACT.Square).then_inc(S("mk_hs"), 1)
            norm_root("n7")
            act.wait_ge(*signal("mk_ss", 1))
            A_(r8[:, :], Q[4][0:8, :], ACT.Sqrt, bias=eps[0:8, :], scale=1.0 / 96).then_inc(S("ml_sd"), 1)
            split_hi(act, SLAB0["xv"])
            split_hi(act, SLAB0["xv"] + 1)
            for j in range(2):
                act.wait_ge(*signal("gl_or", 1))
                A_(sq[:, j, :], pairs(xn, j), ACT.Square).then_inc(S("gl_hs"), 1)
            act.wait_ge(*signal("gl_ss", 1))
            A_(gs8[:, 0:T], Q[3][0:8, 0:T], ACT.Sqrt, bias=eps[0:8, :], scale=1.0 / P).then_inc(S("gl_sd"), 1)
            exps, transposed = attention("ml", [1, 2] * 2, prob2, probT2)
            s = SLAB0["wo2"]
            exps(0)
            transposed(0)
            split_hi(act, s)
            exps(1)
            split_hi(act, s + 1)
            transposed(1)
            exps(2)
            for j in range(2):
                act.wait_ge(*signal("go_y", j + 1))
                A_(pairs(ah, j), pairs(xn, j), ACT.Copy).then_inc(S("go_hi"), 1)
            transposed(2)
            exps(3)
            transposed(3)
            for j in range(2):
                act.wait_ge(*signal("ml_yo", 2 * j + 2))
                A_(pairs(ah, 2 + j), pairs(xn, 2 + j), ACT.Copy).then_inc(S("lo_hi"), 1)
            for k in range(1, 4):
                split_hi(act, s + k + 1)

            norm_parts("n6", V_XA, from_accs("wo2"), xh=mh)
            stage_loop("xq", 2, None, st="n6")
            act.wait_ge(*signal("xk_ok", 1))
            acc_freed(act, ACC0["xk1"])
            for j in range(4):
                if j < 2:
                    acc_freed(act, ACC0["xq"] + j)
                A_(sq[:, j, :], pairs(xq, j), ACT.Square).then_inc(S("xx_hs"), 1)
            act.wait_ge(*signal("xx_ss", 1))
            A_(sx8[:, 0:T], Q[1][0:8, 0:T], ACT.Sqrt, bias=eps[0:8, :], scale=1.0 / P).then_inc(S("xx_sd"), 1)
            in_turn(2, *attention("xa", [2, 2], prob3, probT3))
            for j in range(2):
                act.wait_ge(*signal("xa_yo", 2))
                A_(pairs(mh, j), pairs(xn, j), ACT.Copy).then_inc(S("xo_hi"), 1)
            stage_loop("xo", 4, None)
            norm_parts("n8", V_FFN3, from_accs("xo"))
            feed_forward("f3u", "f3d", "n8", conv=True)
            for k in range(2):
                act.wait_ge(*signal("res_ps", 2 * k + 1))
                A_(res[:, k, 0:512], Q[2 * k][:, :], ACT.Copy).then_inc(S("resa"), 1)

        @block.vector
        def _(dve):
            V = nc.vector
            steps = [0]

            def link(ins, n=1):
                ins.then_inc(S("dve_step"), 1)
                steps[0] += 1
                dve.wait_ge(*signal("dve_step", steps[0]))

            def row_parts(r, sig, o0=0):
                n = r.shape[1]
                link(V.tensor_copy(rh[:, o0:o0 + n], r))
                V.tensor_tensor(rl[:, o0:o0 + n], r, f(rh[:, o0:o0 + n]), SUB).then_inc(S(sig), 1)

            def norm_lows(st, g, src=xT, xh=ah, xl=al):
                for j in range(4):
                    dve.wait_ge(*signal(st + "_hi", j + 1))
                    for c in (2 * j, 2 * j + 1):
                        ins = V.scalar_tensor_tensor(xl[:, c, :], src[:, c, :], col(g + c), f(xh[:, c, :]), MUL, SUB)
                    ins.then_inc(S(st + "_lo"), 1)

            def norm_factor(st):
                n = 2
                if st == "n5":
                    n = 4
                    dve.wait_ge(*signal("n5_ss", 1))
                    link(V.tensor_scalar(vv[:, 2:4], Q[0][:, T:T + 2], EPS, None, ADD))
                    V.scalar_tensor_tensor(vv[:, 0:2], vv[:, 2:4], EPS, Q[0][:, T + 2:T + 4], MUL, ADD).then_inc(S("n5_v"), 1)
                dve.wait_ge(*signal(st + "_sd", 1))
                V.reciprocal(rcol[:, 0:n], root[:, 0:n]).then_inc(S(st + "_rc"), 1)
                dve.wait_ge(*signal(st + "_rc", 1))
                dve.wait_ge(*signal(st + "_sp", 1))
                if st == "n5":
                    V.tensor_copy(std[:, 0:T], Q[1][:, 0:T])
                V.tensor_copy(rstd[:, 0:T], Q[0][:, 0:T]).then_inc(S(st + "_rs"), 1)
                dve.wait_ge(*signal(st + "_rs", 1))

            def lows(st, src, xh, xl, n, j0=0):
                for j in range(n):
                    dve.wait_ge(*signal(st + "_hi", j + 1))
                    V.tensor_tensor(pairs(xl, j0 + j), pairs(src, j0 + j), f(pairs(xh, j0 + j)), SUB)\
                        .then_inc(S(st + "_lo"), 1)

            def stage_loop(name, nslabs, evac, st=None):
                s, n = SLAB0[name], ACC0[name]

                def body(i, last):
                    for r in range(2):
                        if last and r == 1:
                            split_lo(dve, s + 2 * i + 2)
                        else:
                            split_lo(dve, s + r + 1, i)
                        if st is not None and isinstance(i, int) and i + r == 0:
                            norm_factor(st)
                        evac(i, r)
                looped(dve, nslabs // 2, body, peel=st is not None and nslabs > 2)

            def feed_forward(up, down, st, conv=False, then=None):
                s, n = SLAB0[up], ACC0[up]

                def body(i, last):
                    slab_used(dve, s, i)
                    gdst = gpad[:, :, 2:T + 2] if conv else two_t(sil[:, :])
                    V.tensor_tensor(gdst, two_t(L[n % 2][:, :]), factor, MUL).then_inc(free_sem(n), 1)
                    if conv:
                        for j in range(3):
                            for m in range(2):
                                w = vec[:, bass.ds(V_FCW + j * FC + m + i * 2, 1)]
                                o, x = gcv[:, m * T:(m + 1) * T], gpad[:, m, j:j + T]
                                if j == 0:
                                    if m == 0:
                                        acc_freed(dve, n, i)
                                    ins = V.tensor_scalar(o, x, w, vec[:, bass.ds(V_FCB + m + i * 2, 1)], MUL, ADD)
                                else:
                                    dve.wait_ge(*signal(up + "_cv", 6 * i + 2 * j + m - 1))
                                    ins = V.scalar_tensor_tensor(o, x, w, o, MUL, ADD)
                                ins.then_inc(S(up + "_cv"), 1)
                    if last:
                        split_lo(dve, s + 2 * i + 2)
                    else:
                        split_lo(dve, s + 2, i)
                    slab_used(dve, s + 1, i)
                    dve.wait_ge(*signal(up + "_sr", i + 1))
                    V.tensor_tensor(hid[:, :], L[(n + 1) % 2][:, :], sil[:, :], MUL).then_inc(free_sem(n + 1), 1)
                    if last:
                        split_lo(dve, s + 2 * i + 3)
                    else:
                        split_lo(dve, s + 3, i)
                    dve.wait_ge(*signal(up + "_hh", i + 1))
                    V.tensor_tensor(rpair(hl, i), hid[:, :], f(rpair(hh, i)), SUB).then_inc(S(up + "_hl"), 1)
                    if then is not None and isinstance(i, int) and i == 0:
                        then()
                split_lo(dve, s + 1)
                norm_factor(st)
                looped(dve, FP, body, peel=then is not None)
                s, n = SLAB0[down], ACC0[down]
                for q in range(4):
                    if q > 0:
                        split_lo(dve, s + 2 * q + 1)
                    split_lo(dve, s + 2 * q + 2)
                    slab_used(dve, s + 2 * q + 1)
                    V.scalar_tensor_tensor(pairs(xT, q), L[(n + q) % 2][:, :], 1.0 if conv else 0.5, pairs(xT, q),
                                           MUL, ADD).then_inc(free_sem(n + q), 1)

            def add_to_x(name, s, n):
                def evac(i, r):
                    slab_used(dve, s + r, i)
                    V.tensor_tensor(rpair(xT, i * 2 + r), L[(n + r) % 2][:, :], rpair(xT, i * 2 + r), ADD)\
                        .then_inc(free_sem(n + r), 1)
                return evac

            def attention(st, units, prob, scale, mask, yout, sink=None):
                def maxima(u):
                    dve.wait_ge(*signal(st + "_sc", u + 1))
                    if u >= 2:
                        dve.wait_ge(*signal(st + "_tp", u - 1))
                    w = units[u] * P
                    for h in range(4):
                        V.tensor_tensor_reduce(out=prob[:, u % 2, h, 0:w], in0=Q[h % 2][:, (h // 2) * 256:(h // 2) * 256 + w],
                                               in1=mask(units[u]), scale=-scale, scalar=sink(u, h) if sink else 3.0e38,
                                               op0=ADD, op1=MIN, accum_out=rmx[:, u % 2, h:h + 1]).then_inc(S(st + "_mx"), 1)
                    if sink:
                        dve.wait_ge(*signal(st + "_mx", 4 * u + 4))
                        g = u // 2
                        V.tensor_tensor(rs2[:, u % 2, :], rmx[:, u % 2, :], nsink[:, 4 * g:4 * g + 4], SUB)\
                            .then_inc(S(st + "_sk"), 1)

                def divide(u):
                    w = units[u] * P
                    dve.wait_ge(*signal(st + "_ex", 4 * u + 4))
                    if sink:
                        dve.wait_ge(*signal(st + "_se", u + 1))
                        link(V.tensor_tensor(rsm[:, u % 2, :], rsm[:, u % 2, :], rs2[:, u % 2, :], ADD))
                    link(V.reciprocal(rin[:, u % 2, :], rsm[:, u % 2, :]))
                    for h in range(4):
                        V.tensor_scalar(prob[:, u % 2, h, 0:w], prob[:, u % 2, h, 0:w], rin[:, u % 2, h:h + 1], None, MUL)\
                            .then_inc(S(st + "_pn"), 1)

                def leave(u):
                    dve.wait_ge(*signal(st + "_pv", u + 1))
                    yout(u, Q[4 + u % 2]).then_inc(S(st + "_yo"), 1)
                return maxima, divide, leave

            def in_turn(units, maxima, divide, leave):
                maxima(0)
                for u in range(units):
                    if u + 1 < units:
                        maxima(u + 1)
                    divide(u)
                    if u >= 1:
                        leave(u - 1)
                leave(units - 1)

            dve.wait_ge(*signal("ident", 16))
            V.tensor_copy(idr[:, :], cst[0:8, C_ID:C_ID + 8]).then_inc(S("idr"), 1)
            dve.wait_ge(*signal("g1_ps", 1))
            V.tensor_copy(vec[:, 0:8], Q[4][:, 0:8]).then_inc(S("g1_ok"), 1)
            for j in range(4):
                dve.wait_ge(*signal("x_ps", j + 1))
                V.tensor_copy(pairs(xT, j), Q[j][:, :]).then_inc(S("x_ok"), 1)
            dve.wait_ge(*signal("g1_ok", 1))
            dve.wait_ge(*signal("x_ok", 4))
            split_lo(dve, 0)
            norm_lows("n1", V_FFN1)

            def narrow_inputs():
                dve.wait_ge(*signal("vec_ps", 1))
                V.tensor_copy(vec[:, 8:VEC0], Q[4][:, 8:VEC0])
                link(V.tensor_copy(vec[:, P:P + VEC1], Q[4][:, P:P + VEC1]))
                V.tensor_scalar(vec[:, V_FIN32:V_FIN32 + 8], vec[:, V_FINAL:V_FINAL + 8], 1.0 / 32, None, MUL)
                link(V.tensor_tensor(vec[:, V_MIX2:V_MIX2 + 8], vec[:, V_MIX2:V_MIX2 + 8], vec[:, V_FINAL:V_FINAL + 8], MUL))
                dve.wait_ge(*signal("small_in", 16 * SMALL_LOADS))
                for w, g in ((wif, V_MIX), (walr, V_MIX2)):
                    gc = vec[:, g:g + 8].rearrange("p (c a) -> p c a", a=1).broadcast_to([P, 8, 16])
                    V.tensor_tensor(w[:, :, :], w[:, :, :], gc, MUL).then_inc(S("narrow"), 1)
                V.tensor_scalar(bif[:, 2:4], bif[:, 0:2], 1.0 / 15, None, MUL).then_inc(S("if_b"), 1)
                V.tensor_scalar(nsink[:, 0:16], nsink[:, 0:16], -1.0, None, MUL)
                R = slice(64, P)
                TWO_PI = 2 * np.pi
                c1 = 6.28125
                c2 = float(np.float32(np.round((TWO_PI - c1) * 2 ** 21) / 2 ** 21))
                c3 = float(np.float32(TWO_PI - c1 - c2))
                MAGIC = 12582912.0
                link(V.tensor_copy(ang[R, :], posi[R, :]))
                link(V.tensor_scalar(ang[R, :], ang[R, :], cst[R, C_INV:C_INV + 1], None, MUL))
                link(V.tensor_scalar(turn[R, :], ang[R, :], float(1 / TWO_PI), MAGIC, MUL, ADD))
                link(V.tensor_scalar(turn[R, :], turn[R, :], MAGIC, None, SUB))
                for c in (c1, c2, c3):
                    link(V.scalar_tensor_tensor(ang[R, :], turn[R, :], -c, ang[R, :], MUL, ADD))
                link(V.tensor_scalar(quarter[R, :], ang[R, :], float(np.pi / 2), None, ADD))
                link(V.tensor_scalar(tmpr[R, :], quarter[R, :], float(np.pi), TWO_PI, ALU.is_gt, MUL))
                link(V.tensor_tensor(quarter[R, :], quarter[R, :], tmpr[R, :], SUB))
                BOUND = 3.1415925
                V.tensor_scalar(rope_c[R, :], quarter[R, :], BOUND, -BOUND, MIN, MAX)
                V.tensor_scalar(rope_s[R, :], ang[R, :], BOUND, -BOUND, MIN, MAX).then_inc(S("angles"), 1)

            feed_forward("f1u", "f1d", "n1", then=narrow_inputs)
            norm_lows("n2", V_MIX)

            def scaled_out(name, k, dst):
                slab_used(dve, SLAB0[name] + k)
                V.tensor_tensor(dst, two_t(L[(ACC0[name] + k) % 2][:, :]), factor, MUL).then_inc(free_sem(ACC0[name] + k), 1)

            def with_bias(name, dst, v):
                def evac(i, r):
                    k = 2 * i + r
                    scaled_out(name, k, dst(k))
                    acc_freed(dve, ACC0[name] + k)
                    for m in range(2):
                        ins = V.tensor_scalar(dst(k)[:, m, :], dst(k)[:, m, :], col(v + 2 * k + m), None, ADD)
                    ins.then_inc(S("biased"), 1)
                return evac

            def straight(name, nslabs, evac, st=None):
                for k in range(nslabs):
                    split_lo(dve, SLAB0[name] + k + 1)
                    if k == 0 and st is not None:
                        norm_factor(st)
                    evac(k // 2, k % 2)

            straight("wq", 4, with_bias("wq", lambda k: aq[:, 2 * k:2 * k + 2, :], V_BQ), st="n2")
            s, n = SLAB0["wkv"], ACC0["wkv"]
            split_lo(dve, s + 1)
            scaled_out("wkv", 0, two_t(stmp[:, 0, :]))
            acc_freed(dve, n)
            for c in range(2):
                for e in range(2):
                    for to in range(2):
                        ins = V.tensor_scalar(akd[64 * to:64 * to + 64, 2 * c + e, :],
                                              stmp[64 * e:64 * e + 64, 0, c * T:(c + 1) * T],
                                              col(V_BK + c, 64 * e, 64 * e + 64), None, ADD)
            ins.then_inc(S("keys"), 1)
            split_lo(dve, s + 2)
            slab_used(dve, s + 1)
            for b in range(TB):
                ins = V.scalar_tensor_tensor(av[:, b, :], L[(n + 1) % 2][:, b * 256:(b + 1) * 256], rcol[:, b:b + 1],
                                             bav[:, :], MUL, ADD)
            ins.then_inc(free_sem(n + 1), 1)

            def y_first(u, bank):
                g, blk = u // 2, u % 2
                return V.tensor_copy(aq[:, 2 * g:2 * g + 2, blk * P:(blk + 1) * P],
                                     bank[:, 0:256].rearrange("p (c q) -> p c q", c=2))

            maxima, divide, leave = attention(
                "at", [1, 2] * 4, prob1, 0.125,
                lambda b: cst[:, C_OWN:C_OWN + P] if b == 1 else cst[:, C_PREV:C_PREV + 256], y_first,
                sink=lambda u, h: nsink[:, 4 * (u // 2) + h:4 * (u // 2) + h + 1])

            conv_in = with_bias("wmqk", lambda k: pad[:, 2 * k:2 * k + 2, 3:T + 3], V_BMQK)

            def values_out(k):
                slab_used(dve, SLAB0["wmv"] + k)
                for b in range(TB):
                    ins = V.scalar_tensor_tensor(mv[:, b, k * 256:(k + 1) * 256],
                                                 L[(ACC0["wmv"] + k) % 2][:, b * 256:(b + 1) * 256],
                                                 rcol[:, b:b + 1], bmv[:, k * 256:(k + 1) * 256], MUL, ADD)
                ins.then_inc(free_sem(ACC0["wmv"] + k), 1)

            def for_sigmoid(m):
                name, k = ("wmo", m - 8) if m < 12 else ("wg", m - 12)
                if m >= 10:
                    dve.wait_ge(*signal("sig", m - 9))
                scaled_out(name, k, two_t(stmp[:, k % 2, :]))

            def conv(c):
                part = std[:, (c % 2) * T:(c % 2 + 1) * T]
                for j in range(4):
                    x, w = pad[:, c, j:j + T], col(V_MCONV + j * 8 + c)
                    if j == 0:
                        ins = V.tensor_scalar(part, x, w, None, MUL)
                    else:
                        dve.wait_ge(*signal("conv", 4 * c + j))
                        ins = V.scalar_tensor_tensor(pad[:, c, 3:T + 3] if j == 3 else part, x, w, part, MUL, ADD)
                    ins.then_inc(S("conv"), 1)

            def m_gates():
                dve.wait_ge(*signal("m_e", 2))
                link(V.tensor_tensor_scan(Gc[:, :], cst[0:8, C_ONE:C_ONE + 1].broadcast_to([8, T]), lse[:, :], 0.0, MUL, ADD))
                V.scalar_tensor_tensor(ai[:, :], ti[:, 0:T], 15.0, Gc[:, :], MUL, ADD).then_inc(S("m_a"), 1)
                dve.wait_ge(*signal("m_a", 1))
                V.tensor_tensor_scan(Mx[:, :], cst[0:8, C_ONE:C_ONE + 1].broadcast_to([8, T]), ai[:, :], 0.0, MUL, MAX)\
                    .then_inc(S("m_M"), 1)
                dve.wait_ge(*signal("m_M", 1))
                V.tensor_tensor(gm[:, :], Gc[:, :], Mx[:, :], SUB).then_inc(S("m_gm"), 1)

            def m_exponents(heads):
                for h in heads:
                    dve.wait_ge(*signal("mm_sp", h // 2 + 1))
                    for b in range(TB):
                        a = acol[:, b, h:h + 1]
                        V.tensor_scalar(wm[:, h, b * 256:b * 256 + T - b * P], Q[h // 2][:, (h % 2) * T + b * P:(h % 2) * T + T],
                                        a, a, MAX, SUB).then_inc(S("m_D"), 1)

            s_mix = SLAB0["wmqk"]
            for m in range(MIX):
                u, odd = divmod(m, 2)
                if not odd and u < 8:
                    maxima(u)
                if m == 0:
                    dve.wait_ge(*signal("if_ps", 1))
                    for b in range(TB):
                        ins = V.tensor_scalar(gtok[:, b, :], Q[5][:, b * 16:(b + 1) * 16], rcol[:, b:b + 1], None, MUL)
                    ins.then_inc(S("if_tok"), 1)
                split_lo(dve, s_mix + m + 1)
                if not odd and u < 8:
                    divide(u)
                if not odd and 1 <= u <= 8:
                    leave(u - 1)
                if m == 0:
                    dve.wait_ge(*signal("pad0", 1))
                if m < 4:
                    conv_in(m // 2, m % 2)
                elif m < 8:
                    values_out(m - 4)
                else:
                    for_sigmoid(m)
                if m == 3:
                    m_gates()
                    dve.wait_ge(*signal("biased", 8))
                elif 8 <= m < 16:
                    conv(m - 8)
                    if m == 8:
                        row_parts(Mx[:, :], "m_Mr")
                elif m == 18:
                    dve.wait_ge(*signal("m_acol", 1))
                    V.tensor_copy(acol[:, :, :].rearrange("p b h -> p (b h)"), Q[5][:, 0:16]).then_inc(S("m_acolr"), 1)
                    dve.wait_ge(*signal("m_acolr", 1))
                    m_exponents(range(0, 4))
                elif m == 19:
                    m_exponents(range(4, 8))

            def m_weighted(h):
                dve.wait_ge(*signal("m_qkT", h + 1))
                dve.wait_ge(*signal("m_mask", h // 2 + 1))
                V.scalar_tensor_tensor(wm[:, h, :], Q[h % 4][:, 0:384], 0.125, wm[:, h, :], MUL, MUL)\
                    .then_inc(S("m_S"), 1)

            def attention_out(k):
                slab_used(dve, SLAB0["pa"] + k)
                V.tensor_tensor(pairs(gate, k), L[(ACC0["pa"] + k) % 2][:, :], pairs(gate, k), MUL)\
                    .then_inc(free_sem(ACC0["pa"] + k), 1)

            lows("at", aq, ah, al, 4)
            for h in range(4):
                m_weighted(h)
            dve.wait_ge(*signal("sig", 12))
            split_lo(dve, SLAB0["pa"] + 1)
            attention_out(0)
            for h in range(4, 8):
                m_weighted(h)
            for j in range(4):
                dve.wait_ge(*signal("m_num", 2 * j + 2))
                V.tensor_copy(pairs(xn, j), Q[j][:, :]).then_inc(S("m_nu"), 1)
            split_lo(dve, SLAB0["pa"] + 2)
            dve.wait_ge(*signal("m_num", 8))
            dve.wait_ge(*signal("m_en", 1))
            link(V.scalar_tensor_tensor(rden[:, :], Q[5][0:8, 0:T], -1.0, en[:, :], MUL, MAX))
            link(V.tensor_tensor(rden[:, :], rden[:, :], Q[5][0:8, 0:T], MAX))
            link(V.reciprocal(rden[:, :], rden[:, :]))
            link(V.tensor_tensor(gm[:, :], rden[:, :], rden[:, :], MUL))
            attention_out(1)
            dve.wait_ge(*signal("m_ss", 1))
            V.scalar_tensor_tensor(gm[:, :], Q[4][0:8, 0:T], 1.0 / P, gm[:, :], MUL, MUL).then_inc(S("m_v"), 1)
            split_lo(dve, SLAB0["pa"] + 3)
            dve.wait_ge(*signal("m_sd", 1))
            link(V.reciprocal(en[:, :], gm[:, :]))
            link(V.tensor_tensor(rden[:, :], rden[:, :], en[:, :], MUL))
            row_parts(rden[:, :], "m_r")
            attention_out(2)
            for j in range(4):
                dve.wait_ge(*signal("mf_sp", j + 1))
                link(V.tensor_tensor(pairs(xn, j), Q[j][:, :], pairs(xn, j), MUL))
                for h in (2 * j, 2 * j + 1):
                    ins = V.scalar_tensor_tensor(xn[:, h, :], xn[:, h, :], col(V_HEAD + h), sigo[:, h, :], MUL, MUL)
                ins.then_inc(S("mo_y"), 1)
            split_lo(dve, SLAB0["pm"])
            lows("mo", xn, bh, bl, 4)
            attention_out(3)
            acc_freed(dve, ACC0["pa"] + 2)
            acc_freed(dve, ACC0["pa"] + 3)
            for k in range(4):
                s, n = SLAB0["pm"] + k, ACC0["pm"] + k
                split_lo(dve, s + 1)
                slab_used(dve, s)
                V.tensor_tensor(mgb[:, :], L[n % 2][:, :], pairs(gate, 4 + k), MUL).then_inc(free_sem(n), 1)
                acc_freed(dve, n)
                V.tensor_tensor(mgs[:, :], mgb[:, :], pairs(gate, k), ADD).then_inc(S("mg"), 1)
                dve.wait_ge(*signal("mg_hi", k + 1))
                V.tensor_tensor(pairs(cl, k), mgs[:, :], f(pairs(ch, k)), SUB).then_inc(S("mg_lo"), 1)
            stage_loop("wo", 4, add_to_x("wo", SLAB0["wo"], ACC0["wo"]))
            norm_lows("n3", V_FFN2)
            feed_forward("f2u", "f2d", "n3")
            norm_lows("n5", V_MIX2)

            s, n = SLAB0["w2"], ACC0["w2"]

            def acc(k):
                return L[(n + k) % 2]
            for k in range(8):
                split_lo(dve, s + k + 1)
                if k == 0:
                    norm_factor("n5")
                elif k == 3:
                    dve.wait_ge(*signal("alr_ps", 1))
                    V.tensor_tensor(alr, Q[2][0:16, 0:T], rstd[0:16, 0:T], MUL).then_inc(S("alr"), 1)
                elif k == 4:
                    dve.wait_ge(*signal("la_sd", 1))
                    link(V.reciprocal(sq[:, 1, :], sq[:, 0, :]))
                    for c in range(2):
                        V.scalar_tensor_tensor(cq[:, c, :], cq[:, c, :], col(V_QA + c), sq[:, 1, 0:T], MUL, MUL).then_inc(S("la_n"), 1)
                    V.scalar_tensor_tensor(ckv[:, :], ckv[:, :], col(V_KVA), sq[:, 1, T:512], MUL, MUL).then_inc(S("la_n"), 1)
                elif k == 5:
                    dve.wait_ge(*signal("gl_z", 1))
                    for c in range(2):
                        ins = V.tensor_scalar(zg[:, c * T:(c + 1) * T], Q[1][:, c * T:(c + 1) * T], col(V_GATEB + c), None, ADD)
                    ins.then_inc(S("gl_zr"), 1)
                    dve.wait_ge(*signal("la_hi", 2))
                    V.tensor_tensor(cql[:, 0:2, :], cq[:, :, :], f(cqh[:, 0:2, :]), SUB).then_inc(S("la_lo"), 2)
                    V.tensor_tensor(cql[:, 2, :], ckv[:, :], f(cqh[:, 2, :]), SUB).then_inc(S("la_lo"), 1)
                elif k == 6:
                    dve.wait_ge(*signal("gl_l", 3))
                    link(V.scalar_tensor_tensor(zg[:, :], zg[:, :], 0.0, lg[:, :], MIN, SUB))
                    for c in range(2):
                        V.tensor_tensor_scan(cum[:, c * T:(c + 1) * T], cst[:, C_RESET:C_RESET + T], zg[:, c * T:(c + 1) * T],
                                             0.0, MUL, ADD).then_inc(S("gl_cum"), 1)
                    dve.wait_ge(*signal("gl_cum", 2))
                    c8 = cum[:, :].rearrange("p (n c) -> p n c", n=8)
                    V.tensor_tensor(zg[:, :].rearrange("p (n c) -> p n c", n=8), c8, c8[:, :, 63:64].broadcast_to([P, 8, 64]), SUB)\
                        .then_inc(S("gl_d"), 1)
                elif k == 7:
                    dve.wait_ge(*signal("kpe_sq", 1))
                    dve.wait_ge(*signal("rope", 1))
                    V.tensor_copy(gk1[0:64, :], col(V_MLAK, 0, 64))
                    V.memset(gk1[64:96, :], 1.0)
                    link(V.tensor_scalar(kpe[64:P, :], kpe[64:P, :], col(V_MLAK, 64, P), None, MUL))
                    V.tensor_tensor(kr[64:96, 0, :], kpe[64:96, :], rope_c[64:96, :], MUL)
                    link(V.tensor_tensor(kr[64:96, 2, :], kpe[96:P, :], rope_s[96:P, :], MUL))
                    V.tensor_tensor(kr[64:96, 0, :], kr[64:96, 0, :], kr[64:96, 2, :], ADD).then_inc(S("k_rot"), 1)
                slab_used(dve, s + k)
                if k == 0:
                    ins = V.tensor_tensor(cq[:, :, :], two_t(acc(k)[:, :]), factor, MUL)
                elif k == 1:
                    V.tensor_tensor(kpe[64:P, :], acc(k)[64:P, T:512], rstd[64:P, 0:T], MUL)
                    ins = V.tensor_tensor(ckv[:, :], acc(k)[:, 0:T], rstd[:, 0:T], MUL)
                elif k == 2:
                    ins = V.scalar_tensor_tensor(gq[:, :, :], two_t(acc(k)[:, :]), 0.125, factor, MUL, MUL)
                elif k == 3:
                    ins = V.tensor_tensor(gk[:, :, :], two_t(acc(k)[:, :]), factor, MUL)
                elif k in (4, 5):
                    for b in range(TB):
                        ins = V.tensor_scalar(gv[:, b, (k - 4) * 256:(k - 3) * 256], acc(k)[:, b * 256:(b + 1) * 256],
                                              rcol[:, b:b + 1], None, MUL)
                else:
                    ins = V.tensor_tensor(two_t(stmp[:, k % 2, :]), two_t(acc(k)[:, :]), factor, MUL)
                ins.then_inc(free_sem(n + k), 1)

            def query_out(j):
                n_ = ACC0["uq"]
                if j < 3:
                    dve.wait_ge(*signal("uq_ps", j + 1))
                else:
                    slab_used(dve, SLAB0["uq"])
                V.tensor_copy(pairs(qh, j), L[(n_ + j) % 2][:, :]).then_inc(free_sem(n_ + j), 1)

            def memory_low(j):
                dve.wait_ge(*signal("n7_hi", j + 1))
                dve.wait_ge(*signal("n7_sq", j + 1))
                for c in range(2):
                    k = 2 * j + c
                    ins = V.scalar_tensor_tensor(al[:, k, :], Q[2 + j][:, c * T:(c + 1) * T], col(V_MEM + k), f(ah[:, k, :]), MUL, SUB)
                ins.then_inc(S("n7_lo"), 1)

            query_out(0)
            split_lo(dve, SLAB0["xk0"])
            query_out(1)
            memory_low(0)
            query_out(2)
            memory_low(1)
            query_out(3)
            memory_low(2)
            memory_low(3)
            split_lo(dve, SLAB0["ukv"])
            for k, (o, x, e) in enumerate(((qd, gq, lg), (ki, gk, cum), (ke, gk, zg))):
                dve.wait_ge(*signal("gl_e", k + 1))
                ins = V.tensor_tensor(o[:, :, :], x[:, :, :], two_t(e[:, :]), MUL)
            ins.then_inc(S("gl_ke"), 1)
            slab_used(dve, SLAB0["xk0"])
            V.tensor_copy(pairs(xq, 2), L[ACC0["xk0"] % 2][:, :]).then_inc(free_sem(ACC0["xk0"]), 1)
            n = ACC0["ukv"]
            for j in range(4):
                dve.wait_ge(*signal("uk_ps", j + 1))
                V.tensor_copy(kh[0:64, 2 * j:2 * j + 2, :].rearrange("p c t -> p (c t)"), L[(n + j) % 2][0:64, :])\
                    .then_inc(free_sem(n + j), 1)
            for b in range(TB):
                if b == 0:
                    dve.wait_ge(*signal("uv_ps", 1))
                else:
                    slab_used(dve, SLAB0["ukv"])
                V.tensor_copy(vm[:, b, :], L[(n + 4 + b) % 2][:, :]).then_inc(free_sem(n + 4 + b), 1)
            split_lo(dve, SLAB0["xk1"])
            dve.wait_ge(*signal("gl_att", 1))
            dve.wait_ge(*signal("att0", 1))
            gmask = cst[:, C_GLA:C_GLA + P].bitcast(i32).rearrange("p (a c) -> p a c", a=1).broadcast_to([P, 4, P])
            for e in range(2):
                V.copy_predicated(att[:, e, :].rearrange("p (a c) -> p a c", a=4), gmask,
                                  Q[2 + e][:, :].rearrange("p (a c) -> p a c", a=4)).then_inc(S("gl_am"), 1)

            def gl_state(k):
                dve.wait_ge(*signal("gl_dS", k + 1))
                bank = (Q[5], Q[1], Q[2])[k]
                if k >= 1:
                    dve.wait_ge(*signal("gl_S", k))
                for e in range(2):
                    p0 = 64 * e
                    for c in range(2):
                        o = stt_[p0:p0 + 64, k, c, :]
                        x = bank[p0:p0 + 64, c * 256 + e * P:c * 256 + (e + 1) * P]
                        if k == 0:
                            ins = V.tensor_copy(o, x)
                        else:
                            ins = V.scalar_tensor_tensor(o, stt_[p0:p0 + 64, k - 1, c, :], dec[p0:p0 + 64, 4 * c + k:4 * c + k + 1],
                                                         x, MUL, ADD)
                ins.then_inc(S("gl_S"), 1)

            gl_state(0)
            gl_state(1)
            norm_factor("n7")
            dve.wait_ge(*signal("ml_sd", 1))
            link(V.reciprocal(r8[:, :], r8[:, :]))
            row_parts(r8[:, :], "ml_r")
            V.tensor_tensor(xq[:, 4:6, :], xq[:, 4:6, :], factor, MUL).then_inc(S("xk_ok"), 1)
            slab_used(dve, SLAB0["xk1"])
            V.tensor_tensor(xq[:, 6:8, :], two_t(L[ACC0["xk1"] % 2][:, :]), factor, MUL).then_inc(free_sem(ACC0["xk1"]), 1)
            acc_freed(dve, ACC0["xk1"])
            gl_state(2)
            split_lo(dve, SLAB0["xv"])
            dve.wait_ge(*signal("gl_o", 1))
            for e in range(2):
                ins = V.tensor_copy(xn[:, e:4:2, :], (Q[3], Q[5])[e][:, :].rearrange("p (c t) -> p c t", c=2))
            ins.then_inc(S("gl_or"), 1)
            split_lo(dve, SLAB0["xv"] + 1)

            for part, t, g, banks in (("mqf", qh, col(V_MLAQ), Q[1:3]), ("mkf", kh, gk1[0:96, :], (Q[4], Q[0]))):
                if part == "mkf":
                    dve.wait_ge(*signal("k_fill", 1))
                for j in range(4):
                    dve.wait_ge(*signal(part + "_sp", j + 1))
                    rows = P if part == "mqf" else 96
                    V.scalar_tensor_tensor(t[0:rows, 2 * j:2 * j + 2, :], t[0:rows, 2 * j:2 * j + 2, :], g,
                                           two_t(banks[j % 2][0:rows, :]), MUL, MUL).then_inc(S(part + "_use"), 1)

            def rotate(g):
                a, b = qh[64:96, 4 * g:4 * g + 4, :], qh[96:P, 4 * g:4 * g + 4, :]
                tr = stmp[64:96, :, :].rearrange("p r (c t) -> p (r c) t", c=2)
                cosb = rope_c[64:96, :].rearrange("p (a t) -> p a t", a=1).broadcast_to([32, 4, T])
                sinb = rope_s[96:P, :].rearrange("p (a t) -> p a t", a=1).broadcast_to([32, 4, T])
                V.tensor_tensor(a, a, cosb, MUL)
                link(V.tensor_tensor(tr, b, sinb, MUL))
                V.tensor_tensor(a, a, tr, ADD).then_inc(S("ml_k"), 1)

            dve.wait_ge(*signal("mqf_use", 4))
            dve.wait_ge(*signal("sog", 2))
            rotate(0)

            def y_second(u, bank):
                g, blk = u // 2, u % 2
                return V.tensor_copy(xn[:, 4 + 2 * g:6 + 2 * g, blk * P:(blk + 1) * P],
                                     bank[:, 0:256].rearrange("p (c q) -> p c q", c=2))

            def memory_values(r):
                n_v, s_v = ACC0["xv"], SLAB0["xv"]
                slab_used(dve, s_v + r)
                for b in range(TB):
                    ins = V.tensor_scalar(xv[:, b, r * 256:(r + 1) * 256], L[(n_v + r) % 2][:, b * 256:(b + 1) * 256],
                                          rcol[:, b:b + 1], None, MUL)
                ins.then_inc(free_sem(n_v + r), 1)

            def final_normed(chunks):
                for c in chunks:
                    ins = V.scalar_tensor_tensor(xT[:, c, :], xT[:, c, :], col(V_FINAL + c), std[:, 0:T], MUL, MUL)
                ins.then_inc(S("final"), 1)

            maxima, divide, leave = attention(
                "ml", [1, 2] * 2, prob2, 96 ** -0.5,
                lambda b: cst[:, C_OWN2:C_OWN2 + P] if b == 1 else cst[:, C_OWN2 - P:C_OWN2 + P], y_second)
            maxima(0)
            dve.wait_ge(*signal("gl_sd", 1))
            link(V.reciprocal(gs8[:, T:512], gs8[:, 0:T]))
            row_parts(gs8[:, T:512], "gl_r")
            dve.wait_ge(*signal("ml_k", 1))
            rotate(1)
            divide(0)
            memory_values(0)
            maxima(1)
            dve.wait_ge(*signal("gl_or", 1))
            for j in range(2):
                dve.wait_ge(*signal("gf_sp", j + 1))
                link(V.tensor_tensor(pairs(xn, j), (Q[5], Q[4])[j][:, :], pairs(xn, j), MUL))
                V.scalar_tensor_tensor(pairs(xn, j), pairs(xn, j), col(V_GLA), pairs(sog, j), MUL, MUL).then_inc(S("go_y"), 1)
            divide(1)
            split_lo(dve, SLAB0["wo2"])
            memory_values(1)
            leave(0)
            maxima(2)
            split_lo(dve, SLAB0["wo2"] + 1)
            divide(2)
            leave(1)
            maxima(3)
            final_normed(range(0, 4))
            lows("go", xn, ah, al, 2)
            divide(3)
            leave(2)
            leave(3)
            dve.wait_ge(*signal("ml_yo", 4))
            lows("lo", xn, ah, al, 2, j0=2)
            final_normed(range(4, 8))
            dve.wait_ge(*signal("final", 2))
            s, n = SLAB0["wo2"], ACC0["wo2"]
            for k in range(4):
                if k > 0:
                    split_lo(dve, s + k + 1)
                add_to_x("wo2", s, n)(k // 2, k % 2)

            norm_lows("n6", V_XA, xh=mh, xl=ml)
            straight("xq", 2, lambda i, r: scaled_out("xq", r, xq[:, 2 * r:2 * r + 2, :]), st="n6")
            dve.wait_ge(*signal("xx_sd", 1))
            link(V.reciprocal(rx8[:, 0:T], sx8[:, 0:T]))
            row_parts(rx8[:, 0:T], "xx_r")
            acc_freed(dve, ACC0["xq"])
            acc_freed(dve, ACC0["xq"] + 1)
            for j in range(4):
                dve.wait_ge(*signal("xf_sp", j + 1))
                V.scalar_tensor_tensor(pairs(xq, j), pairs(xq, j), col(V_XQ if j < 2 else V_XK), Q[2 + j % 2][:, :], MUL, MUL)\
                    .then_inc(S("xf_use"), 1)

            def y_third(u, bank):
                return V.tensor_copy(xn[:, 0:4, u * P:(u + 1) * P], bank[:, :].rearrange("p (c q) -> p c q", c=4))
            in_turn(2, *attention("xa", [2, 2], prob3, 128 ** -0.5, lambda b: cst[:, C_ZERO:C_ZERO + 256], y_third))
            dve.wait_ge(*signal("xa_yo", 2))
            lows("xo", xn, mh, ml, 2)
            stage_loop("xo", 4, add_to_x("xo", SLAB0["xo"], ACC0["xo"]))
            norm_lows("n8", V_FFN3)
            dve.wait_ge(*signal("gpad0", 1))
            feed_forward("f3u", "f3d", "n8", conv=True)
            for k in range(2):
                dve.wait_ge(*signal("res_ps", 2 * k + 2))
                V.tensor_copy(res[:, k, 512:1024], Q[2 * k + 1][:, :]).then_inc(S("resd"), 1)

        @block.gpsimd
        def _(pool):
            G = nc.gpsimd
            def norm_pairs(st):
                for j in range(1, 4):
                    pool.wait_ge(*signal(st + "_sq", j + 1))
                    if j > 1:
                        pool.wait_ge(*signal(st + "_ps", j - 1))
                    G.tensor_tensor(sq[:, 0, :], sq[:, 0, :], sq[:, j, :], ADD).then_inc(S(st + "_ps"), 1)
                    if st == "n5":
                        if j > 1:
                            pool.wait_ge(*signal("n5_ps2", j - 1))
                        G.tensor_tensor(pairs(xn, 0), pairs(xn, 0), pairs(xn, j), ADD).then_inc(S("n5_ps2"), 1)

            def feed_forward(up):
                with pool.Fori(0, FP) as i:
                    pool.wait_ge(*signal(up + "_si", i + 1))
                    G.tensor_tensor(two_t(sil[:, :]), two_t(sil[:, :]), factor, MUL).then_inc(S(up + "_sr"), 1)

            norm_pairs("n1")
            feed_forward("f1u")
            norm_pairs("n2")
            pool.wait_ge(*signal("n2_ps", 3))
            pool.wait_ge(*signal("sines", 1))
            G.tensor_scalar(rope_s[64:P, :], rope_s[64:P, :], cst[64:P, C_SIGN:C_SIGN + 1], None, MUL).then_inc(S("rope"), 1)
            pool.wait_ge(*signal("rope", 1))
            pool.wait_ge(*signal("n2_ss", 1))
            G.memset(pad[:, :, 0:3], 0.0).then_inc(S("pad0"), 1)
            for j in range(4):
                pool.wait_ge(*signal("m_w", j + 1))
                for c in (0, 256):
                    v = wm[:, 2 * j:2 * j + 2, c:c + P]
                    ins = G.affine_select(out=v, in_=v, pattern=[[0, 2], [1, P]], compare_op=ALU.is_ge, fill=0.0,
                                          base=0, channel_multiplier=-1)
                ins.then_inc(S("m_mask"), 1)
            norm_pairs("n3")
            feed_forward("f2u")
            norm_pairs("n5")
            pool.wait_ge(*signal("n5_ss", 1))
            G.memset(att[:, :, :], 0.0).then_inc(S("att0"), 1)
            pool.wait_ge(*signal("k_rot", 1))
            pool.wait_ge(*signal("att0", 1))
            G.tensor_copy(kh[64:96, :, :], kr[64:96, 0:1, :].broadcast_to([32, 8, T])).then_inc(S("k_fill"), 1)
            pool.wait_ge(*signal("k_fill", 1))
            norm_pairs("n7")
            norm_pairs("n6")
            norm_pairs("n8")
            pool.wait_ge(*signal("n8_ss", 1))
            G.memset(gpad[:, :, 0:2], 0.0).then_inc(S("gpad0"), 1)
            feed_forward("f3u")


def kernel(**inputs):
    import concourse.bacc as _bacc
    from concourse.bass_utils import run_bass_kernel_spmd as _run

    nc = _bacc.Bacc("TRN2", target_bir_lowering=False, num_devices=1)
    arrays, A = {}, {}
    for name, a in inputs.items():
        a = np.ascontiguousarray(a)
        arrays[f"in_{name}"] = a
        A[name] = nc.dram_tensor(f"in_{name}", a.shape, mybir.dt.from_np(a.dtype), kind="ExternalInput").ap()
    c = shape_constants()
    arrays["shape_constants"] = c
    consts = nc.dram_tensor("shape_constants", c.shape, mybir.dt.float32, kind="ExternalInput").ap()
    out = nc.dram_tensor("out", (1, T, D), mybir.dt.float32, kind="ExternalOutput").ap()
    build(nc, A, consts, out)
    r = _run(nc, [arrays], core_ids=[0])
    return r.results[0]["out"]
```
